# Optimizing a Trainium2 kernel written in Bass

```python
import jax
import jax.numpy as jnp
from jax import lax
import numpy as np

D_MODEL = 1024
BATCH = 1
SEQ = 512
DEPTH = 2

PLE_DIM = 256
MIX_WIDTH = D_MODEL
GROUP_WIDTH = MIX_WIDTH // 4
HEAD_DIM = 64
GROUP_HEADS = GROUP_WIDTH // HEAD_DIM

GLA_HEADS = GROUP_HEADS
GLA_DK = HEAD_DIM // 2
GLA_DV = GROUP_WIDTH // GLA_HEADS
GLA_GATE_RANK = 16
GLA_GATE_NORMALIZER = 16.0

HGRN_HEADS = GROUP_HEADS
HGRN_EXPAND = HEAD_DIM
HGRN_DV = GROUP_WIDTH // HGRN_HEADS

SWA_Q_HEADS = GROUP_HEADS
SWA_KV_HEADS = GROUP_HEADS // 2
SWA_HEAD_DIM = GROUP_WIDTH // SWA_Q_HEADS
SWA_WINDOW = 128

RWKV_HEADS = GROUP_HEADS
RWKV_N = GROUP_WIDTH // RWKV_HEADS
RWKV_W_RANK = 16
RWKV_A_RANK = 16
RWKV_V_RANK = 8
RWKV_G_RANK = 32

CHUNK = 16
LN_EPS = 1e-5
RMS_EPS = 1e-6
RWKV_GN_EPS = 64e-5

D_FF = 2816
N_EXPERTS = 8
TOP_K = 2
D_FF_EXPERT = 3584
MOE_ROWS = 128

N_DENSE = (DEPTH + 1) // 2
N_MOE = DEPTH // 2
DEEPNORM_ALPHA = (2.0 * DEPTH) ** 0.25
DEEPNORM_BETA = (8.0 * DEPTH) ** -0.25

RWKV_COLS = 3 * GROUP_WIDTH + RWKV_W_RANK + RWKV_A_RANK + RWKV_G_RANK
IN_SIZES = (
    GLA_HEADS * GLA_DK, GLA_HEADS * GLA_DK, GROUP_WIDTH, GROUP_WIDTH, GLA_GATE_RANK,
    HGRN_HEADS * HGRN_EXPAND, HGRN_HEADS * HGRN_EXPAND, GROUP_WIDTH, GROUP_WIDTH,
    SWA_Q_HEADS * SWA_HEAD_DIM, SWA_KV_HEADS * SWA_HEAD_DIM, SWA_KV_HEADS * SWA_HEAD_DIM,
    RWKV_COLS,
)
P_IN = sum(IN_SIZES)

kernel_name = 'hybrid_gla_hgrn2_swa_rwkv7_moe_deepnorm'

def split_cols(z, sizes):
    out, o = [], 0
    for s in sizes:
        out.append(z[..., o:o + s])
        o += s
    return out

def layer_norm(x, g, b):
    xf = x.astype(jnp.float32)
    mu = jnp.mean(xf, axis=-1, keepdims=True)
    var = jnp.mean(jnp.square(xf - mu), axis=-1, keepdims=True)
    return ((xf - mu) * lax.rsqrt(var + LN_EPS) * g + b).astype(x.dtype)

def rms_norm(x, w):
    xf = x.astype(jnp.float32)
    return xf * lax.rsqrt(jnp.mean(jnp.square(xf), axis=-1, keepdims=True) + RMS_EPS) * w

def token_shift_lerp(z, mu):
    prev = jnp.pad(z, ((0, 0), (1, 0), (0, 0)))[:, :-1]
    return z + (prev - z) * mu

def chunk_gated_linear_attn(q, k, v, log_f):
    bsz, seq, nh, dk = q.shape
    dv = v.shape[-1]
    n = seq // CHUNK
    q, k, log_f = (t.reshape(bsz, n, CHUNK, nh, dk) for t in (q, k, log_f))
    v = v.reshape(bsz, n, CHUNK, nh, dv)
    b = jnp.cumsum(log_f, axis=2)
    causal = jnp.tril(jnp.ones((CHUNK, CHUNK), dtype=bool))[None, None, :, :, None, None]
    rel = jnp.exp(jnp.where(causal, b[:, :, :, None] - b[:, :, None, :], -jnp.inf))
    scores = jnp.einsum('bntshk,bnshk->bnhts', q[:, :, :, None] * rel, k)
    o_intra = jnp.einsum('bnhts,bnshv->bnthv', scores, v)
    b_last = b[:, :, -1]
    kv = jnp.einsum('bnshk,bnshv->nbhkv', k * jnp.exp(b_last[:, :, None] - b), v)
    chunk_decay = jnp.moveaxis(jnp.exp(b_last), 1, 0)

    def step(state, inp):
        decay, update = inp
        return state * decay[..., None] + update, state

    s0 = jnp.zeros((bsz, nh, dk, dv), q.dtype)
    _, s_prev = lax.scan(step, s0, (chunk_decay, kv))
    o_inter = jnp.einsum('bnthk,nbhkv->bnthv', q * jnp.exp(b), s_prev)
    return (o_intra + o_inter).reshape(bsz, seq, nh, dv)

def gla_mixer(q, k, v, g, gk_down, gk_up, gk_bias, norm_w):
    bsz, seq, _ = q.shape
    q = q.reshape(bsz, seq, GLA_HEADS, GLA_DK) * GLA_DK ** -0.5
    k = k.reshape(bsz, seq, GLA_HEADS, GLA_DK)
    v = v.reshape(bsz, seq, GLA_HEADS, GLA_DV)
    log_f = jax.nn.log_sigmoid(gk_down @ gk_up + gk_bias) / GLA_GATE_NORMALIZER
    o = chunk_gated_linear_attn(q, k, v, log_f.reshape(bsz, seq, GLA_HEADS, GLA_DK))
    o = rms_norm(o, norm_w) * jax.nn.silu(g.reshape(bsz, seq, GLA_HEADS, GLA_DV))
    return o.reshape(bsz, seq, GROUP_WIDTH)

def hgrn2_mixer(q, f, i_in, g, lb, norm_w):
    bsz, seq, _ = q.shape
    q = jax.nn.silu(q)
    log_f = jnp.logaddexp(jnp.log(lb), jnp.log1p(-lb) + jax.nn.log_sigmoid(f))
    k = (1.0 - lb) * jax.nn.sigmoid(-f)
    hk = lambda t: t.reshape(bsz, seq, HGRN_HEADS, HGRN_EXPAND)
    o = chunk_gated_linear_attn(hk(q), hk(k), i_in.reshape(bsz, seq, HGRN_HEADS, HGRN_DV), hk(log_f))
    o = rms_norm(o, norm_w) * jax.nn.silu(g.reshape(bsz, seq, HGRN_HEADS, HGRN_DV))
    return o.reshape(bsz, seq, GROUP_WIDTH)

def swa_sink_mixer(q, k, v, sinks):
    bsz, seq, _ = q.shape
    w = SWA_WINDOW
    nb = seq // w
    grp = SWA_Q_HEADS // SWA_KV_HEADS
    q = q.reshape(bsz, nb, w, SWA_KV_HEADS, grp, SWA_HEAD_DIM)
    k = k.reshape(bsz, nb, w, SWA_KV_HEADS, SWA_HEAD_DIM)
    v = v.reshape(bsz, nb, w, SWA_KV_HEADS, SWA_HEAD_DIM)
    shift = lambda t: jnp.concatenate([jnp.zeros_like(t[:, :1]), t[:, :-1]], axis=1)
    kw = jnp.concatenate([shift(k), k], axis=2)
    vw = jnp.concatenate([shift(v), v], axis=2)
    s = jnp.einsum('bnqhgd,bnkhd->bnhgqk', q, kw) * SWA_HEAD_DIM ** -0.5
    q_pos = jnp.arange(nb)[:, None] * w + jnp.arange(w)[None, :]
    k_pos = jnp.arange(nb)[:, None] * w - w + jnp.arange(2 * w)[None, :]
    dist = q_pos[:, :, None] - k_pos[:, None, :]
    mask = (dist >= 0) & (dist < w) & (k_pos[:, None, :] >= 0)
    s = jnp.where(mask[None, :, None, None], s, -jnp.inf).astype(jnp.float32)
    sink = jnp.broadcast_to(sinks.astype(jnp.float32).reshape(1, 1, SWA_KV_HEADS, grp, 1, 1), s.shape[:-1] + (1,))
    prob = jax.nn.softmax(jnp.concatenate([s, sink], axis=-1), axis=-1)[..., :-1]
    o = jnp.einsum('bnhgqk,bnkhd->bnqhgd', prob, vw)
    return o.reshape(bsz, seq, GROUP_WIDTH)

def rwkv7_recurrence(r, log_w, k, v, a, b):
    bsz, seq, nh, n = r.shape
    xs = tuple(jnp.moveaxis(t, 1, 0) for t in (r, jnp.exp(log_w), k, v, a, b))

    def step(state, inp):
        r_t, w_t, k_t, v_t, a_t, b_t = inp
        sa = jnp.einsum('bhvk,bhk->bhv', state, a_t)
        state = state * w_t[:, :, None, :] + sa[..., None] * b_t[:, :, None, :] + v_t[..., None] * k_t[:, :, None, :]
        return state, jnp.einsum('bhvk,bhk->bhv', state, r_t)

    _, y = lax.scan(step, jnp.zeros((bsz, nh, n, n), r.dtype), xs)
    return jnp.moveaxis(y, 0, 1)

def rwkv7_mixer(zr, mu, w0, w_up, a0, a_up, g_up, k_k, k_a, r_k, lnx_w, lnx_b, v_res):
    bsz, seq, _ = zr.shape
    zr = token_shift_lerp(zr, mu)
    r, k, v, wd, ad, gd = split_cols(zr, (GROUP_WIDTH, GROUP_WIDTH, GROUP_WIDTH, RWKV_W_RANK, RWKV_A_RANK, RWKV_G_RANK))
    w = -jax.nn.softplus(-(w0 + jnp.tanh(wd) @ w_up)) - 0.5
    log_decay = -jnp.exp(w)
    a = jax.nn.sigmoid(a0 + ad @ a_up)
    g = jax.nn.sigmoid(gd) @ g_up
    v_layer = v
    if v_res is not None:
        v_first, vd, v0, v_up = v_res
        v = v + (v_first - v) * jax.nn.sigmoid(v0 + vd @ v_up)
    heads = lambda t: t.reshape(bsz, seq, RWKV_HEADS, RWKV_N)
    kk = heads(k * k_k)
    kk = kk / jnp.maximum(jnp.sqrt(jnp.sum(jnp.square(kk), axis=-1, keepdims=True)), 1e-12)
    k = k * (1.0 + (a - 1.0) * k_a)
    r_h, k_h, v_h, a_h = heads(r), heads(k), heads(v), heads(a)
    y = rwkv7_recurrence(r_h, heads(log_decay), k_h, v_h, -kk, kk * a_h)
    mu_y = jnp.mean(y, axis=-1, keepdims=True)
    var_y = jnp.mean(jnp.square(y - mu_y), axis=-1, keepdims=True)
    y = ((y - mu_y) * lax.rsqrt(var_y + RWKV_GN_EPS)).reshape(bsz, seq, GROUP_WIDTH) * lnx_w + lnx_b
    bonus = jnp.sum(r_h * k_h * r_k, axis=-1, keepdims=True) * v_h
    y = y + bonus.reshape(bsz, seq, GROUP_WIDTH)
    return y * g, v_layer

def swiglu(x, w_gate, w_up, w_down):
    return (jax.nn.silu(x @ w_gate) * (x @ w_up)) @ w_down

def moe_swiglu(x, router, w_gate, w_up, w_down):
    bsz, seq, d = x.shape
    n_tok = bsz * seq
    n_assign = n_tok * TOP_K
    xt = x.reshape(n_tok, d)
    logits = jnp.matmul(xt, router).astype(jnp.float32)
    top_logit, top_e = lax.top_k(logits, TOP_K)
    gates = jax.nn.softmax(top_logit, axis=-1)
    e_flat = top_e.reshape(-1)
    tok_flat = jnp.arange(n_assign, dtype=jnp.int32) // TOP_K
    order = jnp.argsort(e_flat)
    e_sorted = e_flat[order]
    counts = jnp.bincount(e_flat, length=N_EXPERTS)
    padded = (counts + MOE_ROWS - 1) // MOE_ROWS * MOE_ROWS
    start = jnp.cumsum(counts) - counts
    pad_end = jnp.cumsum(padded)
    pad_start = pad_end - padded
    dest = pad_start[e_sorted] + jnp.arange(n_assign, dtype=jnp.int32) - start[e_sorted]
    n_blocks = -(-n_assign // MOE_ROWS) + N_EXPERTS
    n_rows = n_blocks * MOE_ROWS
    row_tok = jnp.zeros((n_rows,), jnp.int32).at[dest].set(tok_flat[order])
    row_gate = jnp.zeros((n_rows,), jnp.float32).at[dest].set(gates.reshape(-1)[order])
    block_start = jnp.arange(n_blocks, dtype=jnp.int32) * MOE_ROWS
    block_e = jnp.minimum(jnp.searchsorted(pad_end, block_start, side='right'), N_EXPERTS - 1)
    x_rows = xt[row_tok].reshape(n_blocks, MOE_ROWS, d)

    def expert_block(args):
        xb, e = args
        return (jax.nn.silu(xb @ w_gate[e]) * (xb @ w_up[e])) @ w_down[e]

    y_rows = lax.map(expert_block, (x_rows, block_e)).reshape(n_rows, d)
    y = jnp.zeros((n_tok, d), jnp.float32).at[row_tok].add(y_rows * row_gate[:, None])
    return y.astype(x.dtype).reshape(bsz, seq, d)

def setup_inputs(seed: int = 0) -> dict:
    key = jax.random.key(seed)
    keys = jax.random.split(key, 64)
    counter = [0]
    f32 = jnp.float32

    def nxt():
        kk = keys[counter[0]]
        counter[0] += 1
        return kk

    def nrm(shape, scale):
        return jax.random.normal(nxt(), shape, f32) * scale

    def unif(shape, lo, hi):
        return jax.random.uniform(nxt(), shape, f32, lo, hi)

    L, D, GW = DEPTH, D_MODEL, GROUP_WIDTH
    beta = DEEPNORM_BETA
    return {
        'x': nrm((BATCH, SEQ, D), 1.0),
        'p': nrm((L, BATCH, SEQ, PLE_DIM), 1.0),
        'w_in': nrm((L, D, P_IN), D ** -0.5),
        'w_out': nrm((L, MIX_WIDTH, D), beta * MIX_WIDTH ** -0.5),
        'gla_gk_up': nrm((L, GLA_GATE_RANK, GLA_HEADS * GLA_DK), GLA_GATE_RANK ** -0.5),
        'gla_gk_bias': nrm((L, GLA_HEADS * GLA_DK), 0.1),
        'gla_norm_w': 1.0 + nrm((L, GLA_DV), 0.02),
        'hgrn_lower_bounds': nrm((L, HGRN_HEADS * HGRN_EXPAND), 0.1),
        'hgrn_norm_w': 1.0 + nrm((L, HGRN_DV), 0.02),
        'swa_sinks': nrm((L, SWA_Q_HEADS), 1.0),
        'rwkv_mu': unif((L, RWKV_COLS), 0.0, 1.0),
        'rwkv_w0': unif((L, GW), -6.0, -1.0),
        'rwkv_w_up': nrm((L, RWKV_W_RANK, GW), RWKV_W_RANK ** -0.5),
        'rwkv_a0': nrm((L, GW), 0.1),
        'rwkv_a_up': nrm((L, RWKV_A_RANK, GW), RWKV_A_RANK ** -0.5),
        'rwkv_g_up': nrm((L, RWKV_G_RANK, GW), RWKV_G_RANK ** -0.5),
        'rwkv_k_k': 0.85 + nrm((L, GW), 0.02),
        'rwkv_k_a': 1.0 + nrm((L, GW), 0.02),
        'rwkv_r_k': nrm((L, RWKV_HEADS, RWKV_N), 0.1),
        'rwkv_lnx_w': 1.0 + nrm((L, GW), 0.02),
        'rwkv_lnx_b': nrm((L, GW), 0.02),
        'rwkv_vres_down': nrm((L - 1, D, RWKV_V_RANK), D ** -0.5),
        'rwkv_vres_mu': unif((L - 1, RWKV_V_RANK), 0.0, 1.0),
        'rwkv_v0': nrm((L - 1, GW), 0.1),
        'rwkv_vres_up': nrm((L - 1, RWKV_V_RANK, GW), RWKV_V_RANK ** -0.5),
        'ln1_g': 1.0 + nrm((L, D), 0.02),
        'ln1_b': nrm((L, D), 0.02),
        'ln2_g': 1.0 + nrm((L, D), 0.02),
        'ln2_b': nrm((L, D), 0.02),
        'ffn_w_gate': nrm((N_DENSE, D, D_FF), D ** -0.5),
        'ffn_w_up': nrm((N_DENSE, D, D_FF), D ** -0.5),
        'ffn_w_down': nrm((N_DENSE, D_FF, D), beta * D_FF ** -0.5),
        'moe_router': nrm((N_MOE, D, N_EXPERTS), D ** -0.5),
        'moe_w_gate': nrm((N_MOE, N_EXPERTS, D, D_FF_EXPERT), D ** -0.5),
        'moe_w_up': nrm((N_MOE, N_EXPERTS, D, D_FF_EXPERT), D ** -0.5),
        'moe_w_down': nrm((N_MOE, N_EXPERTS, D_FF_EXPERT, D), beta * D_FF_EXPERT ** -0.5),
        'ple_proj': nrm((L, PLE_DIM, D), beta * PLE_DIM ** -0.5),
        'ple_gate': nrm((L, D, D), D ** -0.5),
    }

def reference(x, p, w_in, w_out, gla_gk_up, gla_gk_bias, gla_norm_w, hgrn_lower_bounds, hgrn_norm_w,
              swa_sinks, rwkv_mu, rwkv_w0, rwkv_w_up, rwkv_a0, rwkv_a_up, rwkv_g_up, rwkv_k_k, rwkv_k_a,
              rwkv_r_k, rwkv_lnx_w, rwkv_lnx_b, rwkv_vres_down, rwkv_vres_mu, rwkv_v0, rwkv_vres_up,
              ln1_g, ln1_b, ln2_g, ln2_b, ffn_w_gate, ffn_w_up, ffn_w_down, moe_router, moe_w_gate,
              moe_w_up, moe_w_down, ple_proj, ple_gate):
    f32 = jnp.float32
    lbs = jnp.cumsum(jax.nn.softmax(hgrn_lower_bounds.astype(f32), axis=0), axis=0)
    lbs = lbs - lbs[0]
    v_first = None
    for i in range(DEPTH):
        w = w_in[i] if i == 0 else jnp.concatenate([w_in[i], rwkv_vres_down[i - 1]], axis=1)
        z = jnp.matmul(x, w).astype(f32)
        (gq, gk, gv, gg, ggk, hq, hf, hi, hg, sq, sk, sv, rz) = split_cols(z, IN_SIZES)
        o_gla = gla_mixer(gq, gk, gv, gg, ggk, gla_gk_up[i], gla_gk_bias[i], gla_norm_w[i])
        o_hgrn = hgrn2_mixer(hq, hf, hi, hg, lbs[i], hgrn_norm_w[i])
        o_swa = swa_sink_mixer(sq, sk, sv, swa_sinks[i])
        if i == 0:
            v_res = None
        else:
            vd = token_shift_lerp(z[..., P_IN:], rwkv_vres_mu[i - 1])
            v_res = (v_first, vd, rwkv_v0[i - 1], rwkv_vres_up[i - 1])
        o_rwkv, v_layer = rwkv7_mixer(rz, rwkv_mu[i], rwkv_w0[i], rwkv_w_up[i], rwkv_a0[i], rwkv_a_up[i],
                                      rwkv_g_up[i], rwkv_k_k[i], rwkv_k_a[i], rwkv_r_k[i], rwkv_lnx_w[i],
                                      rwkv_lnx_b[i], v_res)
        if i == 0:
            v_first = v_layer
        mix = jnp.concatenate([o_gla, o_hgrn, o_swa, o_rwkv], axis=-1).astype(x.dtype)
        x = layer_norm(DEEPNORM_ALPHA * x + mix @ w_out[i], ln1_g[i], ln1_b[i])
        j = i // 2
        if i % 2 == 0:
            f = swiglu(x, ffn_w_gate[j], ffn_w_up[j], ffn_w_down[j])
        else:
            f = moe_swiglu(x, moe_router[j], moe_w_gate[j], moe_w_up[j], moe_w_down[j])
        x = layer_norm(DEEPNORM_ALPHA * x + f, ln2_g[i], ln2_b[i])
        x = x + jax.nn.sigmoid(x @ ple_gate[i]) * (p[i] @ ple_proj[i])
    return x


_drawn_inputs = setup_inputs


def setup_inputs(seed=0):
    import zlib

    import numpy as np

    out = dict(_drawn_inputs(seed))
    spreads = {}
    factors = {'gla_gk_up': 3.077,
     'gla_gk_bias': 4.18,
     'gla_norm_w': 8.0,
     'hgrn_lower_bounds': 8.0,
     'hgrn_norm_w': 8.0,
     'swa_sinks': 8.0,
     'rwkv_w_up': 5.895,
     'rwkv_a0': 6.769,
     'rwkv_k_k': 5.498,
     'rwkv_k_a': 7.406,
     'rwkv_lnx_w': 6.865,
     'rwkv_lnx_b': 8.0,
     'rwkv_v0': 5.895}
    for name, (base, spread) in spreads.items():
        noise = np.random.default_rng([zlib.crc32(name.encode()), seed]).standard_normal(out[name].shape)
        drawn = base * np.exp(spread * noise) if base else spread * noise
        out[name] = jnp.asarray(drawn.astype(out[name].dtype))
    for name, factor in factors.items():
        out[name] = (out[name] * factor).astype(out[name].dtype)
    return out
```

```python
import concourse.bass as bass
from concourse import mybir
from contextlib import ExitStack

F32 = mybir.dt.float32
I32 = mybir.dt.int32
U32 = mybir.dt.uint32
ALU = mybir.AluOpType
ACT = mybir.ActivationFunctionType
AX_X = mybir.AxisListType.X

P = 128
D = 1024
T = 512
NT = T // P
KD = D // P
DEPTH = 2
HALF = 512
ALPHA = (2.0 * DEPTH) ** 0.25
GW = 256
HD = 64
GLA_DK = 32
D_FF = 2816
F_TILES = D_FF // P
N_EXP = 8
D_FFE = 3584
LN_EPS, RMS_EPS, GN_EPS = 1e-5, 1e-6, 64e-5
RW_CHUNK = 64
RW_RATE = 0.6065306597126334
RW_MID = -RW_RATE * RW_CHUNK / 2
NC64 = T // RW_CHUNK
LEVELS = [64, 32, 16, 8, 4, 2, 1]
NEG = -1e30

C_GQ, C_GV, C_GG, C_GGK = 0, 256, 512, 768
C_HQ, C_HF, C_HI, C_HG = 784, 1040, 1296, 1552
C_SQ, C_SK = 1808, 2064
C_R, C_K, C_V, C_WD, C_AD, C_GD = 2320, 2576, 2832, 3088, 3104, 3120
L_WD, L_AD, L_VD, L_GD, L_GK = 0, 32, 48, 64, 96
U_W, U_A, U_V, U_G, U_GK, U_END = 0, 256, 512, 768, 1024, 1152

(R_GKB, R_GNW, R_HNW, R_W0, R_A0, R_KK, R_KA, R_RK, R_LW, R_LB, R_V0, R_MU, R_MUS, R_LBD, R_ROWS) = (
    0, 1, 2, 3, 5, 7, 9, 11, 13, 15, 17, 19, 25, 26, 32)


class Inputs(dict):

    def __getattr__(self, name):
        return self[name]


class Buffers:
    pass


class Stage(ExitStack):

    def __init__(self, nc, tag):
        super().__init__()
        self.nc, self.tag, self.sems = nc, tag, []

    def semaphore(self, name):
        self.sems.append(self.nc.alloc_semaphore(self.tag + name))
        return self.sems[-1]

    def __exit__(self, *error):
        done = super().__exit__(*error)
        if error[0] is None:
            self.nc.clear_and_free_semaphores(self.sems)
            self.nc.all_engine_barrier()
        return done


class Steps:

    def __init__(self, eng, own):
        self.eng, self.own, self.count = eng, own, {}

    def __call__(self, ins, sem=None):
        sem = self.own if sem is None else sem
        ins.then_inc(sem, 1)
        self.count[sem.name] = self.count.get(sem.name, 0) + 1
        self.eng.wait_ge(sem, self.count[sem.name])


class Ring:

    def __init__(self, st, nc, name, psum, banks):
        self.full = st.semaphore(name + "_full")
        self.freed = st.semaphore(name + "_freed")
        self.psum, self.banks, self.filled, self.read = psum, banks, 0, 0

    def fill(self, pe):
        k = self.filled
        self.filled += 1
        if k >= len(self.banks):
            pe.wait_ge(self.freed, k - len(self.banks) + 1)
        return self.psum[:, self.banks[k % len(self.banks)], :]

    def take(self, eng):
        k = self.read
        self.read += 1
        eng.wait_ge(self.full, k + 1)
        return self.psum[:, self.banks[k % len(self.banks)], :]


def over(ap, n):
    return ap.unsqueeze(1).broadcast_to([ap.shape[0], n, ap.shape[1]])


def blocks4(ap):
    return ap.rearrange("p (c t) -> p c t", c=4)


def stage_constants(nc, S, A):
    S.tag = "constants_"
    with Stage(nc, S.tag) as st:
        sem = lambda n: st.semaphore(n)
        rows = st.enter_context(nc.sbuf_tensor("param_rows", [DEPTH * R_ROWS, P], F32))
        zeros = st.enter_context(nc.sbuf_tensor("zeros", [P, P], F32))
        x_in, params_in, consts = sem("x_in"), sem("params_in"), sem("consts")
        pool_step, dve_step, rows_clear = sem("pool_step"), sem("dve_step"), sem("rows_clear")
        ring = Ring(st, nc, "setup", S.bank, list(range(8)))
        loads = []
        for i in range(DEPTH):
            r0 = i * R_ROWS

            def row(r, ap, c0=0):
                n, w = ap.shape
                loads.append((rows[r0 + r:r0 + r + n, c0:c0 + w], ap))

            two = lambda ap: ap.rearrange("(a b) -> a b", b=P)
            one = lambda ap: ap.rearrange("(a b) -> a b", a=1)
            row(R_GKB, one(A.gla_gk_bias[i, :]))
            for h in range(2):
                row(R_GNW, one(A.gla_norm_w[i, :]), h * HD)
                row(R_HNW, one(A.hgrn_norm_w[i, :]), h * HD)
            for r, t in ((R_W0, A.rwkv_w0), (R_A0, A.rwkv_a0), (R_KK, A.rwkv_k_k), (R_KA, A.rwkv_k_a),
                         (R_LW, A.rwkv_lnx_w), (R_LB, A.rwkv_lnx_b)):
                row(r, two(t[i, :]))
            row(R_RK, two(A.rwkv_r_k[i].rearrange("h n -> (h n)")))
            row(R_MU, two(A.rwkv_mu[i, 0:3 * GW]))
            row(R_MUS, one(A.rwkv_mu[i, 768:784]), L_WD)
            row(R_MUS, one(A.rwkv_mu[i, 784:800]), L_AD)
            row(R_MUS, one(A.rwkv_mu[i, 800:832]), L_GD)
            for j in range(DEPTH):
                row(R_LBD + 2 * j, two(A.hgrn_lower_bounds[j, :]))
            if i > 0:
                row(R_V0, two(A.rwkv_v0[i - 1, :]))
                row(R_MUS, one(A.rwkv_vres_mu[i - 1, :]), L_VD)

        with nc.Block() as block:
            @block.sync
            def _(sp):
                for t in range(NT):
                    sp.dma_start(S.x[:, t, :], A.x[0, t * P:(t + 1) * P, :]).then_inc(x_in, 16)
                sp.wait_ge(rows_clear, 1)
                for dst, src in loads:
                    sp.dma_start(dst, src).then_inc(params_in, 16)
                sp.dma_start(S.sinks[:, :], A.swa_sinks.rearrange("l h -> (l h)").partition_broadcast(P)).then_inc(params_in, 16)
                sp.wait_ge(params_in, 16 * (len(loads) + 1))

            @block.gpsimd
            def _(pool):
                step = Steps(pool, pool_step)
                g = nc.gpsimd

                def select(ap, pattern, base, mult, op=ALU.is_ge, fill=0.0):
                    step(g.affine_select(out=ap, in_=ap, compare_op=op, fill=fill, base=base,
                                         pattern=pattern, channel_multiplier=mult))

                step(g.memset(S.ident[:, :], 0.0))
                select(S.ident[:, :], [[-1, P]], 0, 1, ALU.not_equal, 1.0)
                step(g.memset(S.lower[:, :, :], 0.0))
                for l, m in enumerate(LEVELS):
                    second = S.lower[:, l, :].rearrange("p (b h j) -> p b h j", h=2, j=m)[:, :, 1, :]
                    n = P // (2 * m)
                    step(g.memset(second, 1.0))
                    select(second, [[-2 * m, n], [0, m]], 0, 1)
                    select(second, [[2 * m, n], [0, m]], m - 1, -1)
                head = S.head_ones[:, :].rearrange("p (b j) -> p b j", b=2)
                step(g.memset(S.head_ones[:, :], 1.0))
                select(head, [[-HD, 2], [0, HD]], 0, 1)
                select(head, [[HD, 2], [0, HD]], HD - 1, -1)
                step(g.tensor_scalar(S.head_mean[:, :], S.head_ones[:, :], 1.0 / HD, None, ALU.mult))
                for dst, op in ((S.chunk_before, ALU.is_gt), (S.chunk_upto, ALU.is_ge)):
                    step(g.tensor_copy(dst[:, :], S.head_ones[:, :]))
                    select(dst[:, :], [[1, P]], 0, -1, op)
                step(g.memset(S.gla_heads[:, :], 1.0))
                heads4 = S.gla_heads[:, :].rearrange("p (h v) -> p h v", h=4)
                select(heads4, [[-GLA_DK, 4], [0, HD]], 0, 1)
                select(heads4, [[GLA_DK, 4], [0, HD]], GLA_DK - 1, -1)
                step(g.memset(zeros[:, :], 0.0))
                step(g.memset(S.own_bias[:, :], 0.0))
                select(S.own_bias[:, :], [[-1, P]], 0, 1, ALU.is_ge, NEG)
                step(g.memset(S.prev_bias[:, :], 0.0))
                select(S.prev_bias[:, :], [[1, P]], 0, -1, ALU.is_gt, NEG)
                step(g.memset(S.ones[:, :], 1.0))
                step(g.memset(S.before[:, :], 1.0))
                select(S.before[:, :], [[1, P]], 0, -1, ALU.is_gt)
                step(g.iota(S.slots[:, :], pattern=[[1, T]], base=0, channel_multiplier=0,
                            allow_small_or_imprecise_dtypes=True))
                step(g.memset(S.carry128[:, :], 1.0))
                step(g.memset(S.carry128[:, 0:T:P], 0.0))
                step(g.memset(S.carry64[:, :], 1.0))
                step(g.memset(S.carry64[:, 0:T:RW_CHUNK], 0.0))
                for c, v in enumerate((LN_EPS, RMS_EPS, GN_EPS, -RW_MID, RW_MID, 1.0)):
                    step(g.memset(S.eps[:, c:c + 1], v))
                step(g.memset(S.w_low[:, :, :], 0.0))
                g.memset(S.w_up[:, :], 0.0).then_inc(consts, 1)

            @block.tensor
            def _(pe):
                pe.wait_ge(consts, 1)
                for t in range(NT):
                    pe.wait_ge(x_in, 16 * NT)
                    for h in range(2):
                        b = ring.fill(pe)
                        for j in range(4):
                            k = 4 * h + j
                            last = nc.tensor.transpose(b[:, j * P:(j + 1) * P], S.x[:, t, k * P:(k + 1) * P], S.ident[:, :])
                        last.then_inc(ring.full, 1)
                b = ring.fill(pe)
                pe.wait_ge(params_in, 16 * (len(loads) + 1))
                nc.tensor.transpose(b[:, 0:DEPTH * R_ROWS], rows[:, :], S.ident[0:DEPTH * R_ROWS, 0:DEPTH * R_ROWS]).then_inc(ring.full, 1)

            @block.vector
            def _(dve):
                step = Steps(dve, dve_step)
                step(nc.vector.memset(rows[:, :], 0.0), rows_clear)
                for t in range(NT):
                    for h in range(2):
                        b = ring.take(dve)
                        step(nc.vector.tensor_copy(S.xT[:, 4 * h:4 * h + 4, t * P:(t + 1) * P], blocks4(b)), ring.freed)
                b = ring.take(dve)
                step(nc.vector.tensor_copy(S.par[:, :], b[:, 0:DEPTH * R_ROWS]), ring.freed)


def stage_projection(nc, S, A, i):
    S.tag = f"projection{i}_"
    w = A.w_in[i].rearrange("(k p) n -> p k n", p=P)
    SLOTS = 4
    with Stage(nc, S.tag) as st:
        sem = lambda n: st.semaphore(n)
        ws = [st.enter_context(nc.sbuf_tensor(f"{S.tag}w_slot{n}", [P, KD, GW], F32)) for n in range(SLOTS)]
        landed = [sem(f"w_landed{n}") for n in range(SLOTS)]
        low_in, up_in, act_step, dve_step = sem("low_in"), sem("up_in"), sem("act_step"), sem("dve_step")
        rings = [Ring(st, nc, "act_bank", S.bank, [0, 1, 2, 3]), Ring(st, nc, "dve_bank", S.bank, [4, 5, 6, 7])]
        z = lambda n: S.z[:, n, :]
        zr = lambda n: S.zr[:, n, 1:T + 1]
        ch = lambda *tiles: ("channels", tiles)
        chunks = [
            (C_R, ch(zr(0), zr(1))), (C_K, ch(zr(2), zr(3))), (C_V, ch(zr(4), zr(5))),
            (C_GQ, ch(z(0), z(1))), (C_GV, ("tokens", S.v_gla, GW)), (C_GG, ch(z(2), z(3))),
            (C_HQ, ch(z(4), z(5))), (C_HF, ch(z(6), z(7))), (C_HI, ("tokens", S.v_hgrn, GW)), (C_HG, ch(z(8), z(9))),
            (C_SQ, ch(z(10), z(11))), (C_SK, ("keys and values", z(12), S.v_swa)),
        ]
        outs, last_bank = [zr(6)], []
        for _, what in chunks:
            if what[0] == "channels":
                outs += list(what[1])
            elif what[0] == "tokens":
                outs += [what[1][:, t:t + 2, :] for t in (0, 2)]
            else:
                outs += [what[1], what[2][:, :, :]]
            last_bank.append(len(outs) - 1)
        low = [(L_WD, C_WD, 16), (L_AD, C_AD, 16), (L_GD, C_GD, 32), (L_GK, C_GGK, 16)]
        ups = [(L_WD, U_W, A.rwkv_w_up[i]), (L_AD, U_A, A.rwkv_a_up[i]), (L_GD, U_G, A.rwkv_g_up[i]), (L_GK, U_GK, A.gla_gk_up[i])]
        if i > 0:
            ups.append((L_VD, U_V, A.rwkv_vres_up[i - 1]))
        with nc.Block() as block:
            @block.sync
            def _(sp):
                for n, (c0, what) in enumerate(chunks):
                    s = n % SLOTS
                    if n >= SLOTS:
                        j = last_bank[n - SLOTS]
                        sp.wait_ge(rings[j % 2].full, j // 2 + 1)
                    if c0 == C_SQ:
                        for c, h in enumerate((0, 2, 1, 3)):
                            sp.dma_start(ws[s][:, :, c * HD:(c + 1) * HD], w[:, :, c0 + h * HD:c0 + (h + 1) * HD]).then_inc(landed[s], 16)
                    else:
                        sp.dma_start(ws[s][:, :, :], w[:, :, c0:c0 + GW]).then_inc(landed[s], 16)

            @block.gpsimd
            def _(pool):
                nc.gpsimd.memset(S.zr[:, :, 0:1], 0.0)

            @block.tensor
            def _(pe):
                job = 0

                def channels(weights, m=P):
                    nonlocal job
                    r = rings[job % 2]
                    job += 1
                    b = r.fill(pe)
                    for k in range(KD):
                        last = nc.tensor.matmul(b[0:m, :], weights[:, k, :], S.xT[:, k, :], start=(k == 0), stop=(k == KD - 1))
                    last.then_inc(r.full, 1)

                def tokens(weights, n, per_bank):
                    nonlocal job
                    for t0 in range(0, NT, per_bank):
                        r = rings[job % 2]
                        job += 1
                        b = r.fill(pe)
                        for t in range(per_bank):
                            for k in range(KD):
                                last = nc.tensor.matmul(b[:, t * n:(t + 1) * n], S.xT[:, k, (t0 + t) * P:(t0 + t + 1) * P],
                                                        weights[:, k, :], start=(k == 0), stop=(k == KD - 1))
                        last.then_inc(r.full, 1)

                pe.wait_ge(low_in, 16 * (len(low) + (i > 0)))
                channels(S.w_low[:, :, :])
                seen = [0] * SLOTS
                for n, (c0, what) in enumerate(chunks):
                    s = n % SLOTS
                    seen[s] += 16 * (4 if c0 == C_SQ else 1)
                    pe.wait_ge(landed[s], seen[s])
                    if what[0] == "channels":
                        channels(ws[s][:, :, 0:P])
                        channels(ws[s][:, :, P:GW])
                    elif what[0] == "tokens":
                        tokens(ws[s][:, :, :], GW, 2)
                    else:
                        channels(ws[s][:, :, 0:P])
                        tokens(ws[s][:, :, P:GW], P, 4)

            def evacuate(eng, which, op, own):
                step = Steps(eng, own)
                for n, dst in enumerate(outs):
                    if n % 2 == which:
                        b = rings[which].take(eng)
                        b = b if len(dst.shape) == 2 else b.rearrange("p (c t) -> p c t", c=dst.shape[1])
                        step(op(dst, b), rings[which].freed)

            @block.scalar
            def _(act):
                for r, c, k in low:
                    act.dma_start(S.w_low[:, :, r:r + k], w[:, :, c:c + k]).then_inc(low_in, 16)
                if i > 0:
                    act.dma_start(S.w_low[:, :, L_VD:L_VD + 8], A.rwkv_vres_down[i - 1].rearrange("(k p) n -> p k n", p=P)).then_inc(low_in, 16)
                for r, c, src in ups:
                    k, m = src.shape
                    act.dma_start(S.w_up[r:r + k, c:c + m], src).then_inc(up_in, 16)
                act.wait_ge(up_in, 16 * len(ups))
                evacuate(act, 0, lambda o, b: nc.scalar.activation(o, b, ACT.Copy), act_step)

            @block.vector
            def _(dve):
                evacuate(dve, 1, lambda o, b: nc.vector.tensor_copy(o, b), dve_step)


def stage_gates(nc, S, A, i):
    S.tag = f"gates{i}_"
    with Stage(nc, S.tag) as st:
        sem = lambda n: st.semaphore(n)
        tmp = st.enter_context(nc.sbuf_tensor(S.tag + "gate_tmp", [P, 3, T], F32))
        low_shifted, low_ready, shifted, act_step, dve_step = (
            sem("low_shifted"), sem("low_ready"), sem("shifted"), sem("act_step"), sem("dve_step"))
        lb_ready, soft_ready, mins_ready, hk_ready, lb2, log_a = (
            sem("lb_ready"), sem("soft_ready"), sem("mins_ready"), sem("hk_ready"), sem("lb2"), sem("log_a"))
        diff_ready, soft2_ready = sem("diff_ready"), sem("soft2_ready")
        ring = Ring(st, nc, "act_bank", S.bank, list(range(8)))
        par = lambda r: S.par[:, i * R_ROWS + r:i * R_ROWS + r + 1]
        blocks = [(U_W, 2), (U_A, 2), (U_G, 2)] + ([(U_V, 2)] if i else [])
        LD, SOFT = S.log_decay, S.soft
        with nc.Block() as block:
            @block.tensor
            def _(pe):
                pe.wait_ge(low_ready, 2)
                for u0, n in [(U_GK, 1)] + blocks:
                    for j in range(n):
                        b = ring.fill(pe)
                        nc.tensor.matmul(b, S.w_up[:, u0 + j * P:u0 + (j + 1) * P], S.low[:, :], start=True, stop=True).then_inc(ring.full, 1)

            @block.scalar
            def _(act):
                step = Steps(act, act_step)
                f = nc.scalar.activation
                for n in (2, 3, 8, 9, 4, 5):
                    step(f(S.z[:, n, :], S.z[:, n, :], ACT.Silu))
                act.wait_ge(low_shifted, 1)
                step(f(S.low[L_WD:L_WD + 16, :], S.low[L_WD:L_WD + 16, :], ACT.Tanh), low_ready)
                step(f(S.low[L_GD:L_GD + 32, :], S.low[L_GD:L_GD + 32, :], ACT.Sigmoid), low_ready)
                for j in range(2):
                    step(f(S.h_key[:, j, :], S.z[:, 6 + j, :], ACT.Sigmoid, scale=-1.0), hk_ready)
                b = ring.take(act)
                step(f(S.gk_pre[:, :], b, ACT.Identity, bias=par(R_GKB)), ring.freed)
                dest = {U_W: (S.rw_w, R_W0), U_A: (S.rw_a, R_A0), U_G: (S.rw_g, None), U_V: (S.rw_vg, R_V0)}
                for u0, n in blocks:
                    for j in range(n):
                        b = ring.take(act)
                        to, r = dest[u0]
                        if r is None:
                            step(f(to[:, j, :], b, ACT.Copy), ring.freed)
                        else:
                            step(f(to[:, j, :], b, ACT.Sigmoid, bias=par(r + j)), ring.freed)
                src = [S.gk_pre[:, :], S.z[:, 6, :], S.z[:, 7, :]]
                for n in range(3):
                    step(f(SOFT[:, n, :], src[n], ACT.Abs))
                for n in range(3):
                    step(f(SOFT[:, n, :], SOFT[:, n, :], ACT.Exp, scale=-1.0))
                if i:
                    act.wait_ge(lb_ready, 2)
                    step(f(S.lb[:, 4:8], S.lb[:, 0:4], ACT.Abs))
                    step(f(S.lb[:, 4:8], S.lb[:, 4:8], ACT.Exp, scale=-1.0))
                for n in range(3):
                    step(f(SOFT[:, n, :], SOFT[:, n, :], ACT.Ln, bias=S.eps[:, 5:6]), soft_ready)
                if i:
                    step(f(S.lb[:, 4:8], S.lb[:, 4:8], ACT.Ln, bias=S.eps[:, 5:6]), lb2)
                    act.wait_ge(log_a, 1)
                    step(f(S.lb[:, 8:10], S.lb[:, 6:8], ACT.Exp), lb2)
                    for j in range(2):
                        act.wait_ge(diff_ready, j + 1)
                        step(f(tmp[:, j, :], tmp[:, j, :], ACT.Abs))
                    for j in range(2):
                        step(f(tmp[:, j, :], tmp[:, j, :], ACT.Exp, scale=-1.0))
                    for j in range(2):
                        step(f(tmp[:, j, :], tmp[:, j, :], ACT.Ln, bias=S.eps[:, 5:6]), soft2_ready)

            @block.vector
            def _(dve):
                step = Steps(dve, dve_step)
                v = nc.vector

                def shift(n, mu, out, s=None):
                    step(v.tensor_tensor(tmp[:, 2, :], S.zr[:, n, 0:T], S.zr[:, n, 1:T + 1], ALU.subtract))
                    step(v.scalar_tensor_tensor(out, tmp[:, 2, :], mu, S.zr[:, n, 1:T + 1], ALU.mult, ALU.add), s)

                shift(6, par(R_MUS), S.low[:, :], low_shifted)
                if i:
                    step(v.tensor_tensor(S.lb[:, 0:2], S.par[:, i * R_ROWS + R_LBD:i * R_ROWS + R_LBD + 2],
                                         S.par[:, i * R_ROWS + R_LBD + 2:i * R_ROWS + R_LBD + 4], ALU.subtract), lb_ready)
                    step(v.tensor_scalar(S.lb[:, 2:4], S.lb[:, 0:2], -1.0, None, ALU.mult), lb_ready)
                for j in range(2):
                    shift(j, par(R_MU + j), S.r[:, j, :])
                    shift(2 + j, par(R_MU + 2 + j), S.k[:, j, :])
                    shift(4 + j, par(R_MU + 4 + j), S.v_first[:, j, :] if i == 0 else S.v[:, j, :])
                src = [S.gk_pre[:, :], S.z[:, 6, :], S.z[:, 7, :]]
                for n in range(3):
                    dve.wait_ge(soft_ready, n + 1)
                    step(v.scalar_tensor_tensor(LD[:, n, :], src[n], 0.0, SOFT[:, n, :], ALU.min, ALU.subtract))
                if i:
                    dve.wait_ge(lb2, 1)
                    step(v.tensor_scalar(S.lb[:, 0:4], S.lb[:, 0:4], 0.0, -1.0, ALU.max, ALU.mult))
                    step(v.tensor_tensor(S.lb[:, 4:8], S.lb[:, 0:4], S.lb[:, 4:8], ALU.subtract), log_a)
                    for j in range(2):
                        step(v.tensor_scalar(LD[:, 1 + j, :], LD[:, 1 + j, :], S.lb[:, 6 + j:7 + j], None, ALU.add))
                        step(v.tensor_scalar(tmp[:, j, :], LD[:, 1 + j, :], S.lb[:, 4 + j:5 + j], None, ALU.subtract), diff_ready)
                    for j in range(2):
                        dve.wait_ge(soft2_ready, j + 1)
                        step(v.scalar_tensor_tensor(LD[:, 1 + j, :], LD[:, 1 + j, :], S.lb[:, 4 + j:5 + j], tmp[:, j, :], ALU.max, ALU.add))
                    dve.wait_ge(lb2, 2)
                    dve.wait_ge(hk_ready, 2)
                    for j in range(2):
                        step(v.tensor_scalar(S.h_key[:, j, :], S.h_key[:, j, :], S.lb[:, 8 + j:9 + j], None, ALU.mult))
                    for j in range(2):
                        dve.wait_ge(ring.freed, ring.filled)
                        step(v.tensor_tensor(tmp[:, 2, :], S.v_first[:, j, :], S.v[:, j, :], ALU.subtract))
                        step(v.tensor_tensor(tmp[:, 2, :], tmp[:, 2, :], S.rw_vg[:, j, :], ALU.mult))
                        step(v.tensor_tensor(S.v[:, j, :], S.v[:, j, :], tmp[:, 2, :], ALU.add))


def rms_gate(nc, S, step, ring, o, sq, gate, weight, to):
    step(nc.vector.reciprocal(sq, sq))
    step(nc.vector.tensor_tensor(o, o, sq, ALU.mult))
    step(nc.vector.scalar_tensor_tensor(to, o, weight, gate, ALU.mult, ALU.mult))


def stage_gated_linear(nc, S, A, i):
    S.tag = f"gated_linear{i}_"
    par = lambda r: S.par[:, i * R_ROWS + r:i * R_ROWS + r + 1]
    tiles = [
        (1.0 / 16.0, S.z[:, 0, :], S.z[:, 1, :], GLA_DK, S.v_gla, 0, GW, S.gla_heads, [(2, 0), (3, 1)], R_GNW),
        (1.0, S.z[:, 4, :], S.h_key[:, 0, :], HD, S.v_hgrn, 0, P, S.head_ones, [(8, 2)], R_HNW),
        (1.0, S.z[:, 5, :], S.h_key[:, 1, :], HD, S.v_hgrn, P, P, S.head_ones, [(9, 3)], R_HNW),
    ]
    with Stage(nc, S.tag) as st:
        sem = lambda n: st.semaphore(n)
        sb = lambda n, *s: st.enter_context(nc.sbuf_tensor(S.tag + n, list(s), F32))
        cum, scaled = sb("cum", P, T), sb("scaled", P, 4, T)
        q_in, k_out, k_out_tok = sb("q_in", P, T), sb("k_out", P, T), sb("k_out_tok", P, NT, P)
        decay = sb("decay", P, T)
        scores = sb("scores", P, 4, T)
        state, update = sb("state", P, NT, GW), sb("update", P, NT, GW)
        o, sq = sb("o", P, 2, T), sb("sq", P, 2, T)
        act_step, dve_step = sem("act_step"), sem("dve_step")
        dist, exped, ready, cum_ready, cum_exped, qk_ready = (
            sem("dist"), sem("exped"), sem("scaled_ready"), sem("cum_ready"), sem("cum_exped"), sem("qk_ready"))
        tok_ready, states, scored, squared, q_scaled, o_used = sem("tok_ready"), sem("states"), sem("scored"), sem("squared"), sem("q_scaled"), sem("o_used")
        root, sq_used = sem("root"), sem("sq_used")
        to_dve, to_act = Ring(st, nc, "dve_bank", S.bank, [0, 1, 2, 3]), Ring(st, nc, "act_bank", S.bank, [4, 5, 6, 7])
        NL = len(LEVELS)
        with nc.Block() as block:
            @block.tensor
            def _(pe):
                heads_before, outs_before = 0, 0
                for n, (s, q, k, dk, val, v0, vw, mask, outs, nw) in enumerate(tiles):
                    heads = P // dk
                    if n == 0:
                        pe.wait_ge(q_scaled, 1)
                    for h in range(heads):
                        b, r = to_dve.fill(pe), slice(h * dk, (h + 1) * dk)
                        for c in range(NT):
                            cs = slice(c * P, (c + 1) * P)
                            last = nc.tensor.matmul(b[:, cs], k[r, cs], q[r, cs], start=True, stop=True, tile_position=(h * dk, 0))
                        last.then_inc(to_dve.full, 1)
                    for l in range(NL):
                        pe.wait_ge(ready, n * NL + l + 1)
                        x = scaled[:, l % 4, :]
                        for h in range(heads):
                            b, r = to_dve.fill(pe), slice(h * dk, (h + 1) * dk)
                            for c in range(NT):
                                cs = slice(c * P, (c + 1) * P)
                                last = nc.tensor.matmul(b[:, cs], x[r, cs], x[r, cs], start=True, stop=True, tile_position=(h * dk, 0))
                            last.then_inc(to_dve.full, 1)
                    pe.wait_ge(qk_ready, n + 1)
                    b = to_act.fill(pe)
                    for c in range(NT):
                        last = nc.tensor.transpose(b[:, c * P:(c + 1) * P], k_out[:, c * P:(c + 1) * P], S.ident[:, :])
                    last.then_inc(to_act.full, 1)
                    pe.wait_ge(tok_ready, n + 1)
                    per = HALF // vw
                    for c0 in range(0, NT, per):
                        b = to_dve.fill(pe)
                        for c in range(per):
                            last = nc.tensor.matmul(b[:, c * vw:(c + 1) * vw], k_out_tok[:, c0 + c, :], val[:, c0 + c, v0:v0 + vw], start=True, stop=True)
                        last.then_inc(to_dve.full, 1)
                    pe.wait_ge(scored, n + 1)
                    pe.wait_ge(states, n + 1)
                    for j, _ in enumerate(outs):
                        b = to_act.fill(pe)
                        for c in range(NT):
                            cs = slice(c * P, (c + 1) * P)
                            if c:
                                nc.tensor.matmul(b[:, cs], state[:, c, j * P:(j + 1) * P], q_in[:, cs], start=True, stop=False, skip_group_check=True)
                            for hh in range(2):
                                last = nc.tensor.matmul(b[hh * HD:(hh + 1) * HD, cs], val[:, c, v0 + j * P + hh * HD:v0 + j * P + (hh + 1) * HD],
                                                        scores[:, 2 * j + hh, cs], start=(c == 0), stop=True, tile_position=(0, hh * HD), skip_group_check=True)
                        last.then_inc(to_act.full, 1)
                    for j, _ in enumerate(outs):
                        outs_before += 1
                        pe.wait_ge(squared, outs_before)
                        b = to_act.fill(pe)
                        nc.tensor.matmul(b, S.head_mean[:, :], sq[:, j, :], start=True, stop=True).then_inc(to_act.full, 1)

            @block.scalar
            def _(act):
                step = Steps(act, act_step)
                f = nc.scalar.activation
                outs_before = 0
                for n, (s, q, k, dk, val, v0, vw, mask, outs, nw) in enumerate(tiles):
                    act.wait_ge(cum_ready, 2 * n + 1)
                    step(f(decay[:, :], cum[:, :], ACT.Exp, scale=s), cum_exped)
                    act.wait_ge(cum_ready, 2 * n + 2)
                    step(f(k_out[:, :], k_out[:, :], ACT.Exp, scale=s), cum_exped)
                    for l in range(NL):
                        act.wait_ge(dist, n * NL + l + 1)
                        x = scaled[:, l % 4, :]
                        step(f(x, x, ACT.Exp, scale=s), exped)
                    b = to_act.take(act)
                    step(f(k_out_tok[:, :, :], blocks4(b), ACT.Copy), to_act.freed)
                    act.sem_inc(tok_ready, 1)
                    if outs_before:
                        act.wait_ge(o_used, outs_before)
                    for j, _ in enumerate(outs):
                        b = to_act.take(act)
                        step(f(o[:, j, :], b, ACT.Copy), to_act.freed)
                        step(f(sq[:, j, :], o[:, j, :], ACT.Square), squared)
                    for j, _ in enumerate(outs):
                        b = to_act.take(act)
                        step(f(sq[:, j, :], b, ACT.Sqrt, bias=S.eps[:, 1:2]), to_act.freed)
                        act.sem_inc(root, 1)
                    outs_before += len(outs)

            @block.vector
            def _(dve):
                step = Steps(dve, dve_step)
                v = nc.vector
                outs_before = 0
                step(v.tensor_scalar(S.z[:, 0, :], S.z[:, 0, :], GLA_DK ** -0.5, None, ALU.mult), q_scaled)
                for n, (s, q, k, dk, val, v0, vw, mask, outs, nw) in enumerate(tiles):
                    heads = P // dk
                    halves = lambda ap, l: ap.rearrange("p (b h j) -> p b h j", h=2, j=LEVELS[l])

                    def distance(l):
                        m, c, x = LEVELS[l], halves(cum[:, :], l), halves(scaled[:, l % 4, :], l)
                        edge = c[:, :, 0, m - 1:m].broadcast_to([P, T // (2 * m), m])
                        step(v.tensor_tensor(x[:, :, 0, :], edge, c[:, :, 0, :], ALU.subtract))
                        step(v.tensor_tensor(x[:, :, 1, :], c[:, :, 1, :], edge, ALU.subtract), dist)

                    def times(l):
                        dve.wait_ge(exped, n * NL + l + 1)
                        x, kk, qq = halves(scaled[:, l % 4, :], l), halves(k, l), halves(q, l)
                        step(v.tensor_tensor(x[:, :, 0, :], x[:, :, 0, :], kk[:, :, 0, :], ALU.mult))
                        step(v.tensor_tensor(x[:, :, 1, :], x[:, :, 1, :], qq[:, :, 1, :], ALU.mult), ready)

                    def place(l):
                        for h in range(heads):
                            b = to_dve.take(dve)
                            step(v.copy_predicated(blocks4(scores[:, h, :]), over(S.lower[:, l, :].bitcast(U32), 4), blocks4(b)), to_dve.freed)

                    step(v.tensor_tensor_scan(cum[:, :], S.carry128[:, :], S.log_decay[:, n, :], 0.0, ALU.mult, ALU.add), cum_ready)
                    ends = blocks4(cum[:, :])
                    step(v.tensor_tensor(blocks4(k_out[:, :]), ends[:, :, P - 1:P].broadcast_to([P, 4, P]), ends, ALU.subtract), cum_ready)
                    distance(0)
                    distance(1)
                    for h in range(heads):
                        b = to_dve.take(dve)
                        step(v.tensor_tensor(blocks4(scores[:, h, :]), blocks4(b), over(S.ident[:, :], 4), ALU.mult), to_dve.freed)
                    dve.wait_ge(cum_exped, 2 * n + 2)
                    step(v.tensor_tensor(q_in[:, :], q, decay[:, :], ALU.mult))
                    step(v.tensor_tensor(k_out[:, :], k, k_out[:, :], ALU.mult), qk_ready)
                    for l in range(NL):
                        times(l)
                        if l + 2 < NL:
                            distance(l + 2)
                        if l:
                            place(l - 1)
                    place(NL - 1)
                    dve.sem_inc(scored, 1)
                    per = HALF // vw
                    for c0 in range(0, NT, per):
                        b = to_dve.take(dve)
                        step(v.tensor_tensor(update[:, c0:c0 + per, 0:vw], b.rearrange("p (c w) -> p c w", w=vw), over(mask[:, :], per), ALU.mult), to_dve.freed)
                    step(v.tensor_copy(state[:, 1, 0:vw], update[:, 0, 0:vw]))
                    for c in range(1, NT - 1):
                        step(v.scalar_tensor_tensor(state[:, c + 1, 0:vw], state[:, c, 0:vw], decay[:, (c + 1) * P - 1:(c + 1) * P],
                                                    update[:, c, 0:vw], ALU.mult, ALU.add))
                    dve.sem_inc(states, 1)
                    for j, (g, m) in enumerate(outs):
                        outs_before += 1
                        dve.wait_ge(root, outs_before)
                        rms_gate(nc, S, step, to_act, o[:, j, :], sq[:, j, :], S.z[:, g, :], par(nw), S.mixT[:, m, :])
                        dve.sem_inc(o_used, 1)


def stage_window(nc, S, A, i):
    S.tag = f"window{i}_"
    with Stage(nc, S.tag) as st:
        sem = lambda n: st.semaphore(n)
        sb = lambda n, *s: st.enter_context(nc.sbuf_tensor(S.tag + n, list(s), F32))
        s, pT = sb("s", P, 2, 4, 2 * P), sb("pT", P, 2, 4, 2, P)
        peak, neg, total, sink, inv = sb("peak", P, 4), sb("neg", P, 2, 4), sb("total", P, 2, 4), sb("sink", P, 2, 4), sb("inv", P, 4)
        act_step, dve_step = sem("act_step"), sem("dve_step")
        masked, exped, normed, turned = sem("masked"), sem("exped"), sem("normed"), sem("turned")
        to_dve, to_act = Ring(st, nc, "dve_bank", S.bank, [0, 1, 2, 3]), Ring(st, nc, "act_bank", S.bank, [4, 5])
        out_full = sem("out_full")
        SC = HD ** -0.5
        with nc.Block() as block:
            @block.tensor
            def _(pe):
                def scores(n):
                    for pair in range(2):
                        b, r = to_dve.fill(pe), slice(pair * HD, (pair + 1) * HD)
                        for g in range(2):
                            k0 = max(n - 1, 0) * P
                            w = (n + 1) * P - k0
                            last = nc.tensor.matmul(b[:, g * 2 * P:g * 2 * P + w], S.z[r, 10 + g, n * P:(n + 1) * P], S.z[r, 12, k0:k0 + w],
                                                    start=True, stop=True, tile_position=(pair * HD, 0))
                        last.then_inc(to_dve.full, 1)

                def values(n):
                    w = 1 if n == 0 else 2
                    pe.wait_ge(normed, n + 1)
                    for pair in range(2):
                        b = to_act.fill(pe)
                        for g in range(2):
                            for k in range(w):
                                at = (2 * g + k) * P
                                last = nc.tensor.transpose(b[:, at:at + P], s[:, n % 2, 2 * pair + g, k * P:(k + 1) * P], S.ident[:, :])
                        last.then_inc(to_act.full, 1)
                    pe.wait_ge(turned, 2 * n + 2)
                    for pair in range(2):
                        for g in range(2):
                            for k in range(w):
                                c = n if n == 0 else n - 1 + k
                                last = nc.tensor.matmul(S.bank[g * HD:(g + 1) * HD, 6 + pair, n * P:(n + 1) * P], S.v_swa[:, c, pair * HD:(pair + 1) * HD],
                                                        pT[:, n % 2, 2 * pair + g, k, :], start=(k == 0), stop=(k == w - 1),
                                                        tile_position=(0, g * HD), skip_group_check=True)
                    last.then_inc(out_full, 1)

                scores(0)
                for n in range(NT):
                    if n + 1 < NT:
                        scores(n + 1)
                    values(n)

            @block.scalar
            def _(act):
                step = Steps(act, act_step)
                f = nc.scalar.activation
                for n in range(NT):
                    w = P if n == 0 else 2 * P
                    e = n % 2
                    act.wait_ge(masked, n + 1)
                    for h in range(4):
                        step(f(s[:, e, h, 0:w], s[:, e, h, 0:w], ACT.Exp, bias=neg[:, e, h:h + 1], accum_out=total[:, e, h:h + 1]))
                        step(f(sink[:, e, h:h + 1], S.sinks[:, 4 * i + h:4 * i + h + 1], ACT.Exp, bias=neg[:, e, h:h + 1]))
                    act.sem_inc(exped, 1)
                    if n >= 2:
                        act.wait_ge(out_full, n - 1)
                    for pair in range(2):
                        b = to_act.take(act).rearrange("p (g k t) -> p g k t", g=2, k=2)
                        k = w // P
                        step(f(pT[:, e, 2 * pair:2 * pair + 2, 0:k, :], b[:, :, 0:k, :], ACT.Copy), to_act.freed)
                        act.sem_inc(turned, 1)
                act.wait_ge(out_full, NT)
                for pair in range(2):
                    step(f(S.mixT[:, 4 + pair, :], S.bank[:, 6 + pair, :], ACT.Copy))

            @block.vector
            def _(dve):
                step = Steps(dve, dve_step)
                v = nc.vector

                def mask(n):
                    e, w = n % 2, P if n == 0 else 2 * P
                    for pair in range(2):
                        b = to_dve.take(dve).rearrange("p (g k) -> p g k", g=2)
                        to = s[:, e, 2 * pair:2 * pair + 2, :]
                        if n:
                            step(v.scalar_tensor_tensor(to[:, :, 0:P], b[:, :, 0:P], SC, over(S.prev_bias[:, :], 2), ALU.mult, ALU.add))
                        step(v.scalar_tensor_tensor(to[:, :, w - P:w], b[:, :, w - P:w], SC, over(S.own_bias[:, :], 2), ALU.mult, ALU.add), to_dve.freed)
                    step(v.tensor_reduce(peak[:, :], s[:, e, :, 0:w], AX_X, ALU.max))
                    step(v.tensor_tensor(peak[:, :], peak[:, :], S.sinks[:, 4 * i:4 * i + 4], ALU.max))
                    step(v.tensor_scalar(neg[:, e, :], peak[:, :], -1.0, None, ALU.mult), masked)

                mask(0)
                for n in range(NT):
                    e, w = n % 2, P if n == 0 else 2 * P
                    if n + 1 < NT:
                        if n >= 1:
                            dve.wait_ge(turned, 2 * n)
                        mask(n + 1)
                    dve.wait_ge(exped, n + 1)
                    step(v.tensor_tensor(inv[:, :], total[:, e, :], sink[:, e, :], ALU.add))
                    step(v.reciprocal(inv[:, :], inv[:, :]))
                    step(v.tensor_tensor(s[:, e, :, 0:w], s[:, e, :, 0:w], inv[:, :].unsqueeze(2).broadcast_to([P, 4, w]), ALU.mult), normed)


def stage_rwkv(nc, S, A, i):
    S.tag = f"rwkv{i}_"
    par = lambda r: S.par[:, i * R_ROWS + r:i * R_ROWS + r + 1]
    HEADS = 4
    SIZES = [2, 4, 8, 16, 32]
    with Stage(nc, S.tag) as st:
        sem = lambda n: st.semaphore(n)
        sb = lambda n, *s: st.enter_context(nc.sbuf_tensor(S.tag + n, list(s), F32))
        cum, e_at, e_before, e_back = sb("cum", P, 2, T), sb("e_at", P, 2, T), sb("e_before", P, 2, T), sb("e_back", P, 2, T)
        kk, sq, bonus = sb("kk", P, 2, T), sb("sq", P, 2, T), sb("bonus", P, 2, T)
        rt, at, bt, kt = e_at, e_before, e_back, sb("kt", P, 2, T)
        end = sb("end", P, 2, NC64)
        b_tok, k_tok, v_tok = sb("b_tok", P, 2, NT, P), sb("k_tok", P, 2, NT, P), sb("v_tok", P, 2, NT, P)
        rhs = sb("rhs", P, HEADS, NT, P)
        ab, ak, rb, rk = sb("ab", P, HEADS, T), sb("ak", P, HEADS, T), sb("rb", P, HEADS, T), sb("rk", P, HEADS, T)
        inv, invT, part, w1 = sb("inv", P, HEADS, T), sb("invT", P, HEADS, T), sb("part", P, HEADS, T), sb("w1", P, HEADS, T)
        eye64 = sb("eye64", P, HD)
        oz = inv[:, :, :].rearrange("p h (c n) -> p h c n", n=P)
        split = lambda buf, n: buf[:, 2 * n:2 * n + 2, :].rearrange("p j (c n) -> p j c n", n=HD)
        pass_on, take_in, state = split(part, 0), split(part, 1), split(w1, 0)
        rr = kk
        y, ysq = cum, sq
        act_step, dve_step = sem("act_step"), sem("dve_step")
        k_sq, cum_ready, roots, e_ready, prods, bonus_in = sem("k_sq"), sem("cum_ready"), sem("roots"), sem("e_ready"), sem("prods"), sem("bonus_in")
        turned, masked, inv_ready, parts, w1_ready, inv_at, invT_at, rhs_ready, oz_ready = (
            sem("turned"), sem("masked"), sem("inv_ready"), sem("parts"), sem("w1_ready"), sem("inv_at"), sem("invT_at"), sem("rhs_ready"), sem("oz_ready"))
        ops_ready, state_at, rr_ready, y_ready, centred, ysq_ready = sem("ops_ready"), sem("state_at"), sem("rr_ready"), sem("y_ready"), sem("centred"), sem("ysq_ready")
        to_dve, to_act = Ring(st, nc, "dve_bank", S.bank, [0, 1, 2]), Ring(st, nc, "act_bank", S.bank, [3, 4, 5])
        chain = Ring(st, nc, "chain_bank", S.bank, [6, 7])
        rows = lambda h: slice((h % 2) * HD, (h % 2 + 1) * HD)
        val = S.v_first if i == 0 else S.v
        with nc.Block() as block:
            @block.tensor
            def _(pe):
                mm = nc.tensor.matmul

                def one(ring, lhs, rhs_, n=1):
                    b = ring.fill(pe)
                    mm(b, lhs, rhs_, start=True, stop=True).then_inc(ring.full, 1)

                for j in range(2):
                    pe.wait_ge(k_sq, j + 1)
                    one(to_act, S.head_ones[:, :], sq[:, j, :])
                for j in range(2):
                    pe.wait_ge(prods, 5 * j + 1)
                    one(to_dve, S.head_ones[:, :], S.rw_w[:, j, :])
                for j in range(2):
                    pe.wait_ge(prods, 5 * j + 5)
                    for src in (at, bt, kt, val):
                        b = to_act.fill(pe)
                        for c in range(NT):
                            last = nc.tensor.transpose(b[:, c * P:(c + 1) * P], src[:, j, c * P:(c + 1) * P], S.ident[:, :])
                        last.then_inc(to_act.full, 1)
                for h in range(HEADS):
                    r, j = rows(h), h // 2
                    for left, right in ((bt, at), (kt, at), (bt, rt), (kt, rt)):
                        b = to_dve.fill(pe)
                        for c in range(NT):
                            cs = slice(c * P, (c + 1) * P)
                            last = mm(b[:, cs], left[r, j, cs], right[r, j, cs], start=True, stop=True, tile_position=((h % 2) * HD, 0))
                        last.then_inc(to_dve.full, 1)
                for h in range(HEADS):
                    pe.wait_ge(inv_ready, h + 1)
                    b = to_act.fill(pe)
                    for c in range(NT):
                        last = nc.tensor.transpose(b[:, c * P:(c + 1) * P], invT[:, h, c * P:(c + 1) * P], S.ident[:, :])
                    last.then_inc(to_act.full, 1)
                for n, m in enumerate(SIZES):
                    last_size = n == len(SIZES) - 1
                    for h in range(HEADS):
                        pe.wait_ge(parts, n * HEADS + h + 1)
                        if n == 0:
                            pe.wait_ge(inv_at, h + 1)
                        b = to_act.fill(pe)
                        for c in range(NT):
                            cs = slice(c * P, (c + 1) * P)
                            last = mm(b[:, cs], part[:, h, cs], inv[:, h, cs], start=True, stop=True)
                        last.then_inc(to_act.full, 1)
                    for h in range(HEADS):
                        pe.wait_ge(w1_ready, n * HEADS + h + 1)
                        if not last_size:
                            b = to_dve.fill(pe)
                            for c in range(NT):
                                cs = slice(c * P, (c + 1) * P)
                                last = mm(b[:, cs], invT[:, h, cs], w1[:, h, cs], start=True, stop=True)
                            last.then_inc(to_dve.full, 1)
                        b = to_dve.fill(pe)
                        for c in range(NT):
                            cs = slice(c * P, (c + 1) * P)
                            last = mm(b[:, cs], w1[:, h, cs], invT[:, h, cs], start=True, stop=True)
                        last.then_inc(to_dve.full, 1)
                for h in range(HEADS):
                    b = to_act.fill(pe)
                    for c in range(NT):
                        last = mm(b[:, c * HD:(c + 1) * HD], ak[:, h, c * P:(c + 1) * P], v_tok[:, h // 2, c, rows(h)], start=True, stop=True)
                    last.then_inc(to_act.full, 1)
                for h in range(HEADS):
                    pe.wait_ge(rhs_ready, h + 1)
                    pe.wait_ge(invT_at, h + 1)
                    b = to_act.fill(pe)
                    for c in range(NT):
                        cs = slice(c * P, (c + 1) * P)
                        last = mm(b[:, cs], invT[:, h, cs], rhs[:, h, c, :], start=True, stop=True)
                    last.then_inc(to_act.full, 1)
                for j in range(2):
                    pe.wait_ge(oz_ready, 2 * j + 2)
                    for what in range(2):
                        for odd in range(2):
                            b, half = to_dve.fill(pe), slice(odd * HD, (odd + 1) * HD)
                            for c in range(NT):
                                for r in range(2):
                                    h = 2 * j + r
                                    o, pos = b[rows(h), c * HD:(c + 1) * HD], (odd * HD, r * HD)
                                    if what == 0:
                                        last = mm(o, oz[half, h, c, 0:HD], b_tok[half, j, c, rows(h)], start=True, stop=True, tile_position=pos, skip_group_check=True)
                                    else:
                                        mm(o, b_tok[half, j, c, rows(h)], oz[half, h, c, HD:P], start=True, stop=False, tile_position=pos, skip_group_check=True)
                                        last = mm(o, k_tok[half, j, c, rows(h)], v_tok[half, j, c, rows(h)], start=False, stop=True, tile_position=pos, skip_group_check=True)
                            last.then_inc(to_dve.full, 1)
                for j in range(2):
                    b = to_dve.fill(pe)
                    for r in range(2):
                        h = 2 * j + r
                        for c in range(NT):
                            last = mm(b[rows(h), c * P:(c + 1) * P], oz[:, h, c, 0:HD], rb[:, h, c * P:(c + 1) * P], start=True, stop=True,
                                      tile_position=(0, r * HD), skip_group_check=True)
                    last.then_inc(to_dve.full, 1)
                for c in range(1, NC64 - 1):
                    for j in range(2):
                        pe.wait_ge(state_at, 2 * c + j - 1)
                        b = chain.fill(pe)
                        for r in range(2):
                            q = slice(r * HD, (r + 1) * HD)
                            last = mm(b[q, 0:HD], pass_on[q, j, c, :], state[q, j, c, :], start=True, stop=True, tile_position=(r * HD, r * HD), skip_group_check=True)
                        last.then_inc(chain.full, 1)
                pe.wait_ge(state_at, 2 * (NC64 - 1))
                pe.wait_ge(rr_ready, 2)
                for j in range(2):
                    b = to_act.fill(pe)
                    for c in range(NT):
                        cs = slice(c * P, (c + 1) * P)
                        for r in range(2):
                            h = 2 * j + r
                            pos = (0, r * HD)
                            mm(b[rows(h), cs], oz[:, h, c, HD:P], rb[:, h, cs], start=True, stop=False, tile_position=pos, skip_group_check=True)
                            last = mm(b[rows(h), cs], v_tok[:, j, c, rows(h)], rk[:, h, cs], start=False, stop=False, tile_position=pos, skip_group_check=True)
                            for c2 in (2 * c, 2 * c + 1):
                                if c2:
                                    last = mm(b[rows(h), c2 * HD:(c2 + 1) * HD], state[rows(h), j, c2, :], rr[rows(h), j, c2 * HD:(c2 + 1) * HD],
                                              start=False, stop=True, tile_position=(r * HD, r * HD), skip_group_check=True)
                    last.then_inc(to_act.full, 1)
                for j in range(2):
                    pe.wait_ge(y_ready, j + 1)
                    one(to_dve, S.head_mean[:, :], y[:, j, :])
                for j in range(2):
                    pe.wait_ge(ysq_ready, j + 1)
                    one(to_act, S.head_mean[:, :], ysq[:, j, :])

            @block.scalar
            def _(act):
                step = Steps(act, act_step)
                f = nc.scalar.activation
                for j in range(2):
                    b = to_act.take(act)
                    step(f(sq[:, j, :], b, ACT.Sqrt), to_act.freed)
                    act.sem_inc(roots, 1)
                for j in range(2):
                    act.wait_ge(cum_ready, j + 1)
                    step(f(e_at[:, j, :], cum[:, j, :], ACT.Exp, bias=S.eps[:, 3:4]), e_ready)
                    step(f(e_back[:, j, :], cum[:, j, :], ACT.Exp, bias=S.eps[:, 4:5], scale=-1.0), e_ready)
                    step(f(e_before[:, j, :], e_before[:, j, :], ACT.Exp, bias=S.eps[:, 3:4]), e_ready)
                    step(f(end[:, j, :], cum[:, j, RW_CHUNK - 1:T:RW_CHUNK], ACT.Exp), e_ready)
                for j in range(2):
                    b = to_act.take(act).rearrange("p (c r n) -> p r c n", r=2, n=HD)
                    for r in range(2):
                        step(f(rhs[:, 2 * j + r, :, 0:HD], b[:, r, :, :], ACT.Copy), to_act.freed if r else None)
                    for to in (b_tok, k_tok, v_tok):
                        b = to_act.take(act)
                        step(f(to[:, j, :, :], blocks4(b), ACT.Copy), to_act.freed)
                act.sem_inc(turned, 1)
                for h in range(HEADS):
                    b = to_act.take(act)
                    step(f(inv[:, h, :], b, ACT.Copy), to_act.freed)
                    act.sem_inc(inv_at, 1)
                for n in range(len(SIZES)):
                    for h in range(HEADS):
                        b = to_act.take(act)
                        step(f(w1[:, h, :], b, ACT.Copy), to_act.freed)
                        act.sem_inc(w1_ready, 1)
                for h in range(HEADS):
                    b = to_act.take(act)
                    step(f(rhs[:, h, :, HD:P], b[:, 0:NT * HD].rearrange("p (c n) -> p c n", n=HD), ACT.Copy), to_act.freed)
                    act.sem_inc(rhs_ready, 1)
                for h in range(HEADS):
                    b = to_act.take(act)
                    step(f(oz[:, h, :, :], blocks4(b), ACT.Copy), to_act.freed)
                    act.sem_inc(oz_ready, 1)
                for j in range(2):
                    b = to_act.take(act)
                    step(f(y[:, j, :], b, ACT.Copy), to_act.freed)
                    act.sem_inc(y_ready, 1)
                for j in range(2):
                    act.wait_ge(centred, j + 1)
                    step(f(ysq[:, j, :], y[:, j, :], ACT.Square), ysq_ready)
                for j in range(2):
                    b = to_act.take(act)
                    step(f(ysq[:, j, :], b, ACT.Sqrt, bias=S.eps[:, 2:3]), to_act.freed)
                    act.sem_inc(roots, 1)

            @block.vector
            def _(dve):
                step = Steps(dve, dve_step)
                v = nc.vector
                tt, ts, stt = v.tensor_tensor, v.tensor_scalar, v.scalar_tensor_tensor
                step(tt(eye64[:, :], S.ident[:, 0:HD], S.ident[:, HD:P], ALU.add))
                for j in range(2):
                    step(ts(kk[:, j, :], S.k[:, j, :], par(R_KK + j), None, ALU.mult))
                    step(tt(sq[:, j, :], kk[:, j, :], kk[:, j, :], ALU.mult), k_sq)
                for j in range(2):
                    step(ts(S.rw_w[:, j, :], S.rw_w[:, j, :], -RW_RATE, None, ALU.mult))
                    step(v.tensor_tensor_scan(cum[:, j, :], S.carry64[:, :], S.rw_w[:, j, :], 0.0, ALU.mult, ALU.add))
                    step(tt(e_before[:, j, :], cum[:, j, :], S.rw_w[:, j, :], ALU.subtract), cum_ready)
                for j in range(2):
                    step(ts(kt[:, j, :], S.rw_a[:, j, :], 1.0, par(R_KA + j), ALU.subtract, ALU.mult))
                    step(stt(kt[:, j, :], kt[:, j, :], 1.0, S.k[:, j, :], ALU.add, ALU.mult))
                    step(stt(S.rw_w[:, j, :], kt[:, j, :], par(R_RK + j), S.r[:, j, :], ALU.mult, ALU.mult), prods)
                    dve.wait_ge(roots, j + 1)
                    step(ts(sq[:, j, :], sq[:, j, :], 1e-12, None, ALU.max))
                    step(v.reciprocal(sq[:, j, :], sq[:, j, :]))
                    step(tt(kk[:, j, :], kk[:, j, :], sq[:, j, :], ALU.mult))
                    dve.wait_ge(e_ready, 4 * j + 4)
                    step(tt(rt[:, j, :], S.r[:, j, :], e_at[:, j, :], ALU.mult), prods)
                    step(stt(at[:, j, :], kk[:, j, :], -1.0, e_before[:, j, :], ALU.mult, ALU.mult), prods)
                    step(tt(kt[:, j, :], kt[:, j, :], e_back[:, j, :], ALU.mult), prods)
                    step(tt(kk[:, j, :], kk[:, j, :], S.rw_a[:, j, :], ALU.mult))
                    step(tt(bt[:, j, :], kk[:, j, :], e_back[:, j, :], ALU.mult), prods)
                for j in range(2):
                    b = to_dve.take(dve)
                    step(tt(bonus[:, j, :], b, val[:, j, :], ALU.mult), to_dve.freed)
                for h in range(HEADS):
                    for to, mask in ((ab, S.chunk_before), (ak, S.chunk_before), (rb, S.chunk_upto), (rk, S.chunk_upto)):
                        b = to_dve.take(dve)
                        step(tt(blocks4(to[:, h, :]), blocks4(b), over(mask[:, :], 4), ALU.mult), to_dve.freed)
                for h in range(HEADS):
                    step(tt(blocks4(invT[:, h, :]), blocks4(ab[:, h, :]), over(S.lower[:, LEVELS.index(1), :], 4), ALU.mult))
                    step(tt(blocks4(invT[:, h, :]), blocks4(invT[:, h, :]), over(S.ident[:, :], 4), ALU.add), inv_ready)

                def part_of(n, h):
                    step(tt(blocks4(part[:, h, :]), blocks4(ab[:, h, :]), over(S.lower[:, LEVELS.index(SIZES[n]), :], 4), ALU.mult), parts)

                for h in range(HEADS):
                    part_of(0, h)
                for n in range(len(SIZES)):
                    last_size = n == len(SIZES) - 1
                    for h in range(HEADS):
                        if not last_size:
                            b = to_dve.take(dve)
                            step(tt(inv[:, h, :], inv[:, h, :], b, ALU.add), to_dve.freed)
                        b = to_dve.take(dve)
                        step(tt(invT[:, h, :], invT[:, h, :], b, ALU.add), to_dve.freed)
                        if last_size:
                            dve.sem_inc(invT_at, 1)
                        else:
                            part_of(n + 1, h)
                for j in range(2):
                    for odd in range(2):
                        b = to_dve.take(dve)[:, 0:NT * HD].rearrange("p (c n) -> p c n", n=HD)
                        step(tt(pass_on[:, j, odd:NC64:2, :], b, over(eye64[:, :], NT), ALU.add), to_dve.freed)
                    for odd in range(2):
                        b = to_dve.take(dve)[:, 0:NT * HD].rearrange("p (c n) -> p c n", n=HD)
                        step(tt(take_in[:, j, odd:NC64:2, :], b, end[:, j, odd:NC64:2].unsqueeze(2).broadcast_to([P, NT, HD]), ALU.mult), to_dve.freed)
                for j in range(2):
                    b = to_dve.take(dve)
                    step(tt(rr[:, j, :], b, rt[:, j, :], ALU.add), to_dve.freed)
                    dve.sem_inc(rr_ready, 1)
                for j in range(2):
                    step(v.tensor_copy(state[:, j, 1, :], take_in[:, j, 0, :]), state_at)
                for c in range(1, NC64 - 1):
                    for j in range(2):
                        b = chain.take(dve)
                        step(stt(state[:, j, c + 1, :], b[:, 0:HD], end[:, j, c:c + 1], take_in[:, j, c, :], ALU.mult, ALU.add), chain.freed)
                        dve.sem_inc(state_at, 1)
                for j in range(2):
                    b = to_dve.take(dve)
                    step(tt(y[:, j, :], y[:, j, :], b, ALU.subtract), to_dve.freed)
                    dve.sem_inc(centred, 1)
                for j in range(2):
                    dve.wait_ge(roots, 2 + j + 1)
                    step(v.reciprocal(ysq[:, j, :], ysq[:, j, :]))
                    step(tt(y[:, j, :], y[:, j, :], ysq[:, j, :], ALU.mult))
                    step(ts(y[:, j, :], y[:, j, :], par(R_LW + j), par(R_LB + j), ALU.mult, ALU.add))
                    step(tt(y[:, j, :], y[:, j, :], bonus[:, j, :], ALU.add))
                    step(tt(S.mixT[:, 6 + j, :], y[:, j, :], S.rw_g[:, j, :], ALU.mult))


class Norm:

    def __init__(self, st, nc, S, g, b, ring, normed, transposed):
        self.nc, self.S, self.g, self.b, self.ring, self.normed = nc, S, g, b, ring, normed
        sb = lambda n, *s: st.enter_context(nc.sbuf_tensor(S.tag + n, list(s), F32))
        self.stats, self.mv = sb("stats", P, NT, 2, 6), sb("mv", P, NT, 2)
        self.transposed = transposed
        self.var_ready, self.root_ready = st.semaphore("var_ready"), st.semaphore("root_ready")

    def statistics(self, step, t):
        v, S = self.nc.vector, self.S
        for h in range(2):
            step(v.bn_stats(self.stats[:, t, h, :], S.x[:, t, h * HALF:(h + 1) * HALF]))
        step(v.bn_aggr(self.mv[:, t, :], self.stats[:, t, :, :]), self.var_ready)

    def root(self, act, step, t):
        act.wait_ge(self.var_ready, t + 1)
        step(self.nc.scalar.activation(self.mv[:, t, 1:2], self.mv[:, t, 1:2], ACT.Sqrt, bias=self.S.eps[:, 0:1]), self.root_ready)

    def scale(self, dve, step, t):
        v, x, mv = self.nc.vector, self.S.x[:, t, :], self.mv
        dve.wait_ge(self.root_ready, t + 1)
        step(v.reciprocal(mv[:, t, 1:2], mv[:, t, 1:2]))
        step(v.tensor_scalar(x, x, mv[:, t, 0:1], mv[:, t, 1:2], ALU.subtract, ALU.mult))
        step(v.tensor_tensor(x, x, self.g, ALU.mult))
        step(v.tensor_tensor(x, x, self.b, ALU.add), self.normed)

    def transpose(self, pe, t):
        pe.wait_ge(self.normed, t + 1)
        for h in range(2):
            b = self.ring.fill(pe)
            for j in range(4):
                k = 4 * h + j
                last = self.nc.tensor.transpose(b[:, j * P:(j + 1) * P], self.S.x[:, t, k * P:(k + 1) * P], self.S.ident[:, :])
            last.then_inc(self.ring.full, 1)

    def copy(self, act, step, t):
        for h in range(2):
            b = self.ring.take(act)
            step(self.nc.scalar.activation(self.S.xT[:, 4 * h:4 * h + 4, t * P:(t + 1) * P], blocks4(b), ACT.Copy), self.ring.freed)


def load_rows(nc, eng, sem, g, b, g_dram, b_dram):
    eng.dma_start(g[:, :], g_dram.partition_broadcast(P)).then_inc(sem, 16)
    eng.dma_start(b[:, :], b_dram.partition_broadcast(P)).then_inc(sem, 16)


def stage_mix_out(nc, S, A, i):
    S.tag = f"mix_out{i}_"
    with Stage(nc, S.tag) as st:
        sem = lambda n: st.semaphore(n)
        sb = lambda n, *s: st.enter_context(nc.sbuf_tensor(S.tag + n, list(s), F32))
        wo, g, bb = sb("wo", P, KD, D), sb("g", P, D), sb("b", P, D)
        w_in = [sem(f"wo_in{k}") for k in range(KD)]
        gb_in, act_step, dve_step, normed = sem("gb_in"), sem("act_step"), sem("dve_step"), sem("normed")
        mm_ring, tr_ring = Ring(st, nc, "sum_bank", S.bank, [0, 1, 2, 3, 4, 5]), Ring(st, nc, "turn_bank", S.bank, [6, 7])
        norm = Norm(st, nc, S, g[:, :], bb[:, :], tr_ring, normed, None)
        with nc.Block() as block:
            @block.sync
            def _(sp):
                for k in range(KD):
                    sp.dma_start(wo[:, k, :], A.w_out[i, k * P:(k + 1) * P, :]).then_inc(w_in[k], 16)
                load_rows(nc, sp, gb_in, g, bb, A.ln1_g[i, :], A.ln1_b[i, :])

            @block.tensor
            def _(pe):
                for t in range(NT):
                    for h in range(2):
                        b = mm_ring.fill(pe)
                        for k in range(KD):
                            if t == 0 and h == 0:
                                pe.wait_ge(w_in[k], 16)
                            last = nc.tensor.matmul(b, S.mixT[:, k, t * P:(t + 1) * P], wo[:, k, h * HALF:(h + 1) * HALF], start=(k == 0), stop=(k == KD - 1))
                        last.then_inc(mm_ring.full, 1)
                    if t:
                        norm.transpose(pe, t - 1)
                norm.transpose(pe, NT - 1)

            @block.scalar
            def _(act):
                step = Steps(act, act_step)
                for t in range(NT):
                    norm.root(act, step, t)
                    norm.copy(act, step, t)

            @block.vector
            def _(dve):
                step = Steps(dve, dve_step)
                dve.wait_ge(gb_in, 32)
                for t in range(NT):
                    for h in range(2):
                        b, x = mm_ring.take(dve), S.x[:, t, h * HALF:(h + 1) * HALF]
                        step(nc.vector.scalar_tensor_tensor(x, x, ALPHA, b, ALU.mult, ALU.add), mm_ring.freed)
                    norm.statistics(step, t)
                    norm.scale(dve, step, t)


def stage_dense(nc, S, A, i):
    S.tag = f"dense{i}_"
    j = i // 2
    NS = 3
    CH = D_FF // GW
    wg_v = A.ffn_w_gate[j].rearrange("(k p) n -> p k n", p=P)
    wu_v = A.ffn_w_up[j].rearrange("(k p) n -> p k n", p=P)
    wd_v = A.ffn_w_down[j].rearrange("(c p) n -> p c n", p=P)
    DS = 6
    with Stage(nc, S.tag) as st:
        sem = lambda n: st.semaphore(n)
        sb = lambda n, *s: st.enter_context(nc.sbuf_tensor(S.tag + n, list(s), F32))
        wg, wu = sb("wg", P, NS, KD, GW), sb("wu", P, NS, KD, GW)
        g, bb = sb("g", P, D), sb("b", P, D)
        hT = sb("hT", P, F_TILES, T)
        sg = sb("sg", P, 2, T)
        w_in = [sem(f"w_in{n}") for n in range(NS)]
        d_in = [sem(f"d_in{n}") for n in range(DS)]
        gb_in, act_step, dve_step, normed, silu, multiplied, down_done = (
            sem("gb_in"), sem("act_step"), sem("dve_step"), sem("normed"), sem("silu"), sem("multiplied"), sem("down_done"))
        gate, up = Ring(st, nc, "gate_bank", S.bank, [0, 1, 2]), Ring(st, nc, "up_bank", S.bank, [3, 4, 5])
        tr_ring = Ring(st, nc, "turn_bank", S.bank, [0, 1])
        sums = sem("sums_full")
        norm = Norm(st, nc, S, g[:, :], bb[:, :], tr_ring, normed, None)
        down = [w[:, n, :, :].rearrange("p k n -> p (k n)").rearrange("p (c n) -> p c n", c=2) for w in (wg, wu) for n in range(NS)]
        with nc.Block() as block:
            @block.sync
            def _(sp):
                load_rows(nc, sp, gb_in, g, bb, A.ln2_g[i, :], A.ln2_b[i, :])
                for c in range(CH):
                    if c >= NS:
                        sp.wait_ge(up.full, 2 * (c - NS) + 2)
                    sp.dma_start(wg[:, c % NS, :, :], wg_v[:, :, c * GW:(c + 1) * GW]).then_inc(w_in[c % NS], 16)
                    sp.dma_start(wu[:, c % NS, :, :], wu_v[:, :, c * GW:(c + 1) * GW]).then_inc(w_in[c % NS], 16)
                for c in range(CH):
                    if c < DS:
                        n = c % NS
                        last = max(q for q in range(CH) if q % NS == n)
                        sp.wait_ge(up.full, 2 * last + 2)
                    else:
                        sp.wait_ge(down_done, c - DS + 1)
                    sp.dma_start(down[c % DS], wd_v[:, 2 * c:2 * c + 2, :]).then_inc(d_in[c % DS], 16)

            @block.tensor
            def _(pe):
                for c in range(CH):
                    pe.wait_ge(w_in[c % NS], 32 * (c // NS + 1))
                    for q in range(2):
                        for ring, w in ((gate, wg), (up, wu)):
                            b = ring.fill(pe)
                            for k in range(KD):
                                last = nc.tensor.matmul(b, w[:, c % NS, k, q * P:(q + 1) * P], S.xT[:, k, :], start=(k == 0), stop=(k == KD - 1))
                            last.then_inc(ring.full, 1)
                pe.wait_ge(gate.freed, F_TILES)
                pe.wait_ge(up.freed, F_TILES)
                for c in range(CH):
                    pe.wait_ge(d_in[c % DS], 16 * (c // DS + 1))
                    for q in range(2):
                        f = 2 * c + q
                        pe.wait_ge(multiplied, f + 1)
                        for t in range(NT):
                            for h in range(2):
                                last = nc.tensor.matmul(S.bank[:, 2 * t + h, :], hT[:, f, t * P:(t + 1) * P], down[c % DS][:, q, h * HALF:(h + 1) * HALF],
                                                        start=(f == 0), stop=(f == F_TILES - 1), skip_group_check=True)
                    last.then_inc(down_done, 1)
                for t in range(NT):
                    norm.transpose(pe, t)

            @block.scalar
            def _(act):
                step = Steps(act, act_step)
                for f in range(F_TILES):
                    if f >= 2:
                        act.wait_ge(multiplied, f - 1)
                    b = gate.take(act)
                    step(nc.scalar.activation(sg[:, f % 2, :], b, ACT.Silu), gate.freed)
                    act.sem_inc(silu, 1)
                for t in range(NT):
                    norm.root(act, step, t)
                for t in range(NT):
                    norm.copy(act, step, t)

            @block.vector
            def _(dve):
                step = Steps(dve, dve_step)
                for f in range(F_TILES):
                    dve.wait_ge(silu, f + 1)
                    b = up.take(dve)
                    step(nc.vector.tensor_tensor(hT[:, f, :], b, sg[:, f % 2, :], ALU.mult), up.freed)
                    dve.sem_inc(multiplied, 1)
                dve.wait_ge(gb_in, 32)
                dve.wait_ge(down_done, CH)
                for t in range(NT):
                    for h in range(2):
                        x = S.x[:, t, h * HALF:(h + 1) * HALF]
                        step(nc.vector.scalar_tensor_tensor(x, x, ALPHA, S.bank[:, 2 * t + h, :], ALU.mult, ALU.add))
                    norm.statistics(step, t)
                for t in range(NT):
                    norm.scale(dve, step, t)


def stage_embedding(nc, S, A, i, out):
    S.tag = f"embedding{i}_"
    last_layer = i == DEPTH - 1
    KP = GW // P
    with Stage(nc, S.tag) as st:
        sem = lambda n: st.semaphore(n)
        sb = lambda n, *s: st.enter_context(nc.sbuf_tensor(S.tag + n, list(s), F32))
        wg, wp = sb("wg", P, KD, D), sb("wp", P, KP, D)
        p, pT = sb("p", P, NT, GW), sb("pT", P, KP, T)
        sg = sb("sg", P, 4, HALF)
        wg_in = [sem(f"wg_in{h}") for h in range(2)]
        wp_in, p_in, act_step, dve_step, sig, added, turned, stored = (
            sem("wp_in"), sem("p_in"), sem("act_step"), sem("dve_step"), sem("sig"), sem("added"), sem("p_turned"), sem("stored"))
        gate, proj = Ring(st, nc, "gate_bank", S.bank, [0, 1, 2]), Ring(st, nc, "proj_bank", S.bank, [3, 4, 5])
        tr_ring = Ring(st, nc, "turn_bank", S.bank, [6, 7])
        with nc.Block() as block:
            @block.sync
            def _(sp):
                sp.dma_start(p[:, :, :], A.p[i, 0].rearrange("(t p) n -> p t n", p=P)).then_inc(p_in, 16)
                sp.dma_start(wp[:, :, :], A.ple_proj[i].rearrange("(k p) n -> p k n", p=P)).then_inc(wp_in, 16)
                for h in range(2):
                    sp.dma_start(wg[:, :, h * HALF:(h + 1) * HALF], A.ple_gate[i].rearrange("(k p) n -> p k n", p=P)[:, :, h * HALF:(h + 1) * HALF]).then_inc(wg_in[h], 16)
                if last_layer:
                    for t in range(NT):
                        sp.wait_ge(added, 2 * t + 2)
                        sp.dma_start(out[0, t * P:(t + 1) * P, :], S.x[:, t, :]).then_inc(stored, 16)
                    sp.wait_ge(stored, 16 * NT)

            @block.tensor
            def _(pe):
                pe.wait_ge(p_in, 16)
                for k in range(KP):
                    b = tr_ring.fill(pe)
                    for t in range(NT):
                        last = nc.tensor.transpose(b[:, t * P:(t + 1) * P], p[:, t, k * P:(k + 1) * P], S.ident[:, :])
                    last.then_inc(tr_ring.full, 1)
                pe.wait_ge(turned, KP)
                pe.wait_ge(wp_in, 16)

                def turn(t):
                    pe.wait_ge(added, 2 * t + 2)
                    for h in range(2):
                        b = tr_ring.fill(pe)
                        for j in range(4):
                            k = 4 * h + j
                            last = nc.tensor.transpose(b[:, j * P:(j + 1) * P], S.x[:, t, k * P:(k + 1) * P], S.ident[:, :])
                        last.then_inc(tr_ring.full, 1)

                for t in range(NT):
                    for h in range(2):
                        cols, ts = slice(h * HALF, (h + 1) * HALF), slice(t * P, (t + 1) * P)
                        b = proj.fill(pe)
                        for k in range(KP):
                            last = nc.tensor.matmul(b, pT[:, k, ts], wp[:, k, cols], start=(k == 0), stop=(k == KP - 1))
                        last.then_inc(proj.full, 1)
                        b = gate.fill(pe)
                        pe.wait_ge(wg_in[h], 16)
                        for k in range(KD):
                            last = nc.tensor.matmul(b, S.xT[:, k, ts], wg[:, k, cols], start=(k == 0), stop=(k == KD - 1))
                        last.then_inc(gate.full, 1)
                    if t and not last_layer:
                        turn(t - 1)
                if not last_layer:
                    turn(NT - 1)

            @block.scalar
            def _(act):
                step = Steps(act, act_step)
                for k in range(KP):
                    b = tr_ring.take(act)
                    step(nc.scalar.activation(pT[:, k, :], b, ACT.Copy), tr_ring.freed)
                    act.sem_inc(turned, 1)

                def copy(t):
                    for h in range(2):
                        b = tr_ring.take(act)
                        step(nc.scalar.activation(S.xT[:, 4 * h:4 * h + 4, t * P:(t + 1) * P], blocks4(b), ACT.Copy), tr_ring.freed)

                for n in range(2 * NT):
                    if n >= 4:
                        act.wait_ge(added, n - 3)
                    b = gate.take(act)
                    step(nc.scalar.activation(sg[:, n % 4, :], b, ACT.Sigmoid), gate.freed)
                    act.sem_inc(sig, 1)
                    if n >= 3 and n % 2 and not last_layer:
                        copy(n // 2 - 1)
                if not last_layer:
                    copy(NT - 1)

            @block.vector
            def _(dve):
                step = Steps(dve, dve_step)
                for n in range(2 * NT):
                    t, h = n // 2, n % 2
                    x = S.x[:, t, h * HALF:(h + 1) * HALF]
                    dve.wait_ge(sig, n + 1)
                    b = proj.take(dve)
                    step(nc.vector.tensor_tensor(sg[:, n % 4, :], sg[:, n % 4, :], b, ALU.mult), proj.freed)
                    step(nc.vector.tensor_tensor(x, x, sg[:, n % 4, :], ALU.add), added)


def stage_route(nc, S, A, j):
    S.tag = "route_"
    with Stage(nc, S.tag) as st:
        sem = lambda n: st.semaphore(n)
        sb = lambda n, s, dt=F32: st.enter_context(nc.sbuf_tensor(S.tag + n, s, dt))
        router, logits = sb("router", [P, KD, N_EXP]), sb("logits", [P, NT, N_EXP])
        top, idx, idxf = sb("top", [P, NT, 8]), sb("idx", [P, NT, 8], U32), sb("idxf", [P, NT, 8])
        first, second, member = sb("first", [P, NT, N_EXP]), sb("second", [P, NT, N_EXP]), sb("member", [P, NT, N_EXP])
        e2, g = sb("e2", [P, NT]), sb("gates2", [P, NT])
        counts, more, running = sb("counts", [P, N_EXP]), sb("more", [P, N_EXP]), sb("running", [P, N_EXP])
        r_in, logits_full, dve_step, act_step, gap, exped, member_ready, counted = (
            sem("router_in"), sem("logits_full"), sem("dve_step"), sem("act_step"), sem("gap_ready"), sem("exped"), sem("member_ready"), sem("counted"))
        with nc.Block() as block:
            @block.sync
            def _(sp):
                sp.dma_start(router[:, :, :], A.moe_router[j].rearrange("(k p) e -> p k e", p=P)).then_inc(r_in, 16)

            @block.tensor
            def _(pe):
                pe.wait_ge(r_in, 16)
                for t in range(NT):
                    for k in range(KD):
                        last = nc.tensor.matmul(S.bank[:, 0, t * N_EXP:(t + 1) * N_EXP], S.xT[:, k, t * P:(t + 1) * P], router[:, k, :], start=(k == 0), stop=(k == KD - 1))
                last.then_inc(logits_full, 1)
                pe.wait_ge(member_ready, 1)
                for t in range(NT + 1):
                    o = S.bank[:, 1, t * N_EXP:(t + 1) * N_EXP]
                    for s in range(min(t, NT - 1) + 1):
                        left = S.before if s == t else S.ones
                        last = nc.tensor.matmul(o, left[:, :], member[:, s, :], start=(s == 0), stop=(s == min(t, NT - 1)))
                last.then_inc(counted, 1)

            @block.scalar
            def _(act):
                act.wait_ge(gap, 1)
                nc.scalar.activation(e2[:, :], e2[:, :], ACT.Exp).then_inc(exped, 1)

            @block.vector
            def _(dve):
                step = Steps(dve, dve_step)
                v = nc.vector
                dve.wait_ge(logits_full, 1)
                step(v.tensor_copy(logits[:, :, :], S.bank[:, 0, 0:NT * N_EXP].rearrange("p (t e) -> p t e", t=NT)))
                for t in range(NT):
                    step(v.max(top[:, t, :], logits[:, t, :]))
                    step(v.max_index(idx[:, t, :], top[:, t, :], logits[:, t, :]))
                step(v.tensor_tensor(e2[:, :], top[:, :, 1], top[:, :, 0], ALU.subtract), gap)
                step(v.tensor_copy(idxf[:, :, :], idx[:, :, :]))
                for k, to in ((0, first), (1, second)):
                    step(v.tensor_tensor(to[:, :, :], over(S.slots[:, 0:N_EXP], NT), idxf[:, :, k:k + 1].broadcast_to([P, NT, N_EXP]), ALU.is_equal))
                step(v.tensor_tensor(member[:, :, :], first[:, :, :], second[:, :, :], ALU.add), member_ready)
                dve.wait_ge(exped, 1)
                step(v.tensor_scalar(g[:, :], e2[:, :], 1.0, None, ALU.add))
                step(v.reciprocal(g[:, :], g[:, :]))
                step(v.tensor_tensor(e2[:, :], e2[:, :], g[:, :], ALU.mult))
                wide = lambda ap: ap.unsqueeze(2).broadcast_to([P, NT, N_EXP])
                step(v.tensor_tensor(first[:, :, :], first[:, :, :], wide(g[:, :]), ALU.mult))
                step(v.tensor_tensor(second[:, :, :], second[:, :, :], wide(e2[:, :]), ALU.mult))
                step(v.tensor_tensor(S.gates[:, :, :], first[:, :, :], second[:, :, :], ALU.add))
                dve.wait_ge(counted, 1)
                step(v.scalar_tensor_tensor(S.place[:, :, :], S.bank[:, 1, 0:NT * N_EXP].rearrange("p (t e) -> p t e", t=NT), 1.0, member[:, :, :], ALU.add, ALU.mult))
                step(v.tensor_scalar(S.place[:, :, :], S.place[:, :, :], -1.0, None, ALU.add))
                step(v.tensor_scalar(more[:, :], S.bank[:, 1, NT * N_EXP:(NT + 1) * N_EXP], float(P), 1.0, ALU.is_gt, ALU.add))
                step(v.tensor_copy(counts[:, :], S.bank[:, 1, NT * N_EXP:(NT + 1) * N_EXP]))
                for n in range(2, NT):
                    step(v.scalar_tensor_tensor(more[:, :], counts[:, :], float(n * P), more[:, :], ALU.is_gt, ALU.add))
                step(v.tensor_tensor_scan(running[:, :], S.ones[:, 0:N_EXP], more[:, :], 0.0, ALU.mult, ALU.add))
                step(v.tensor_tensor(running[:, :], running[:, :], more[:, :], ALU.subtract))
                step(v.tensor_copy(S.blocks[0:1, 0:N_EXP], more[0:1, :]))
                step(v.tensor_copy(S.blocks[0:1, N_EXP:2 * N_EXP], running[0:1, :]))


def stage_experts(nc, S, A, i):
    S.tag = f"experts{i}_"
    j = i // 2
    FC = 512
    NCH = D_FFE // FC
    Q = FC // P
    wg_v = A.moe_w_gate[j].rearrange("e (k p) n -> e p k n", p=P)
    wu_v = A.moe_w_up[j].rearrange("e (k p) n -> e p k n", p=P)
    wd_v = A.moe_w_down[j].rearrange("e (c p) n -> e p c n", p=P)
    with Stage(nc, S.tag) as st:
        sem = lambda n: st.semaphore(n)
        sb = lambda n, *s: st.enter_context(nc.sbuf_tensor(S.tag + n, list(s), F32))
        wg = [sb(f"wg{n}", P, KD, FC) for n in range(2)]
        wu = [sb(f"wu{n}", P, KD, FC) for n in range(2)]
        wd = [sb(f"wd{n}", P, Q, D) for n in range(2)]
        xg = sb("xg", P, NT * KD * P)
        ysum = sb("ysum", P, NT * D)
        acc = sb("acc", P, NT, D)
        pick, pick_w, back = sb("pick", P, NT, P), sb("pick_w", P, NT, P), sb("back", P, NT, P)
        sg, hT = sb("sg", P, 2, P), sb("hT", P, Q, P)
        landed = [sem(f"w_landed{n}") for n in range(2)]
        gate_full, up_full, gate_free, up_free = sem("gate_full"), sem("up_full"), sem("gate_free"), sem("up_free")
        y_full, y_free, pick_ready, gath_full, gath_done = sem("y_full"), sem("y_free"), sem("pick_ready"), sem("gath_full"), sem("gath_done")
        back_pick, back_turned, back_ready, sc_full, sc_done = sem("back_pick"), sem("back_turned"), sem("back_ready"), sem("sc_full"), sem("sc_done")
        slot_free = [sem(f"slot_free{n}") for n in range(2)]
        cleared, gb_in, act_step, dve_step, normed = sem("cleared"), sem("gb_in"), sem("act_step"), sem("dve_step"), sem("normed")
        G, U = (0, 2), (1, 3)
        bank = S.bank

        def experts(eng):
            with eng.Fori(0, N_EXP // 2) as pair:
                for e2 in range(2):
                    e = pair * 2 + e2
                    nb = eng.value_load(S.blocks[0:1, bass.ds(e, 1)], min_val=1, max_val=NT)
                    base = eng.value_load(S.blocks[0:1, bass.ds(e + N_EXP, 1)], min_val=0, max_val=2 * N_EXP)
                    yield pair, e2, e, nb, base

        def chunks(eng, pair, e2):
            with eng.Fori(0, NCH // 2) as c2:
                for h in range(2):
                    yield c2 * 2 + h, (e2 + h) % 2, pair * NCH + c2 + (NCH * e2 + h) // 2
            yield NCH - 1, (e2 + NCH - 1) % 2, pair * NCH + NCH // 2 + (NCH * e2) // 2

        with nc.Block() as block:
            @block.sync
            def _(sp):
                for pair, e2, e, nb, base in experts(sp):
                    for c, s, use in chunks(sp, pair, e2):
                        sp.wait_ge(slot_free[s], use + 1)
                        sp.dma_start(wg[s][:, :, :], wg_v[bass.ds(e, 1), :, :, bass.ds(c * FC, FC)].rearrange("a p k n -> (a p) k n")).then_inc(landed[s], 16)
                        sp.dma_start(wu[s][:, :, :], wu_v[bass.ds(e, 1), :, :, bass.ds(c * FC, FC)].rearrange("a p k n -> (a p) k n")).then_inc(landed[s], 16)
                        sp.dma_start(wd[s][:, :, :], wd_v[bass.ds(e, 1), :, bass.ds(c * Q, Q), :].rearrange("a p c n -> (a p) c n")).then_inc(landed[s], 16)

            @block.tensor
            def _(pe):
                mm = nc.tensor.matmul
                pe.wait_ge(cleared, 1)
                for pair, e2, e, nb, base in experts(pe):
                    with pe.Fori(0, nb) as b:
                        v = base + b
                        pe.wait_ge(sc_done, base * 8 + 1)
                        pe.wait_ge(pick_ready, v + 1)
                        pe.wait_ge(gath_done, v * 2 + 1)
                        for h in range(2):
                            for q in range(4):
                                k = 4 * h + q
                                for t in range(NT):
                                    last = mm(bank[:, 6 + h, q * P:(q + 1) * P], S.x[:, t, k * P:(k + 1) * P], pick[:, t, :], start=(t == 0), stop=(t == NT - 1))
                            last.then_inc(gath_full, 1)
                    for c, s, use in chunks(pe, pair, e2):
                        with pe.Fori(0, nb) as b:
                            u = base * NCH + c * nb + b
                            pe.wait_ge(gath_done, (base + b) * 2 + 3)
                            pe.wait_ge(landed[s], use * 48 + 48)

                            def gate_up(q):
                                pe.wait_ge(gate_free, u * Q + (q + 1))
                                for k in range(KD):
                                    last = mm(bank[:, G[q % 2], 0:P], wg[s][:, k, q * P:(q + 1) * P], xg[:, bass.ds(b * (KD * P) + k * P, P)], start=(k == 0), stop=(k == KD - 1))
                                last.then_inc(gate_full, 1)
                                pe.wait_ge(up_free, u * Q + (q + 1))
                                for k in range(KD):
                                    last = mm(bank[:, U[q % 2], 0:P], wu[s][:, k, q * P:(q + 1) * P], xg[:, bass.ds(b * (KD * P) + k * P, P)], start=(k == 0), stop=(k == KD - 1))
                                last.then_inc(up_full, 1)

                            def down(q):
                                pe.wait_ge(up_free, u * Q + (q + 3))
                                if q == 0:
                                    pe.wait_ge(y_free, u + 1)
                                for h in range(2):
                                    last = mm(bank[:, 4 + h, :], hT[:, q, :], wd[s][:, q, h * HALF:(h + 1) * HALF], start=(q == 0), stop=(q == Q - 1))
                                if q == Q - 1:
                                    last.then_inc(y_full, 1)

                            gate_up(0)
                            for q in range(1, Q):
                                gate_up(q)
                                down(q - 1)
                            down(Q - 1)
                    with pe.Fori(0, nb) as b:
                        v = base + b
                        pe.wait_ge(y_free, (base + nb) * NCH + 1)
                        pe.wait_ge(back_pick, v + 1)
                        pe.wait_ge(sc_done, v * 8 + 1)
                        for t in range(NT):
                            last = nc.tensor.transpose(bank[:, 6, t * P:(t + 1) * P], pick_w[:, t, :], S.ident[:, :])
                        last.then_inc(back_turned, 1)
                        pe.wait_ge(back_ready, v + 1)
                        for t in range(NT):
                            for h in range(2):
                                mm(bank[:, 2 * t + h, :], back[:, t, :], ysum[:, bass.ds(b * D + h * HALF, HALF)], start=True, stop=True).then_inc(sc_full, 1)

            @block.scalar
            def _(act):
                act.sem_inc(gate_free, 2)
                for pair, e2, e, nb, base in experts(act):
                    for c, s, use in chunks(act, pair, e2):
                        with act.Fori(0, nb) as b:
                            u = base * NCH + c * nb + b
                            for q in range(Q):
                                act.wait_ge(gate_full, u * Q + (q + 1))
                                act.wait_ge(up_free, u * Q + (q + 1))
                                nc.scalar.activation(sg[:, q % 2, :], bank[:, G[q % 2], 0:P], ACT.Silu).then_inc(gate_free, 1)
                    with act.Fori(0, nb) as b:
                        v = base + b
                        act.wait_ge(back_turned, v + 1)
                        nc.scalar.activation(back[:, :, :], blocks4(bank[:, 6, :]), ACT.Copy).then_inc(back_ready, 1)

            @block.vector
            def _(dve):
                v_ = nc.vector
                dve.sem_inc(up_free, 2)
                for n in (y_free, gath_full, gath_done, sc_done, slot_free[0], slot_free[1]):
                    dve.sem_inc(n, 1)
                v_.memset(acc[:, :, :], 0.0).then_inc(cleared, 1)
                dve.wait_ge(cleared, 1)
                for pair, e2, e, nb, base in experts(dve):
                    with dve.Fori(0, nb) as b:
                        v = base + b
                        dve.wait_ge(gath_full, v * 2 + 1)
                        for t in range(NT):
                            last = v_.tensor_scalar(pick[:, t, :], S.slots[:, bass.ds(b * P, P)], S.place[:, t, bass.ds(e, 1)], None, ALU.is_equal)
                        last.then_inc(pick_ready, 1)
                        v_.tensor_scalar(ysum[:, bass.ds(b * D, D)], acc[:, 0, :], 0.0, None, ALU.mult).then_inc(dve_step, 1)
                        for h in range(2):
                            dve.wait_ge(gath_full, v * 2 + (h + 2))
                            v_.tensor_scalar(xg[:, bass.ds(b * (KD * P) + h * HALF, HALF)], bank[:, 6 + h, :], 1.0, None, ALU.mult).then_inc(gath_done, 1)
                    for c, s, use in chunks(dve, pair, e2):
                        with dve.Fori(0, nb) as b:
                            u = base * NCH + c * nb + b
                            for q in range(Q):
                                dve.wait_ge(up_full, u * Q + (q + 1))
                                dve.wait_ge(gate_free, u * Q + (q + 3))
                                v_.tensor_tensor(hT[:, q, :], sg[:, q % 2, :], bank[:, U[q % 2], 0:P], ALU.mult).then_inc(up_free, 1)
                            dve.wait_ge(y_full, u + 1)
                            dve.wait_ge(y_free, u + 1)
                            dve.wait_ge(dve_step, base + nb)
                            for h in range(2):
                                y = ysum[:, bass.ds(b * D + h * HALF, HALF)]
                                last = v_.tensor_tensor(y, y, bank[:, 4 + h, :], ALU.add)
                            last.then_inc(y_free, 1)
                        dve.sem_inc(slot_free[s], 1)
                    with dve.Fori(0, nb) as b:
                        v = base + b
                        for t in range(NT):
                            last = v_.tensor_scalar(pick_w[:, t, :], S.slots[:, bass.ds(b * P, P)], S.place[:, t, bass.ds(e, 1)], S.gates[:, t, bass.ds(e, 1)],
                                                    ALU.is_equal, ALU.mult)
                        last.then_inc(back_pick, 1)
                        for n in range(2 * NT):
                            dve.wait_ge(sc_full, v * 8 + (n + 1))
                            dve.wait_ge(sc_done, v * 8 + (n + 1))
                            a = acc[:, n // 2, (n % 2) * HALF:(n % 2 + 1) * HALF]
                            v_.tensor_tensor(a, a, bank[:, n, :], ALU.add).then_inc(sc_done, 1)

        with nc.Block() as block:
            g, bb = wg[0][:, 0:2, :].rearrange("p k n -> p (k n)"), wg[1][:, 0:2, :].rearrange("p k n -> p (k n)")
            tr_ring = Ring(st, nc, "turn_bank", S.bank, [0, 1, 2, 3])
            norm = Norm(st, nc, S, g, bb, tr_ring, normed, None)

            @block.sync
            def _(sp):
                load_rows(nc, sp, gb_in, g, bb, A.ln2_g[i, :], A.ln2_b[i, :])

            @block.tensor
            def _(pe):
                for t in range(NT):
                    norm.transpose(pe, t)

            @block.scalar
            def _(act):
                step = Steps(act, act_step)
                for t in range(NT):
                    norm.root(act, step, t)
                    norm.copy(act, step, t)

            @block.vector
            def _(dve):
                dve_step2 = st.semaphore("norm_step")
                step = Steps(dve, dve_step2)
                dve.wait_ge(gb_in, 32)
                for t in range(NT):
                    step(nc.vector.scalar_tensor_tensor(S.x[:, t, :], S.x[:, t, :], ALPHA, acc[:, t, :], ALU.mult, ALU.add))
                    norm.statistics(step, t)
                    norm.scale(dve, step, t)


def build_trunk(nc, A, out):
    with ExitStack() as ctx:
        sb = lambda n, s, dt=F32: ctx.enter_context(nc.sbuf_tensor(n, s, dt))
        S = Buffers()
        S.bank = ctx.enter_context(nc.psum_tensor("bank", [P, 8, HALF], F32))
        S.x = sb("x_tok", [P, NT, D])
        S.xT = sb("x_ch", [P, KD, T])
        S.mixT = S.xT
        S.v_first = sb("v_first", [P, 2, T])
        S.ident, S.lower = sb("ident", [P, P]), sb("lower", [P, len(LEVELS), P])
        S.head_ones, S.head_mean = sb("head_ones", [P, P]), sb("head_mean", [P, P])
        S.chunk_before, S.chunk_upto = sb("chunk_before", [P, P]), sb("chunk_upto", [P, P])
        S.gla_heads = sb("gla_heads", [P, GW])
        S.own_bias, S.prev_bias = sb("own_bias", [P, P]), sb("prev_bias", [P, P])
        S.ones, S.before, S.slots = sb("ones", [P, P]), sb("before", [P, P]), sb("slots", [P, T])
        S.eps, S.par, S.sinks = sb("eps", [P, 8]), sb("par", [P, DEPTH * R_ROWS]), sb("sinks", [P, DEPTH * 4])
        S.lb = sb("lb", [P, 10])
        with ExitStack() as low:
            sl = lambda n, s: low.enter_context(nc.sbuf_tensor(n, s, F32))
            S.carry128, S.carry64 = sl("carry128", [P, T]), sl("carry64", [P, T])
            S.w_low, S.w_up = sl("w_low", [P, KD, P]), sl("w_up", [P, U_END])
            stage_constants(nc, S, A)
            for i in range(DEPTH):
                with ExitStack() as lay:
                    sy = lambda n, s: lay.enter_context(nc.sbuf_tensor(f"{n}_layer{i}", s, F32))
                    S.rw_w, S.rw_a, S.rw_g = sy("rw_w", [P, 2, T]), sy("rw_a", [P, 2, T]), sy("rw_g", [P, 2, T])
                    S.r, S.k, S.v = sy("r", [P, 2, T]), sy("k", [P, 2, T]), sy("v", [P, 2, T]) if i else None
                    with ExitStack() as pre:
                        sp = lambda n, s: pre.enter_context(nc.sbuf_tensor(f"{n}_layer{i}", s, F32))
                        S.z = sp("z", [P, 13, T])
                        S.zr = sp("zr", [P, 7, T + 1])
                        S.v_gla, S.v_hgrn, S.v_swa = sp("v_gla", [P, NT, GW]), sp("v_hgrn", [P, NT, GW]), sp("v_swa", [P, NT, P])
                        S.log_decay, S.h_key = sp("log_decay", [P, 3, T]), sp("h_key", [P, 2, T])
                        stage_projection(nc, S, A, i)
                        with ExitStack() as gat:
                            sg = lambda n, s: gat.enter_context(nc.sbuf_tensor(f"{n}_layer{i}", s, F32))
                            S.low, S.gk_pre, S.soft, S.rw_vg = sg("low", [P, T]), sg("gk_pre", [P, T]), sg("soft", [P, 3, T]), sg("rw_vg", [P, 2, T])
                            stage_gates(nc, S, A, i)
                        stage_gated_linear(nc, S, A, i)
                        stage_window(nc, S, A, i)
                    stage_rwkv(nc, S, A, i)
                stage_mix_out(nc, S, A, i)
                if i % 2 == 0:
                    stage_dense(nc, S, A, i)
                    stage_embedding(nc, S, A, i, out)
        S.gates, S.place = sb("gates", [P, NT, N_EXP]), sb("place", [P, NT, N_EXP])
        S.blocks = sb("blocks", [1, 2 * N_EXP], I32)
        stage_route(nc, S, A, 0)
        stage_experts(nc, S, A, DEPTH - 1)
        stage_embedding(nc, S, A, DEPTH - 1, out)


_INS = ['x', 'p', 'w_in', 'w_out', 'gla_gk_up', 'gla_gk_bias', 'gla_norm_w', 'hgrn_lower_bounds', 'hgrn_norm_w',
        'swa_sinks', 'rwkv_mu', 'rwkv_w0', 'rwkv_w_up', 'rwkv_a0', 'rwkv_a_up', 'rwkv_g_up', 'rwkv_k_k', 'rwkv_k_a',
        'rwkv_r_k', 'rwkv_lnx_w', 'rwkv_lnx_b', 'rwkv_vres_down', 'rwkv_vres_mu', 'rwkv_v0', 'rwkv_vres_up',
        'ln1_g', 'ln1_b', 'ln2_g', 'ln2_b', 'ffn_w_gate', 'ffn_w_up', 'ffn_w_down', 'moe_router', 'moe_w_gate',
        'moe_w_up', 'moe_w_down', 'ple_proj', 'ple_gate']


def kernel(**inputs):
    import numpy as np
    import concourse.bacc as bacc
    from concourse.bass_utils import run_bass_kernel_spmd

    nc = bacc.Bacc("TRN2", target_bir_lowering=False, num_devices=1)
    arrays, aps = {}, {}
    for name in _INS:
        a = np.ascontiguousarray(inputs[name])
        arrays[name + "_in"] = a
        aps[name] = nc.dram_tensor(name + "_in", a.shape, mybir.dt.from_np(a.dtype), kind="ExternalInput").ap()
    out = nc.dram_tensor("out_0", (1, T, D), F32, kind="ExternalOutput").ap()
    build_trunk(nc, Inputs(aps), out)
    result = run_bass_kernel_spmd(nc, [arrays], core_ids=[0])
    return result.results[0]["out_0"]
```

```python
import concourse.bass as bass
from concourse import mybir
from contextlib import ExitStack

F32 = mybir.dt.float32
F32R = mybir.dt.float32r
I32 = mybir.dt.int32
U32 = mybir.dt.uint32
ALU = mybir.AluOpType
ACT = mybir.ActivationFunctionType
AX_X = mybir.AxisListType.X

P = 128
D = 1024
T = 512
NT = T // P
KD = D // P
DEPTH = 2
HALF = 512
ALPHA = (2.0 * DEPTH) ** 0.25
GW = 256
HD = 64
GLA_DK = 32
D_FF = 2816
F_TILES = D_FF // P
N_EXP = 8
D_FFE = 3584
LN_EPS, RMS_EPS, GN_EPS = 1e-5, 1e-6, 64e-5
RW_CHUNK = 64
RW_RATE = 0.6065306597126334
RW_MID = -RW_RATE * RW_CHUNK / 2
NC64 = T // RW_CHUNK
LEVELS = [64, 32, 16, 8, 4, 2, 1]
NEG = -1e30

C_GQ, C_GV, C_GG, C_GGK = 0, 256, 512, 768
C_HQ, C_HF, C_HI, C_HG = 784, 1040, 1296, 1552
C_SQ, C_SK = 1808, 2064
C_R, C_K, C_V, C_WD, C_AD, C_GD = 2320, 2576, 2832, 3088, 3104, 3120
L_WD, L_AD, L_VD, L_GD, L_GK = 0, 32, 48, 64, 96
U_W, U_A, U_V, U_G, U_GK, U_END = 0, 256, 512, 768, 1024, 1152

(R_GKB, R_GNW, R_HNW, R_W0, R_A0, R_KK, R_KA, R_RK, R_LW, R_LB, R_V0, R_MU, R_MUS, R_LBD, R_ROWS) = (
    0, 1, 2, 3, 5, 7, 9, 11, 13, 15, 17, 19, 25, 26, 32)


class Inputs(dict):

    def __getattr__(self, name):
        return self[name]


class Buffers:
    pass


class Stage(ExitStack):

    def __init__(self, nc, tag):
        super().__init__()
        self.nc, self.tag, self.sems = nc, tag, []

    def semaphore(self, name):
        self.sems.append(self.nc.alloc_semaphore(self.tag + name))
        return self.sems[-1]

    def __exit__(self, *error):
        done = super().__exit__(*error)
        if error[0] is None:
            self.nc.clear_and_free_semaphores(self.sems)
            self.nc.all_engine_barrier()
        return done


class Steps:

    def __init__(self, eng, own):
        self.eng, self.own, self.count = eng, own, {}

    def __call__(self, ins, sem=None):
        sem = self.own if sem is None else sem
        ins.then_inc(sem, 1)
        self.count[sem.name] = self.count.get(sem.name, 0) + 1
        self.eng.wait_ge(sem, self.count[sem.name])


class Ring:

    def __init__(self, st, nc, name, psum, banks):
        self.full = st.semaphore(name + "_full")
        self.freed = st.semaphore(name + "_freed")
        self.psum, self.banks, self.filled, self.read = psum, banks, 0, 0

    def fill(self, pe):
        k = self.filled
        self.filled += 1
        if k >= len(self.banks):
            pe.wait_ge(self.freed, k - len(self.banks) + 1)
        return self.psum[:, self.banks[k % len(self.banks)], :]

    def take(self, eng):
        k = self.read
        self.read += 1
        eng.wait_ge(self.full, k + 1)
        return self.psum[:, self.banks[k % len(self.banks)], :]


def over(ap, n):
    return ap.unsqueeze(1).broadcast_to([ap.shape[0], n, ap.shape[1]])


def blocks4(ap):
    return ap.rearrange("p (c t) -> p c t", c=4)


class SplitWeights:

    def __init__(self, st, nc, tag, raws, parts, through):
        self.nc, self.raws, self.parts, self.through = nc, raws, parts, through
        tensor = lambda n, m, dt: st.enter_context(nc.sbuf_tensor(tag + n, [P, m, D], dt))
        self.raw, self.hi, self.lo = tensor("raw", raws, F32), tensor("hi", parts, F32R), tensor("lo", parts, F32R)
        self.landed = [st.semaphore(f"raw{n}_landed") for n in range(raws)]
        self.high, self.low = st.semaphore("high_parts"), st.semaphore("low_parts")

    def load(self, eng, n, src):
        if n >= self.raws:
            eng.wait_ge(self.low, n - self.raws + 1)
        to = self.raw[:, n % self.raws, :]
        if len(src.shape) == 3:
            to = to.rearrange("p (k n) -> p k n", k=src.shape[1])
        eng.dma_start(to, src).then_inc(self.landed[n % self.raws], 16)

    def make_high(self, act, n):
        if n >= self.parts:
            act.wait_ge(*self.through(n - self.parts))
        act.wait_ge(self.landed[n % self.raws], 16 * (n // self.raws + 1))
        self.nc.scalar.activation(self.hi[:, n % self.parts, :], self.raw[:, n % self.raws, :], ACT.Copy).then_inc(self.high, 1)

    def make_low(self, dve, n):
        dve.wait_ge(self.high, n + 1)
        m = n % self.parts
        self.nc.vector.tensor_tensor(self.lo[:, m, :], self.raw[:, n % self.raws, :], self.hi[:, m, :].bitcast(F32), ALU.subtract).then_inc(self.low, 1)

    def take(self, pe, n):
        pe.wait_ge(self.low, n + 1)
        return self.hi[:, n % self.parts, :], self.lo[:, n % self.parts, :]


class SplitTiles:

    def __init__(self, st, nc, tag, name, slots):
        self.nc, self.slots = nc, slots
        self.hi, self.lo = (st.enter_context(nc.sbuf_tensor(tag + name + part, [P, slots, T], F32R)) for part in ("_hi", "_lo"))
        self.high, self.low = st.semaphore(name + "_high"), st.semaphore(name + "_low")

    def make_high(self, act, n, src):
        self.nc.scalar.activation(self.hi[:, n % self.slots, :], src, ACT.Copy).then_inc(self.high, 1)

    def make_low(self, dve, n, src):
        dve.wait_ge(self.high, n + 1)
        m = n % self.slots
        self.nc.vector.tensor_tensor(self.lo[:, m, :], src, self.hi[:, m, :].bitcast(F32), ALU.subtract).then_inc(self.low, 1)


def three_passes(nc, o, left, right, start, stop, **flags):
    nc.tensor.matmul(o, left[0], right[0], start=start, stop=False, **flags)
    nc.tensor.matmul(o, left[1], right[0], start=False, stop=False, **flags)
    return nc.tensor.matmul(o, left[0], right[1], start=False, stop=stop, **flags)


W_SLOTS = 2
K_AHEAD = 4
W_IN_ORDER = (C_R, C_K, C_V, C_GQ, C_GV, C_GG, C_HQ, C_HF, C_HI, C_HG, C_SQ, C_SK)


def slot_of(S, n):
    return S.ahead[:, n % W_SLOTS, :].rearrange("p (k n) -> p k n", k=KD)


def load_w_in(S, A, eng, i, n):
    w, c0, to, landed = A.w_in[i].rearrange("(k p) n -> p k n", p=P), W_IN_ORDER[n], slot_of(S, n), S.w_landed[n % W_SLOTS]
    if c0 == C_SQ:
        for c, h in enumerate((0, 2, 1, 3)):
            eng.dma_start(to[:, :, c * HD:(c + 1) * HD], w[:, :, c0 + h * HD:c0 + (h + 1) * HD]).then_inc(landed, 16)
    else:
        eng.dma_start(to, w[:, :, c0:c0 + GW]).then_inc(landed, 16)


def load_first_w_in(S, A, eng, i):
    for n in range(W_SLOTS):
        load_w_in(S, A, eng, i, n)


def load_w_out(S, A, eng, i, ks):
    for k in ks:
        eng.dma_start(S.wo(k), A.w_out[i, k * P:(k + 1) * P, :]).then_inc(S.wo_in[k], 16)


def stage_constants(nc, S, A):
    S.tag = "constants_"
    with Stage(nc, S.tag) as st:
        sem = lambda n: st.semaphore(n)
        rows = st.enter_context(nc.sbuf_tensor("param_rows", [DEPTH * R_ROWS, P], F32))
        zeros = st.enter_context(nc.sbuf_tensor("zeros", [P, P], F32))
        x_in, params_in, consts = sem("x_in"), sem("params_in"), sem("consts")
        pool_step, dve_step, rows_clear, ident_ready = sem("pool_step"), sem("dve_step"), sem("rows_clear"), sem("ident_ready")
        ring = Ring(st, nc, "setup", S.bank, list(range(8)))
        loads = []
        for i in range(DEPTH):
            r0 = i * R_ROWS

            def row(r, ap, c0=0):
                n, w = ap.shape
                loads.append((rows[r0 + r:r0 + r + n, c0:c0 + w], ap))

            two = lambda ap: ap.rearrange("(a b) -> a b", b=P)
            one = lambda ap: ap.rearrange("(a b) -> a b", a=1)
            row(R_GKB, one(A.gla_gk_bias[i, :]))
            for h in range(2):
                row(R_GNW, one(A.gla_norm_w[i, :]), h * HD)
                row(R_HNW, one(A.hgrn_norm_w[i, :]), h * HD)
            for r, t in ((R_W0, A.rwkv_w0), (R_A0, A.rwkv_a0), (R_KK, A.rwkv_k_k), (R_KA, A.rwkv_k_a),
                         (R_LW, A.rwkv_lnx_w), (R_LB, A.rwkv_lnx_b)):
                row(r, two(t[i, :]))
            row(R_RK, two(A.rwkv_r_k[i].rearrange("h n -> (h n)")))
            row(R_MU, two(A.rwkv_mu[i, 0:3 * GW]))
            row(R_MUS, one(A.rwkv_mu[i, 768:784]), L_WD)
            row(R_MUS, one(A.rwkv_mu[i, 784:800]), L_AD)
            row(R_MUS, one(A.rwkv_mu[i, 800:832]), L_GD)
            for j in range(DEPTH):
                row(R_LBD + 2 * j, two(A.hgrn_lower_bounds[j, :]))
            if i > 0:
                row(R_V0, two(A.rwkv_v0[i - 1, :]))
                row(R_MUS, one(A.rwkv_vres_mu[i - 1, :]), L_VD)

        with nc.Block() as block:
            @block.sync
            def _(sp):
                for t in range(NT):
                    sp.dma_start(S.x[:, t, :], A.x[0, t * P:(t + 1) * P, :]).then_inc(x_in, 16)
                load_first_w_in(S, A, sp, 0)
                sp.wait_ge(rows_clear, 1)
                for dst, src in loads:
                    sp.dma_start(dst, src).then_inc(params_in, 16)
                sp.dma_start(S.sinks[:, :], A.swa_sinks.rearrange("l h -> (l h)").partition_broadcast(P)).then_inc(params_in, 16)
                sp.wait_ge(params_in, 16 * (len(loads) + 1))

            @block.gpsimd
            def _(pool):
                step = Steps(pool, pool_step)
                g = nc.gpsimd

                def select(ap, pattern, base, mult, op=ALU.is_ge, fill=0.0):
                    step(g.affine_select(out=ap, in_=ap, compare_op=op, fill=fill, base=base,
                                         pattern=pattern, channel_multiplier=mult))

                step(g.memset(S.ident[:, :], 0.0))
                step(g.affine_select(out=S.ident[:, :], in_=S.ident[:, :], compare_op=ALU.not_equal, fill=1.0, base=0,
                                     pattern=[[-1, P]], channel_multiplier=1), ident_ready)
                step(g.memset(S.lower[:, :, :], 0.0))
                for l, m in enumerate(LEVELS):
                    second = S.lower[:, l, :].rearrange("p (b h j) -> p b h j", h=2, j=m)[:, :, 1, :]
                    n = P // (2 * m)
                    step(g.memset(second, 1.0))
                    select(second, [[-2 * m, n], [0, m]], 0, 1)
                    select(second, [[2 * m, n], [0, m]], m - 1, -1)
                head = S.head_ones[:, :].rearrange("p (b j) -> p b j", b=2)
                step(g.memset(S.head_ones[:, :], 1.0))
                select(head, [[-HD, 2], [0, HD]], 0, 1)
                select(head, [[HD, 2], [0, HD]], HD - 1, -1)
                step(g.tensor_scalar(S.head_mean[:, :], S.head_ones[:, :], 1.0 / HD, None, ALU.mult))
                for dst, op in ((S.chunk_before, ALU.is_gt), (S.chunk_upto, ALU.is_ge)):
                    step(g.tensor_copy(dst[:, :], S.head_ones[:, :]))
                    select(dst[:, :], [[1, P]], 0, -1, op)
                step(g.memset(S.gla_heads[:, :], 1.0))
                heads4 = S.gla_heads[:, :].rearrange("p (h v) -> p h v", h=4)
                select(heads4, [[-GLA_DK, 4], [0, HD]], 0, 1)
                select(heads4, [[GLA_DK, 4], [0, HD]], GLA_DK - 1, -1)
                step(g.memset(zeros[:, :], 0.0))
                step(g.memset(S.own_bias[:, :], 0.0))
                select(S.own_bias[:, :], [[-1, P]], 0, 1, ALU.is_ge, NEG)
                step(g.memset(S.prev_bias[:, :], 0.0))
                select(S.prev_bias[:, :], [[1, P]], 0, -1, ALU.is_gt, NEG)
                step(g.memset(S.ones[:, :], 1.0))
                step(g.memset(S.carry128[:, :], 1.0))
                step(g.memset(S.carry128[:, 0:T:P], 0.0))
                step(g.memset(S.carry64[:, :], 1.0))
                step(g.memset(S.carry64[:, 0:T:RW_CHUNK], 0.0))
                for c, v in enumerate((LN_EPS, RMS_EPS, GN_EPS, -RW_MID, RW_MID, 1.0)):
                    step(g.memset(S.eps[:, c:c + 1], v))
                step(g.memset(S.w_low[:, :, :], 0.0))
                g.memset(S.w_up[:, :], 0.0).then_inc(consts, 1)

            @block.tensor
            def _(pe):
                pe.wait_ge(ident_ready, 1)
                pe.wait_ge(x_in, 16 * NT)
                for t in range(NT):
                    for h in range(2):
                        b = ring.fill(pe)
                        for j in range(4):
                            k = 4 * h + j
                            last = nc.tensor.transpose(b[:, j * P:(j + 1) * P], S.x[:, t, k * P:(k + 1) * P], S.ident[:, :])
                        last.then_inc(ring.full, 1)
                b = ring.fill(pe)
                pe.wait_ge(params_in, 16 * (len(loads) + 1))
                nc.tensor.transpose(b[:, 0:DEPTH * R_ROWS], rows[:, :], S.ident[0:DEPTH * R_ROWS, 0:DEPTH * R_ROWS]).then_inc(ring.full, 1)

            @block.vector
            def _(dve):
                step = Steps(dve, dve_step)
                step(nc.vector.memset(rows[:, :], 0.0), rows_clear)
                for t in range(NT):
                    for h in range(2):
                        b = ring.take(dve)
                        step(nc.vector.tensor_copy(S.xT[:, 4 * h:4 * h + 4, t * P:(t + 1) * P], blocks4(b)), ring.freed)
                b = ring.take(dve)
                step(nc.vector.tensor_copy(S.par[:, :], b[:, 0:DEPTH * R_ROWS]), ring.freed)


def stage_projection(nc, S, A, i):
    S.tag = f"projection{i}_"
    w = A.w_in[i].rearrange("(k p) n -> p k n", p=P)
    LOW_AT = 3
    with Stage(nc, S.tag) as st:
        sem = lambda n: st.semaphore(n)
        ws, landed = [slot_of(S, n) for n in range(W_SLOTS)], S.w_landed
        low_in, up_in, act_step, dve_step = sem("low_in"), sem("up_in"), sem("act_step"), sem("dve_step")
        rings = [Ring(st, nc, "act_bank", S.bank, [0, 1, 2, 3]), Ring(st, nc, "dve_bank", S.bank, [4, 5, 6, 7])]
        z = lambda n: S.z[:, n, :]
        zr = lambda n: S.zr[:, n, 1:T + 1]
        ch = lambda *tiles: ("channels", tiles)
        chunks = [
            (C_R, ch(zr(0), zr(1))), (C_K, ch(zr(2), zr(3))), (C_V, ch(zr(4), zr(5))),
            (C_GQ, ch(z(0), z(1))), (C_GV, ("tokens", S.v_gla, GW)), (C_GG, ch(z(2), z(3))),
            (C_HQ, ch(z(4), z(5))), (C_HF, ch(z(6), z(7))), (C_HI, ("tokens", S.v_hgrn, GW)), (C_HG, ch(z(8), z(9))),
            (C_SQ, ch(z(10), z(11))), (C_SK, ("keys and values", z(12), S.v_swa)),
        ]
        outs, last_bank, part_jobs, landed_at, seen = [], [], [], [], [0] * W_SLOTS
        silu_jobs = set()
        assert tuple(c for c, _ in chunks) == W_IN_ORDER
        for n, (_, what) in enumerate(chunks):
            s = n % W_SLOTS
            if n == LOW_AT:
                part_jobs.append((len(outs), low_in, 16 * (4 + (i > 0)), S.w_low[:, :, :]))
                outs.append(zr(6))
            seen[s] += 16 * (4 if W_IN_ORDER[n] == C_SQ else 1)
            landed_at.append(seen[s])
            for q in range({"channels": 2, "tokens": 0, "keys and values": 1}[what[0]]):
                part_jobs.append((len(outs) + q, landed[s], seen[s], ws[s][:, :, q * P:(q + 1) * P]))
            if W_IN_ORDER[n] in (C_GG, C_HG, C_HQ):
                silu_jobs |= {len(outs), len(outs) + 1}
            if what[0] == "channels":
                outs += list(what[1])
            elif what[0] == "tokens":
                outs += [what[1][:, t:t + 2, :] for t in (0, 2)]
            else:
                outs += [what[1], what[2][:, :, :]]
            last_bank.append(len(outs) - 1)
        part_of = {job[0]: n for n, job in enumerate(part_jobs)}
        PARTS = 2
        xs = SplitTiles(st, nc, S.tag, "x", KD)
        w_hi, w_lo = (st.enter_context(nc.sbuf_tensor(S.tag + n, [P, PARTS, KD, P], F32R)) for n in ("w_hi", "w_lo"))
        high, low_part = sem("high_parts"), sem("low_parts")

        def make_high(act, n):
            _, s, value, src = part_jobs[n]
            if n >= PARTS:
                job = part_jobs[n - PARTS][0]
                act.wait_ge(rings[job % 2].full, job // 2 + 1)
            act.wait_ge(s, value)
            nc.scalar.activation(w_hi[:, n % PARTS, :, :], src, ACT.Copy).then_inc(high, 1)

        def make_low(dve, n):
            dve.wait_ge(high, n + 1)
            nc.vector.tensor_tensor(w_lo[:, n % PARTS, :, :], part_jobs[n][3], w_hi[:, n % PARTS, :, :].bitcast(F32), ALU.subtract).then_inc(low_part, 1)

        low = [(L_WD, C_WD, 16), (L_AD, C_AD, 16), (L_GD, C_GD, 32), (L_GK, C_GGK, 16)]
        ups = [(L_WD, U_W, A.rwkv_w_up[i]), (L_AD, U_A, A.rwkv_a_up[i]), (L_GD, U_G, A.rwkv_g_up[i]), (L_GK, U_GK, A.gla_gk_up[i])]
        if i > 0:
            ups.append((L_VD, U_V, A.rwkv_vres_up[i - 1]))
        with nc.Block() as block:
            @block.sync
            def _(sp):
                for n in range(W_SLOTS, len(chunks)):
                    j = last_bank[n - W_SLOTS]
                    sp.wait_ge(rings[j % 2].full, j // 2 + 1)
                    load_w_in(S, A, sp, i, n)

            @block.gpsimd
            def _(pool):
                nc.gpsimd.memset(S.zr[:, :, 0:1], 0.0)

            @block.tensor
            def _(pe):
                job = 0

                def channels():
                    nonlocal job
                    r, n = rings[job % 2], part_of[job]
                    job += 1
                    b = r.fill(pe)
                    pe.wait_ge(low_part, n + 1)
                    for k in range(KD):
                        if n == 0:
                            pe.wait_ge(xs.low, k + 1)
                        last = three_passes(nc, b, (w_hi[:, n % PARTS, k, :], w_lo[:, n % PARTS, k, :]), (xs.hi[:, k, :], xs.lo[:, k, :]), k == 0, k == KD - 1)
                    last.then_inc(r.full, 1)

                def tokens(weights, n, per_bank):
                    nonlocal job
                    for t0 in range(0, NT, per_bank):
                        r = rings[job % 2]
                        job += 1
                        b = r.fill(pe)
                        for t in range(per_bank):
                            for k in range(KD):
                                last = nc.tensor.matmul(b[:, t * n:(t + 1) * n], S.xT[:, k, (t0 + t) * P:(t0 + t + 1) * P],
                                                        weights[:, k, :], start=(k == 0), stop=(k == KD - 1))
                        last.then_inc(r.full, 1)

                for n, (c0, what) in enumerate(chunks):
                    s = n % W_SLOTS
                    if n == LOW_AT:
                        channels()
                    if what[0] == "channels":
                        channels()
                        channels()
                        continue
                    if what[0] == "keys and values":
                        channels()
                    pe.wait_ge(landed[s], landed_at[n])
                    if what[0] == "tokens":
                        tokens(ws[s][:, :, :], GW, 2)
                    else:
                        tokens(ws[s][:, :, P:GW], P, 4)

            def evacuate(eng, which, op, own, split):
                step = Steps(eng, own)
                for n in range(PARTS):
                    split(eng, n)
                for n, dst in enumerate(outs):
                    if n % 2 == which:
                        b = rings[which].take(eng)
                        b = b if len(dst.shape) == 2 else b.rearrange("p (c t) -> p c t", c=dst.shape[1])
                        step(op(dst, b), rings[which].freed)
                        for m in (n - 1, n):
                            if which == 0 and m in silu_jobs:
                                if m % 2:
                                    eng.wait_ge(rings[1].freed, m // 2 + 1)
                                step(nc.scalar.activation(outs[m], outs[m], ACT.Silu))
                    if n in part_of and part_of[n] + PARTS < len(part_jobs):
                        split(eng, part_of[n] + PARTS)

            @block.scalar
            def _(act):
                for r, c, k in low:
                    act.dma_start(S.w_low[:, :, r:r + k], w[:, :, c:c + k]).then_inc(low_in, 16)
                if i > 0:
                    act.dma_start(S.w_low[:, :, L_VD:L_VD + 8], A.rwkv_vres_down[i - 1].rearrange("(k p) n -> p k n", p=P)).then_inc(low_in, 16)
                for r, c, src in ups:
                    k, m = src.shape
                    act.dma_start(S.w_up[r:r + k, c:c + m], src).then_inc(up_in, 16)
                for k in range(KD):
                    xs.make_high(act, k, S.xT[:, k, :])
                evacuate(act, 0, lambda o, b: nc.scalar.activation(o, b, ACT.Copy), act_step, make_high)
                act.wait_ge(up_in, 16 * len(ups))

            @block.vector
            def _(dve):
                for k in range(KD):
                    xs.make_low(dve, k, S.xT[:, k, :])
                evacuate(dve, 1, lambda o, b: nc.vector.tensor_copy(o, b), dve_step, make_low)


def stage_gates(nc, S, A, i):
    S.tag = f"gates{i}_"
    with Stage(nc, S.tag) as st:
        sem = lambda n: st.semaphore(n)
        tmp = st.enter_context(nc.sbuf_tensor(S.tag + "gate_tmp", [P, 3, T], F32))
        low_shifted, low_ready, shifted, act_step, dve_step = (
            sem("low_shifted"), sem("low_ready"), sem("shifted"), sem("act_step"), sem("dve_step"))
        lb_ready, soft_ready, mins_ready, hk_ready, lb2, log_a = (
            sem("lb_ready"), sem("soft_ready"), sem("mins_ready"), sem("hk_ready"), sem("lb2"), sem("log_a"))
        diff_ready, soft2_ready = sem("diff_ready"), sem("soft2_ready")
        ring = Ring(st, nc, "act_bank", S.bank, list(range(8)))
        par = lambda r: S.par[:, i * R_ROWS + r:i * R_ROWS + r + 1]
        blocks = [(U_W, 2), (U_A, 2), (U_G, 2)] + ([(U_V, 2)] if i else [])
        LD, SOFT = S.log_decay, S.soft
        with nc.Block() as block:
            @block.tensor
            def _(pe):
                pe.wait_ge(low_ready, 2)
                for u0, n in [(U_GK, 1)] + blocks:
                    for j in range(n):
                        b = ring.fill(pe)
                        nc.tensor.matmul(b, S.w_up[:, u0 + j * P:u0 + (j + 1) * P], S.low[:, :], start=True, stop=True).then_inc(ring.full, 1)

            @block.scalar
            def _(act):
                step = Steps(act, act_step)
                f = nc.scalar.activation
                for j in range(2):
                    step(f(S.h_key[:, j, :], S.z[:, 6 + j, :], ACT.Sigmoid, scale=-1.0), hk_ready)
                act.wait_ge(low_shifted, 1)
                step(f(S.low[L_WD:L_WD + 16, :], S.low[L_WD:L_WD + 16, :], ACT.Tanh), low_ready)
                step(f(S.low[L_GD:L_GD + 32, :], S.low[L_GD:L_GD + 32, :], ACT.Sigmoid), low_ready)
                b = ring.take(act)
                step(f(S.gk_pre[:, :], b, ACT.Identity, bias=par(R_GKB)), ring.freed)
                dest = {U_W: (S.rw_w, R_W0), U_A: (S.rw_a, R_A0), U_G: (S.rw_g, None), U_V: (S.rw_vg, R_V0)}
                for u0, n in blocks:
                    for j in range(n):
                        b = ring.take(act)
                        to, r = dest[u0]
                        if r is None:
                            step(f(to[:, j, :], b, ACT.Copy), ring.freed)
                        else:
                            step(f(to[:, j, :], b, ACT.Sigmoid, bias=par(r + j)), ring.freed)
                src = [S.gk_pre[:, :], S.z[:, 6, :], S.z[:, 7, :]]
                for n in range(3):
                    step(f(SOFT[:, n, :], src[n], ACT.Abs))
                for n in range(3):
                    step(f(SOFT[:, n, :], SOFT[:, n, :], ACT.Exp, scale=-1.0))
                if i:
                    act.wait_ge(lb_ready, 2)
                    step(f(S.lb[:, 4:8], S.lb[:, 0:4], ACT.Abs))
                    step(f(S.lb[:, 4:8], S.lb[:, 4:8], ACT.Exp, scale=-1.0))
                for n in range(3):
                    step(f(SOFT[:, n, :], SOFT[:, n, :], ACT.Ln, bias=S.eps[:, 5:6]), soft_ready)
                if i:
                    step(f(S.lb[:, 4:8], S.lb[:, 4:8], ACT.Ln, bias=S.eps[:, 5:6]), lb2)
                    act.wait_ge(log_a, 1)
                    step(f(S.lb[:, 8:10], S.lb[:, 6:8], ACT.Exp), lb2)
                    for j in range(2):
                        act.wait_ge(diff_ready, j + 1)
                        step(f(tmp[:, j, :], tmp[:, j, :], ACT.Abs))
                    for j in range(2):
                        step(f(tmp[:, j, :], tmp[:, j, :], ACT.Exp, scale=-1.0))
                    for j in range(2):
                        step(f(tmp[:, j, :], tmp[:, j, :], ACT.Ln, bias=S.eps[:, 5:6]), soft2_ready)

            @block.vector
            def _(dve):
                step = Steps(dve, dve_step)
                v = nc.vector

                def shift(n, mu, out, s=None):
                    step(v.tensor_tensor(tmp[:, 2, :], S.zr[:, n, 0:T], S.zr[:, n, 1:T + 1], ALU.subtract))
                    step(v.scalar_tensor_tensor(out, tmp[:, 2, :], mu, S.zr[:, n, 1:T + 1], ALU.mult, ALU.add), s)

                shift(6, par(R_MUS), S.low[:, :], low_shifted)
                if i:
                    step(v.tensor_tensor(S.lb[:, 0:2], S.par[:, i * R_ROWS + R_LBD:i * R_ROWS + R_LBD + 2],
                                         S.par[:, i * R_ROWS + R_LBD + 2:i * R_ROWS + R_LBD + 4], ALU.subtract), lb_ready)
                    step(v.tensor_scalar(S.lb[:, 2:4], S.lb[:, 0:2], -1.0, None, ALU.mult), lb_ready)
                for j in range(2):
                    shift(j, par(R_MU + j), S.r[:, j, :])
                    shift(2 + j, par(R_MU + 2 + j), S.k[:, j, :])
                    shift(4 + j, par(R_MU + 4 + j), S.v_first[:, j, :] if i == 0 else S.v[:, j, :])
                if i:
                    for j in range(2):
                        dve.wait_ge(ring.freed, ring.filled)
                        step(v.tensor_tensor(tmp[:, 2, :], S.v_first[:, j, :], S.v[:, j, :], ALU.subtract))
                        step(v.tensor_tensor(tmp[:, 2, :], tmp[:, 2, :], S.rw_vg[:, j, :], ALU.mult))
                        step(v.tensor_tensor(S.v[:, j, :], S.v[:, j, :], tmp[:, 2, :], ALU.add))
                src = [S.gk_pre[:, :], S.z[:, 6, :], S.z[:, 7, :]]
                for n in range(3):
                    dve.wait_ge(soft_ready, n + 1)
                    step(v.scalar_tensor_tensor(LD[:, n, :], src[n], 0.0, SOFT[:, n, :], ALU.min, ALU.subtract))
                if i:
                    dve.wait_ge(lb2, 1)
                    step(v.tensor_scalar(S.lb[:, 0:4], S.lb[:, 0:4], 0.0, -1.0, ALU.max, ALU.mult))
                    step(v.tensor_tensor(S.lb[:, 4:8], S.lb[:, 0:4], S.lb[:, 4:8], ALU.subtract), log_a)
                    for j in range(2):
                        step(v.tensor_scalar(LD[:, 1 + j, :], LD[:, 1 + j, :], S.lb[:, 6 + j:7 + j], None, ALU.add))
                        step(v.tensor_scalar(tmp[:, j, :], LD[:, 1 + j, :], S.lb[:, 4 + j:5 + j], None, ALU.subtract), diff_ready)
                    for j in range(2):
                        dve.wait_ge(soft2_ready, j + 1)
                        step(v.scalar_tensor_tensor(LD[:, 1 + j, :], LD[:, 1 + j, :], S.lb[:, 4 + j:5 + j], tmp[:, j, :], ALU.max, ALU.add))
                    dve.wait_ge(lb2, 2)
                    dve.wait_ge(hk_ready, 2)
                    for j in range(2):
                        step(v.tensor_scalar(S.h_key[:, j, :], S.h_key[:, j, :], S.lb[:, 8 + j:9 + j], None, ALU.mult))


def rms_gate(nc, S, step, ring, o, sq, gate, weight, to):
    step(nc.vector.reciprocal(sq, sq))
    step(nc.vector.tensor_tensor(o, o, sq, ALU.mult))
    step(nc.vector.scalar_tensor_tensor(to, o, weight, gate, ALU.mult, ALU.mult))


def stage_gated_linear(nc, S, A, i):
    S.tag = f"gated_linear{i}_"
    par = lambda r: S.par[:, i * R_ROWS + r:i * R_ROWS + r + 1]
    tiles = [
        (1.0 / 16.0, S.z[:, 0, :], S.z[:, 1, :], GLA_DK, S.v_gla, 0, GW, S.gla_heads, [(2, 0), (3, 1)], R_GNW),
        (1.0, S.z[:, 4, :], S.h_key[:, 0, :], HD, S.v_hgrn, 0, P, S.head_ones, [(8, 2)], R_HNW),
        (1.0, S.z[:, 5, :], S.h_key[:, 1, :], HD, S.v_hgrn, P, P, S.head_ones, [(9, 3)], R_HNW),
    ]
    with Stage(nc, S.tag) as st:
        sem = lambda n: st.semaphore(n)
        sb = lambda n, *s: st.enter_context(nc.sbuf_tensor(S.tag + n, list(s), F32))
        cum, scaled = sb("cum", P, T), sb("scaled", P, 4, T)
        q_in, k_out, k_out_tok = sb("q_in", P, T), sb("k_out", P, T), sb("k_out_tok", P, NT, P)
        decay = sb("decay", P, T)
        scores = sb("scores", P, 4, T)
        state, update = sb("state", P, NT, GW), sb("update", P, NT, GW)
        o, sq = sb("o", P, 2, T), sb("sq", P, 2, T)
        act_step, dve_step = sem("act_step"), sem("dve_step")
        dist, exped, ready, cum_ready, cum_exped, qk_ready = (
            sem("dist"), sem("exped"), sem("scaled_ready"), sem("cum_ready"), sem("cum_exped"), sem("qk_ready"))
        tok_ready, states, scored, squared, q_scaled, o_used = sem("tok_ready"), sem("states"), sem("scored"), sem("squared"), sem("q_scaled"), sem("o_used")
        root, sq_used = sem("root"), sem("sq_used")
        to_dve, to_act = Ring(st, nc, "dve_bank", S.bank, [0, 1, 2, 3]), Ring(st, nc, "act_bank", S.bank, [4, 5, 6, 7])
        NL = len(LEVELS)
        with nc.Block() as block:
            @block.tensor
            def _(pe):
                heads_before, outs_before = 0, 0
                for n, (s, q, k, dk, val, v0, vw, mask, outs, nw) in enumerate(tiles):
                    heads = P // dk
                    if n == 0:
                        pe.wait_ge(q_scaled, 1)
                    for h in range(heads):
                        b, r = to_dve.fill(pe), slice(h * dk, (h + 1) * dk)
                        for c in range(NT):
                            cs = slice(c * P, (c + 1) * P)
                            last = nc.tensor.matmul(b[:, cs], k[r, cs], q[r, cs], start=True, stop=True, tile_position=(h * dk, 0))
                        last.then_inc(to_dve.full, 1)
                    for l in range(NL):
                        pe.wait_ge(ready, n * NL + l + 1)
                        x = scaled[:, l % 4, :]
                        for h in range(heads):
                            b, r = to_dve.fill(pe), slice(h * dk, (h + 1) * dk)
                            for c in range(NT):
                                cs = slice(c * P, (c + 1) * P)
                                last = nc.tensor.matmul(b[:, cs], x[r, cs], x[r, cs], start=True, stop=True, tile_position=(h * dk, 0))
                            last.then_inc(to_dve.full, 1)
                    pe.wait_ge(qk_ready, n + 1)
                    b = to_act.fill(pe)
                    for c in range(NT):
                        last = nc.tensor.transpose(b[:, c * P:(c + 1) * P], k_out[:, c * P:(c + 1) * P], S.ident[:, :])
                    last.then_inc(to_act.full, 1)
                    pe.wait_ge(tok_ready, n + 1)
                    per = HALF // vw
                    for c0 in range(0, NT, per):
                        b = to_dve.fill(pe)
                        for c in range(per):
                            last = nc.tensor.matmul(b[:, c * vw:(c + 1) * vw], k_out_tok[:, c0 + c, :], val[:, c0 + c, v0:v0 + vw], start=True, stop=True)
                        last.then_inc(to_dve.full, 1)
                    pe.wait_ge(scored, n + 1)
                    pe.wait_ge(states, n + 1)
                    for j, _ in enumerate(outs):
                        b = to_act.fill(pe)
                        for c in range(NT):
                            cs = slice(c * P, (c + 1) * P)
                            if c:
                                nc.tensor.matmul(b[:, cs], state[:, c, j * P:(j + 1) * P], q_in[:, cs], start=True, stop=False, skip_group_check=True)
                            for hh in range(2):
                                last = nc.tensor.matmul(b[hh * HD:(hh + 1) * HD, cs], val[:, c, v0 + j * P + hh * HD:v0 + j * P + (hh + 1) * HD],
                                                        scores[:, 2 * j + hh, cs], start=(c == 0), stop=True, tile_position=(0, hh * HD), skip_group_check=True)
                        last.then_inc(to_act.full, 1)
                    for j, _ in enumerate(outs):
                        outs_before += 1
                        pe.wait_ge(squared, outs_before)
                        b = to_act.fill(pe)
                        nc.tensor.matmul(b, S.head_mean[:, :], sq[:, j, :], start=True, stop=True).then_inc(to_act.full, 1)

            @block.scalar
            def _(act):
                step = Steps(act, act_step)
                f = nc.scalar.activation
                outs_before = 0
                for n, (s, q, k, dk, val, v0, vw, mask, outs, nw) in enumerate(tiles):
                    act.wait_ge(cum_ready, 2 * n + 1)
                    step(f(decay[:, :], cum[:, :], ACT.Exp, scale=s), cum_exped)
                    act.wait_ge(cum_ready, 2 * n + 2)
                    step(f(k_out[:, :], k_out[:, :], ACT.Exp, scale=s), cum_exped)
                    for l in range(NL):
                        act.wait_ge(dist, n * NL + l + 1)
                        x = scaled[:, l % 4, :]
                        step(f(x, x, ACT.Exp, scale=s), exped)
                    b = to_act.take(act)
                    step(f(k_out_tok[:, :, :], blocks4(b), ACT.Copy), to_act.freed)
                    act.sem_inc(tok_ready, 1)
                    if outs_before:
                        act.wait_ge(o_used, outs_before)
                    for j, _ in enumerate(outs):
                        b = to_act.take(act)
                        step(f(o[:, j, :], b, ACT.Copy), to_act.freed)
                        step(f(sq[:, j, :], o[:, j, :], ACT.Square), squared)
                    for j, _ in enumerate(outs):
                        b = to_act.take(act)
                        step(f(sq[:, j, :], b, ACT.Sqrt, bias=S.eps[:, 1:2]), to_act.freed)
                        act.sem_inc(root, 1)
                    outs_before += len(outs)

            @block.vector
            def _(dve):
                step = Steps(dve, dve_step)
                v = nc.vector
                outs_before = 0
                step(v.tensor_scalar(S.z[:, 0, :], S.z[:, 0, :], GLA_DK ** -0.5, None, ALU.mult), q_scaled)
                for n, (s, q, k, dk, val, v0, vw, mask, outs, nw) in enumerate(tiles):
                    heads = P // dk
                    halves = lambda ap, l: ap.rearrange("p (b h j) -> p b h j", h=2, j=LEVELS[l])

                    def distance(l):
                        m, c, x = LEVELS[l], halves(cum[:, :], l), halves(scaled[:, l % 4, :], l)
                        edge = c[:, :, 0, m - 1:m].broadcast_to([P, T // (2 * m), m])
                        step(v.tensor_tensor(x[:, :, 0, :], edge, c[:, :, 0, :], ALU.subtract))
                        step(v.tensor_tensor(x[:, :, 1, :], c[:, :, 1, :], edge, ALU.subtract), dist)

                    def times(l):
                        dve.wait_ge(exped, n * NL + l + 1)
                        x, kk, qq = halves(scaled[:, l % 4, :], l), halves(k, l), halves(q, l)
                        step(v.tensor_tensor(x[:, :, 0, :], x[:, :, 0, :], kk[:, :, 0, :], ALU.mult))
                        step(v.tensor_tensor(x[:, :, 1, :], x[:, :, 1, :], qq[:, :, 1, :], ALU.mult), ready)

                    def place(l):
                        for h in range(heads):
                            b = to_dve.take(dve)
                            step(v.copy_predicated(blocks4(scores[:, h, :]), over(S.lower[:, l, :].bitcast(U32), 4), blocks4(b)), to_dve.freed)

                    step(v.tensor_tensor_scan(cum[:, :], S.carry128[:, :], S.log_decay[:, n, :], 0.0, ALU.mult, ALU.add), cum_ready)
                    ends = blocks4(cum[:, :])
                    step(v.tensor_tensor(blocks4(k_out[:, :]), ends[:, :, P - 1:P].broadcast_to([P, 4, P]), ends, ALU.subtract), cum_ready)
                    distance(0)
                    distance(1)
                    for h in range(heads):
                        b = to_dve.take(dve)
                        step(v.tensor_tensor(blocks4(scores[:, h, :]), blocks4(b), over(S.ident[:, :], 4), ALU.mult), to_dve.freed)
                    dve.wait_ge(cum_exped, 2 * n + 2)
                    step(v.tensor_tensor(q_in[:, :], q, decay[:, :], ALU.mult))
                    step(v.tensor_tensor(k_out[:, :], k, k_out[:, :], ALU.mult), qk_ready)
                    for l in range(NL):
                        times(l)
                        if l + 2 < NL:
                            distance(l + 2)
                        if l:
                            place(l - 1)
                    place(NL - 1)
                    dve.sem_inc(scored, 1)
                    per = HALF // vw
                    for c0 in range(0, NT, per):
                        b = to_dve.take(dve)
                        step(v.tensor_tensor(update[:, c0:c0 + per, 0:vw], b.rearrange("p (c w) -> p c w", w=vw), over(mask[:, :], per), ALU.mult), to_dve.freed)
                    step(v.tensor_copy(state[:, 1, 0:vw], update[:, 0, 0:vw]))
                    for c in range(1, NT - 1):
                        step(v.scalar_tensor_tensor(state[:, c + 1, 0:vw], state[:, c, 0:vw], decay[:, (c + 1) * P - 1:(c + 1) * P],
                                                    update[:, c, 0:vw], ALU.mult, ALU.add))
                    dve.sem_inc(states, 1)
                    for j, (g, m) in enumerate(outs):
                        outs_before += 1
                        dve.wait_ge(root, outs_before)
                        rms_gate(nc, S, step, to_act, o[:, j, :], sq[:, j, :], S.z[:, g, :], par(nw), S.mixT[:, m, :])
                        dve.sem_inc(o_used, 1)


def stage_window(nc, S, A, i):
    S.tag = f"window{i}_"
    with Stage(nc, S.tag) as st:
        sem = lambda n: st.semaphore(n)
        sb = lambda n, *s: st.enter_context(nc.sbuf_tensor(S.tag + n, list(s), F32))
        s, pT = sb("s", P, 2, 4, 2 * P), sb("pT", P, 2, 4, 2, P)
        peak, neg, total, sink, inv = sb("peak", P, 4), sb("neg", P, 2, 4), sb("total", P, 2, 4), sb("sink", P, 2, 4), sb("inv", P, 4)
        act_step, dve_step = sem("act_step"), sem("dve_step")
        masked, exped, normed, turned = sem("masked"), sem("exped"), sem("normed"), sem("turned")
        to_dve, to_act = Ring(st, nc, "dve_bank", S.bank, [0, 1, 2, 3]), Ring(st, nc, "act_bank", S.bank, [4, 5])
        out_full = sem("out_full")
        SC = HD ** -0.5
        with nc.Block() as block:
            @block.tensor
            def _(pe):
                def scores(n):
                    for pair in range(2):
                        b, r = to_dve.fill(pe), slice(pair * HD, (pair + 1) * HD)
                        for g in range(2):
                            k0 = max(n - 1, 0) * P
                            w = (n + 1) * P - k0
                            last = nc.tensor.matmul(b[:, g * 2 * P:g * 2 * P + w], S.z[r, 10 + g, n * P:(n + 1) * P], S.z[r, 12, k0:k0 + w],
                                                    start=True, stop=True, tile_position=(pair * HD, 0))
                        last.then_inc(to_dve.full, 1)

                def values(n):
                    w = 1 if n == 0 else 2
                    pe.wait_ge(normed, n + 1)
                    for pair in range(2):
                        b = to_act.fill(pe)
                        for g in range(2):
                            for k in range(w):
                                at = (2 * g + k) * P
                                last = nc.tensor.transpose(b[:, at:at + P], s[:, n % 2, 2 * pair + g, k * P:(k + 1) * P], S.ident[:, :])
                        last.then_inc(to_act.full, 1)
                    pe.wait_ge(turned, 2 * n + 2)
                    for pair in range(2):
                        for g in range(2):
                            for k in range(w):
                                c = n if n == 0 else n - 1 + k
                                last = nc.tensor.matmul(S.bank[g * HD:(g + 1) * HD, 6 + pair, n * P:(n + 1) * P], S.v_swa[:, c, pair * HD:(pair + 1) * HD],
                                                        pT[:, n % 2, 2 * pair + g, k, :], start=(k == 0), stop=(k == w - 1),
                                                        tile_position=(0, g * HD), skip_group_check=True)
                    last.then_inc(out_full, 1)

                scores(0)
                for n in range(NT):
                    if n + 1 < NT:
                        scores(n + 1)
                    values(n)

            @block.scalar
            def _(act):
                step = Steps(act, act_step)
                f = nc.scalar.activation
                for n in range(NT):
                    w = P if n == 0 else 2 * P
                    e = n % 2
                    act.wait_ge(masked, n + 1)
                    for h in range(4):
                        step(f(s[:, e, h, 0:w], s[:, e, h, 0:w], ACT.Exp, bias=neg[:, e, h:h + 1], accum_out=total[:, e, h:h + 1]))
                        step(f(sink[:, e, h:h + 1], S.sinks[:, 4 * i + h:4 * i + h + 1], ACT.Exp, bias=neg[:, e, h:h + 1]))
                    act.sem_inc(exped, 1)
                    if n >= 2:
                        act.wait_ge(out_full, n - 1)
                    for pair in range(2):
                        b = to_act.take(act).rearrange("p (g k t) -> p g k t", g=2, k=2)
                        k = w // P
                        step(f(pT[:, e, 2 * pair:2 * pair + 2, 0:k, :], b[:, :, 0:k, :], ACT.Copy), to_act.freed)
                        act.sem_inc(turned, 1)
                act.wait_ge(out_full, NT)
                for pair in range(2):
                    step(f(S.mixT[:, 4 + pair, :], S.bank[:, 6 + pair, :], ACT.Copy))

            @block.vector
            def _(dve):
                step = Steps(dve, dve_step)
                v = nc.vector

                def mask(n):
                    e, w = n % 2, P if n == 0 else 2 * P
                    for pair in range(2):
                        b = to_dve.take(dve).rearrange("p (g k) -> p g k", g=2)
                        to = s[:, e, 2 * pair:2 * pair + 2, :]
                        if n:
                            step(v.scalar_tensor_tensor(to[:, :, 0:P], b[:, :, 0:P], SC, over(S.prev_bias[:, :], 2), ALU.mult, ALU.add))
                        step(v.scalar_tensor_tensor(to[:, :, w - P:w], b[:, :, w - P:w], SC, over(S.own_bias[:, :], 2), ALU.mult, ALU.add), to_dve.freed)
                    step(v.tensor_reduce(peak[:, :], s[:, e, :, 0:w], AX_X, ALU.max))
                    step(v.tensor_tensor(peak[:, :], peak[:, :], S.sinks[:, 4 * i:4 * i + 4], ALU.max))
                    step(v.tensor_scalar(neg[:, e, :], peak[:, :], -1.0, None, ALU.mult), masked)

                mask(0)
                for n in range(NT):
                    e, w = n % 2, P if n == 0 else 2 * P
                    if n + 1 < NT:
                        if n >= 1:
                            dve.wait_ge(turned, 2 * n)
                        mask(n + 1)
                    dve.wait_ge(exped, n + 1)
                    step(v.tensor_tensor(inv[:, :], total[:, e, :], sink[:, e, :], ALU.add))
                    step(v.reciprocal(inv[:, :], inv[:, :]))
                    step(v.tensor_tensor(s[:, e, :, 0:w], s[:, e, :, 0:w], inv[:, :].unsqueeze(2).broadcast_to([P, 4, w]), ALU.mult), normed)


def stage_rwkv(nc, S, A, i):
    S.tag = f"rwkv{i}_"
    par = lambda r: S.par[:, i * R_ROWS + r:i * R_ROWS + r + 1]
    HEADS = 4
    SIZES = [2, 4, 8, 16, 32]
    with Stage(nc, S.tag) as st:
        sem = lambda n: st.semaphore(n)
        sb = lambda n, *s: st.enter_context(nc.sbuf_tensor(S.tag + n, list(s), F32))
        cum, e_at, e_before, e_back = sb("cum", P, 2, T), sb("e_at", P, 2, T), sb("e_before", P, 2, T), sb("e_back", P, 2, T)
        kk, sq, bonus = sb("kk", P, 2, T), sb("sq", P, 2, T), sb("bonus", P, 2, T)
        rt, at, bt, kt = e_at, e_before, e_back, sb("kt", P, 2, T)
        end = sb("end", P, 2, NC64)
        b_tok, k_tok, v_tok = sb("b_tok", P, 2, NT, P), sb("k_tok", P, 2, NT, P), sb("v_tok", P, 2, NT, P)
        rhs = sb("rhs", P, HEADS, NT, P)
        ab, ak = (S.ahead[:, n, :].rearrange("p (h t) -> p h t", h=HEADS) for n in range(2))
        rb, rk = sb("rb", P, HEADS, T), sb("rk", P, HEADS, T)
        inv, invT, part, w1 = sb("inv", P, HEADS, T), sb("invT", P, HEADS, T), sb("part", P, HEADS, T), sb("w1", P, HEADS, T)
        eye64 = sb("eye64", P, HD)
        oz = inv[:, :, :].rearrange("p h (c n) -> p h c n", n=P)
        split = lambda buf, n: buf[:, 2 * n:2 * n + 2, :].rearrange("p j (c n) -> p j c n", n=HD)
        pass_on, take_in, state = split(part, 0), split(part, 1), split(w1, 0)
        rr = kk
        y, ysq = cum, sq
        act_step, dve_step = sem("act_step"), sem("dve_step")
        k_sq, cum_ready, roots, e_ready, prods, bonus_in = sem("k_sq"), sem("cum_ready"), sem("roots"), sem("e_ready"), sem("prods"), sem("bonus_in")
        turned, masked, inv_ready, parts, w1_ready, inv_at, invT_at, rhs_ready, oz_ready = (
            sem("turned"), sem("masked"), sem("inv_ready"), sem("parts"), sem("w1_ready"), sem("inv_at"), sem("invT_at"), sem("rhs_ready"), sem("oz_ready"))
        ops_ready, state_at, rr_ready, y_ready, centred, ysq_ready = sem("ops_ready"), sem("state_at"), sem("rr_ready"), sem("y_ready"), sem("centred"), sem("ysq_ready")
        to_dve, to_act = Ring(st, nc, "dve_bank", S.bank, [0, 1, 2]), Ring(st, nc, "act_bank", S.bank, [3, 4, 5])
        chain = Ring(st, nc, "chain_bank", S.bank, [6, 7])
        rows = lambda h: slice((h % 2) * HD, (h % 2 + 1) * HD)
        val = S.v_first if i == 0 else S.v
        with nc.Block() as block:
            @block.sync
            def _(sp):
                sp.wait_ge(rhs_ready, HEADS)
                load_w_out(S, A, sp, i, range(K_AHEAD))

            @block.tensor
            def _(pe):
                mm = nc.tensor.matmul

                def one(ring, lhs, rhs_, n=1):
                    b = ring.fill(pe)
                    mm(b, lhs, rhs_, start=True, stop=True).then_inc(ring.full, 1)

                for j in range(2):
                    pe.wait_ge(k_sq, j + 1)
                    one(to_act, S.head_ones[:, :], sq[:, j, :])
                for j in range(2):
                    pe.wait_ge(prods, 5 * j + 1)
                    one(to_dve, S.head_ones[:, :], S.rw_w[:, j, :])
                for j in range(2):
                    pe.wait_ge(prods, 5 * j + 5)
                    for src in (at, bt, kt, val):
                        b = to_act.fill(pe)
                        for c in range(NT):
                            last = nc.tensor.transpose(b[:, c * P:(c + 1) * P], src[:, j, c * P:(c + 1) * P], S.ident[:, :])
                        last.then_inc(to_act.full, 1)
                for h in range(HEADS):
                    r, j = rows(h), h // 2
                    for left, right in ((bt, at), (kt, at), (bt, rt), (kt, rt)):
                        b = to_dve.fill(pe)
                        for c in range(NT):
                            cs = slice(c * P, (c + 1) * P)
                            last = mm(b[:, cs], left[r, j, cs], right[r, j, cs], start=True, stop=True, tile_position=((h % 2) * HD, 0))
                        last.then_inc(to_dve.full, 1)
                for h in range(HEADS):
                    pe.wait_ge(inv_ready, h + 1)
                    b = to_act.fill(pe)
                    for c in range(NT):
                        last = nc.tensor.transpose(b[:, c * P:(c + 1) * P], invT[:, h, c * P:(c + 1) * P], S.ident[:, :])
                    last.then_inc(to_act.full, 1)
                for n, m in enumerate(SIZES):
                    last_size = n == len(SIZES) - 1
                    for h in range(HEADS):
                        pe.wait_ge(parts, n * HEADS + h + 1)
                        if n == 0:
                            pe.wait_ge(inv_at, h + 1)
                        b = to_act.fill(pe)
                        for c in range(NT):
                            cs = slice(c * P, (c + 1) * P)
                            last = mm(b[:, cs], part[:, h, cs], inv[:, h, cs], start=True, stop=True)
                        last.then_inc(to_act.full, 1)
                    for h in range(HEADS):
                        pe.wait_ge(w1_ready, n * HEADS + h + 1)
                        if not last_size:
                            b = to_dve.fill(pe)
                            for c in range(NT):
                                cs = slice(c * P, (c + 1) * P)
                                last = mm(b[:, cs], invT[:, h, cs], w1[:, h, cs], start=True, stop=True)
                            last.then_inc(to_dve.full, 1)
                        b = to_dve.fill(pe)
                        for c in range(NT):
                            cs = slice(c * P, (c + 1) * P)
                            last = mm(b[:, cs], w1[:, h, cs], invT[:, h, cs], start=True, stop=True)
                        last.then_inc(to_dve.full, 1)
                for h in range(HEADS):
                    b = to_act.fill(pe)
                    for c in range(NT):
                        last = mm(b[:, c * HD:(c + 1) * HD], ak[:, h, c * P:(c + 1) * P], v_tok[:, h // 2, c, rows(h)], start=True, stop=True)
                    last.then_inc(to_act.full, 1)
                for h in range(HEADS):
                    pe.wait_ge(rhs_ready, h + 1)
                    pe.wait_ge(invT_at, h + 1)
                    b = to_act.fill(pe)
                    for c in range(NT):
                        cs = slice(c * P, (c + 1) * P)
                        last = mm(b[:, cs], invT[:, h, cs], rhs[:, h, c, :], start=True, stop=True)
                    last.then_inc(to_act.full, 1)
                for j in range(2):
                    pe.wait_ge(oz_ready, 2 * j + 2)
                    for what in range(2):
                        for odd in range(2):
                            b, half = to_dve.fill(pe), slice(odd * HD, (odd + 1) * HD)
                            for c in range(NT):
                                for r in range(2):
                                    h = 2 * j + r
                                    o, pos = b[rows(h), c * HD:(c + 1) * HD], (odd * HD, r * HD)
                                    if what == 0:
                                        last = mm(o, oz[half, h, c, 0:HD], b_tok[half, j, c, rows(h)], start=True, stop=True, tile_position=pos, skip_group_check=True)
                                    else:
                                        mm(o, b_tok[half, j, c, rows(h)], oz[half, h, c, HD:P], start=True, stop=False, tile_position=pos, skip_group_check=True)
                                        last = mm(o, k_tok[half, j, c, rows(h)], v_tok[half, j, c, rows(h)], start=False, stop=True, tile_position=pos, skip_group_check=True)
                            last.then_inc(to_dve.full, 1)
                for j in range(2):
                    b = to_dve.fill(pe)
                    for r in range(2):
                        h = 2 * j + r
                        for c in range(NT):
                            last = mm(b[rows(h), c * P:(c + 1) * P], oz[:, h, c, 0:HD], rb[:, h, c * P:(c + 1) * P], start=True, stop=True,
                                      tile_position=(0, r * HD), skip_group_check=True)
                    last.then_inc(to_dve.full, 1)
                for c in range(1, NC64 - 1):
                    for j in range(2):
                        pe.wait_ge(state_at, 2 * c + j - 1)
                        b = chain.fill(pe)
                        for r in range(2):
                            q = slice(r * HD, (r + 1) * HD)
                            last = mm(b[q, 0:HD], pass_on[q, j, c, :], state[q, j, c, :], start=True, stop=True, tile_position=(r * HD, r * HD), skip_group_check=True)
                        last.then_inc(chain.full, 1)
                pe.wait_ge(state_at, 2 * (NC64 - 1))
                pe.wait_ge(rr_ready, 2)
                for j in range(2):
                    b = to_act.fill(pe)
                    for c in range(NT):
                        cs = slice(c * P, (c + 1) * P)
                        for r in range(2):
                            h = 2 * j + r
                            pos = (0, r * HD)
                            mm(b[rows(h), cs], oz[:, h, c, HD:P], rb[:, h, cs], start=True, stop=False, tile_position=pos, skip_group_check=True)
                            last = mm(b[rows(h), cs], v_tok[:, j, c, rows(h)], rk[:, h, cs], start=False, stop=False, tile_position=pos, skip_group_check=True)
                            for c2 in (2 * c, 2 * c + 1):
                                if c2:
                                    last = mm(b[rows(h), c2 * HD:(c2 + 1) * HD], state[rows(h), j, c2, :], rr[rows(h), j, c2 * HD:(c2 + 1) * HD],
                                              start=False, stop=True, tile_position=(r * HD, r * HD), skip_group_check=True)
                    last.then_inc(to_act.full, 1)
                for j in range(2):
                    pe.wait_ge(y_ready, j + 1)
                    one(to_dve, S.head_mean[:, :], y[:, j, :])
                for j in range(2):
                    pe.wait_ge(ysq_ready, j + 1)
                    one(to_act, S.head_mean[:, :], ysq[:, j, :])

            @block.scalar
            def _(act):
                step = Steps(act, act_step)
                f = nc.scalar.activation
                for j in range(2):
                    b = to_act.take(act)
                    step(f(sq[:, j, :], b, ACT.Sqrt), to_act.freed)
                    act.sem_inc(roots, 1)
                for j in range(2):
                    act.wait_ge(cum_ready, j + 1)
                    step(f(e_at[:, j, :], cum[:, j, :], ACT.Exp, bias=S.eps[:, 3:4]), e_ready)
                    step(f(e_back[:, j, :], cum[:, j, :], ACT.Exp, bias=S.eps[:, 4:5], scale=-1.0), e_ready)
                    step(f(e_before[:, j, :], e_before[:, j, :], ACT.Exp, bias=S.eps[:, 3:4]), e_ready)
                    step(f(end[:, j, :], cum[:, j, RW_CHUNK - 1:T:RW_CHUNK], ACT.Exp), e_ready)
                for j in range(2):
                    b = to_act.take(act).rearrange("p (c r n) -> p r c n", r=2, n=HD)
                    for r in range(2):
                        step(f(rhs[:, 2 * j + r, :, 0:HD], b[:, r, :, :], ACT.Copy), to_act.freed if r else None)
                    for to in (b_tok, k_tok, v_tok):
                        b = to_act.take(act)
                        step(f(to[:, j, :, :], blocks4(b), ACT.Copy), to_act.freed)
                act.sem_inc(turned, 1)
                for h in range(HEADS):
                    b = to_act.take(act)
                    step(f(inv[:, h, :], b, ACT.Copy), to_act.freed)
                    act.sem_inc(inv_at, 1)
                for n in range(len(SIZES)):
                    for h in range(HEADS):
                        b = to_act.take(act)
                        step(f(w1[:, h, :], b, ACT.Copy), to_act.freed)
                        act.sem_inc(w1_ready, 1)
                for h in range(HEADS):
                    b = to_act.take(act)
                    step(f(rhs[:, h, :, HD:P], b[:, 0:NT * HD].rearrange("p (c n) -> p c n", n=HD), ACT.Copy), to_act.freed)
                    act.sem_inc(rhs_ready, 1)
                for h in range(HEADS):
                    b = to_act.take(act)
                    step(f(oz[:, h, :, :], blocks4(b), ACT.Copy), to_act.freed)
                    act.sem_inc(oz_ready, 1)
                for j in range(2):
                    b = to_act.take(act)
                    step(f(y[:, j, :], b, ACT.Copy), to_act.freed)
                    act.sem_inc(y_ready, 1)
                for j in range(2):
                    act.wait_ge(centred, j + 1)
                    step(f(ysq[:, j, :], y[:, j, :], ACT.Square), ysq_ready)
                for j in range(2):
                    b = to_act.take(act)
                    step(f(ysq[:, j, :], b, ACT.Sqrt, bias=S.eps[:, 2:3]), to_act.freed)
                    act.sem_inc(roots, 1)

            @block.vector
            def _(dve):
                step = Steps(dve, dve_step)
                v = nc.vector
                tt, ts, stt = v.tensor_tensor, v.tensor_scalar, v.scalar_tensor_tensor
                step(tt(eye64[:, :], S.ident[:, 0:HD], S.ident[:, HD:P], ALU.add))
                for j in range(2):
                    step(ts(kk[:, j, :], S.k[:, j, :], par(R_KK + j), None, ALU.mult))
                    step(tt(sq[:, j, :], kk[:, j, :], kk[:, j, :], ALU.mult), k_sq)
                for j in range(2):
                    step(ts(S.rw_w[:, j, :], S.rw_w[:, j, :], -RW_RATE, None, ALU.mult))
                    step(v.tensor_tensor_scan(cum[:, j, :], S.carry64[:, :], S.rw_w[:, j, :], 0.0, ALU.mult, ALU.add))
                    step(tt(e_before[:, j, :], cum[:, j, :], S.rw_w[:, j, :], ALU.subtract), cum_ready)
                for j in range(2):
                    step(ts(kt[:, j, :], S.rw_a[:, j, :], 1.0, par(R_KA + j), ALU.subtract, ALU.mult))
                    step(stt(kt[:, j, :], kt[:, j, :], 1.0, S.k[:, j, :], ALU.add, ALU.mult))
                    step(stt(S.rw_w[:, j, :], kt[:, j, :], par(R_RK + j), S.r[:, j, :], ALU.mult, ALU.mult), prods)
                    dve.wait_ge(roots, j + 1)
                    step(ts(sq[:, j, :], sq[:, j, :], 1e-12, None, ALU.max))
                    step(v.reciprocal(sq[:, j, :], sq[:, j, :]))
                    step(tt(kk[:, j, :], kk[:, j, :], sq[:, j, :], ALU.mult))
                    dve.wait_ge(e_ready, 4 * j + 4)
                    step(tt(rt[:, j, :], S.r[:, j, :], e_at[:, j, :], ALU.mult), prods)
                    step(stt(at[:, j, :], kk[:, j, :], -1.0, e_before[:, j, :], ALU.mult, ALU.mult), prods)
                    step(tt(kt[:, j, :], kt[:, j, :], e_back[:, j, :], ALU.mult), prods)
                    step(tt(kk[:, j, :], kk[:, j, :], S.rw_a[:, j, :], ALU.mult))
                    step(tt(bt[:, j, :], kk[:, j, :], e_back[:, j, :], ALU.mult), prods)
                for j in range(2):
                    b = to_dve.take(dve)
                    step(tt(bonus[:, j, :], b, val[:, j, :], ALU.mult), to_dve.freed)
                for h in range(HEADS):
                    for to, mask in ((ab, S.chunk_before), (ak, S.chunk_before), (rb, S.chunk_upto), (rk, S.chunk_upto)):
                        b = to_dve.take(dve)
                        step(tt(blocks4(to[:, h, :]), blocks4(b), over(mask[:, :], 4), ALU.mult), to_dve.freed)
                for h in range(HEADS):
                    step(tt(blocks4(invT[:, h, :]), blocks4(ab[:, h, :]), over(S.lower[:, LEVELS.index(1), :], 4), ALU.mult))
                    step(tt(blocks4(invT[:, h, :]), blocks4(invT[:, h, :]), over(S.ident[:, :], 4), ALU.add), inv_ready)

                def part_of(n, h):
                    step(tt(blocks4(part[:, h, :]), blocks4(ab[:, h, :]), over(S.lower[:, LEVELS.index(SIZES[n]), :], 4), ALU.mult), parts)

                for h in range(HEADS):
                    part_of(0, h)
                for n in range(len(SIZES)):
                    last_size = n == len(SIZES) - 1
                    for h in range(HEADS):
                        if not last_size:
                            b = to_dve.take(dve)
                            step(tt(inv[:, h, :], inv[:, h, :], b, ALU.add), to_dve.freed)
                        b = to_dve.take(dve)
                        step(tt(invT[:, h, :], invT[:, h, :], b, ALU.add), to_dve.freed)
                        if last_size:
                            dve.sem_inc(invT_at, 1)
                        else:
                            part_of(n + 1, h)
                for j in range(2):
                    for odd in range(2):
                        b = to_dve.take(dve)[:, 0:NT * HD].rearrange("p (c n) -> p c n", n=HD)
                        step(tt(pass_on[:, j, odd:NC64:2, :], b, over(eye64[:, :], NT), ALU.add), to_dve.freed)
                    for odd in range(2):
                        b = to_dve.take(dve)[:, 0:NT * HD].rearrange("p (c n) -> p c n", n=HD)
                        step(tt(take_in[:, j, odd:NC64:2, :], b, end[:, j, odd:NC64:2].unsqueeze(2).broadcast_to([P, NT, HD]), ALU.mult), to_dve.freed)
                for j in range(2):
                    b = to_dve.take(dve)
                    step(tt(rr[:, j, :], b, rt[:, j, :], ALU.add), to_dve.freed)
                    dve.sem_inc(rr_ready, 1)
                for j in range(2):
                    step(v.tensor_copy(state[:, j, 1, :], take_in[:, j, 0, :]), state_at)
                for c in range(1, NC64 - 1):
                    for j in range(2):
                        b = chain.take(dve)
                        step(stt(state[:, j, c + 1, :], b[:, 0:HD], end[:, j, c:c + 1], take_in[:, j, c, :], ALU.mult, ALU.add), chain.freed)
                        dve.sem_inc(state_at, 1)
                for j in range(2):
                    b = to_dve.take(dve)
                    step(tt(y[:, j, :], y[:, j, :], b, ALU.subtract), to_dve.freed)
                    dve.sem_inc(centred, 1)
                for j in range(2):
                    dve.wait_ge(roots, 2 + j + 1)
                    step(v.reciprocal(ysq[:, j, :], ysq[:, j, :]))
                    step(tt(y[:, j, :], y[:, j, :], ysq[:, j, :], ALU.mult))
                    step(ts(y[:, j, :], y[:, j, :], par(R_LW + j), par(R_LB + j), ALU.mult, ALU.add))
                    step(tt(y[:, j, :], y[:, j, :], bonus[:, j, :], ALU.add))
                    step(tt(S.mixT[:, 6 + j, :], y[:, j, :], S.rw_g[:, j, :], ALU.mult))


class Norm:

    def __init__(self, st, nc, S, g, b, ring, normed, transposed):
        self.nc, self.S, self.g, self.b, self.ring, self.normed = nc, S, g, b, ring, normed
        sb = lambda n, *s: st.enter_context(nc.sbuf_tensor(S.tag + n, list(s), F32))
        self.stats, self.mv = sb("stats", P, NT, 2, 6), sb("mv", P, NT, 2)
        self.transposed = transposed
        self.var_ready, self.root_ready = st.semaphore("var_ready"), st.semaphore("root_ready")

    def statistics(self, step, t):
        v, S = self.nc.vector, self.S
        for h in range(2):
            step(v.bn_stats(self.stats[:, t, h, :], S.x[:, t, h * HALF:(h + 1) * HALF]))
        step(v.bn_aggr(self.mv[:, t, :], self.stats[:, t, :, :]), self.var_ready)

    def root(self, act, step, t):
        act.wait_ge(self.var_ready, t + 1)
        step(self.nc.scalar.activation(self.mv[:, t, 1:2], self.mv[:, t, 1:2], ACT.Sqrt, bias=self.S.eps[:, 0:1]), self.root_ready)

    def scale(self, dve, step, t):
        v, x, mv = self.nc.vector, self.S.x[:, t, :], self.mv
        dve.wait_ge(self.root_ready, t + 1)
        step(v.reciprocal(mv[:, t, 1:2], mv[:, t, 1:2]))
        step(v.tensor_scalar(x, x, mv[:, t, 0:1], mv[:, t, 1:2], ALU.subtract, ALU.mult))
        step(v.tensor_tensor(x, x, self.g, ALU.mult))
        step(v.tensor_tensor(x, x, self.b, ALU.add), self.normed)

    def transpose(self, pe, t):
        pe.wait_ge(self.normed, t + 1)
        for h in range(2):
            b = self.ring.fill(pe)
            for j in range(4):
                k = 4 * h + j
                last = self.nc.tensor.transpose(b[:, j * P:(j + 1) * P], self.S.x[:, t, k * P:(k + 1) * P], self.S.ident[:, :])
            last.then_inc(self.ring.full, 1)

    def copy(self, act, step, t):
        for h in range(2):
            b = self.ring.take(act)
            step(self.nc.scalar.activation(self.S.xT[:, 4 * h:4 * h + 4, t * P:(t + 1) * P], blocks4(b), ACT.Copy), self.ring.freed)


def load_rows(nc, eng, sem, g, b, g_dram, b_dram):
    eng.dma_start(g[:, :], g_dram.partition_broadcast(P)).then_inc(sem, 16)
    eng.dma_start(b[:, :], b_dram.partition_broadcast(P)).then_inc(sem, 16)


def stage_mix_out(nc, S, A, i):
    S.tag = f"mix_out{i}_"
    with Stage(nc, S.tag) as st:
        sem = lambda n: st.semaphore(n)
        sb = lambda n, *s: st.enter_context(nc.sbuf_tensor(S.tag + n, list(s), F32))
        wo_more, g, bb = sb("wo_more", P, KD - K_AHEAD, D), sb("g", P, D), sb("b", P, D)
        S.wo = lambda k: S.wo_ahead[:, k, :] if k < K_AHEAD else wo_more[:, k - K_AHEAD, :]
        gb_in, act_step, dve_step, normed = sem("gb_in"), sem("act_step"), sem("dve_step"), sem("normed")
        mm_ring, tr_ring = Ring(st, nc, "sum_bank", S.bank, [0, 1, 2, 3, 4, 5]), Ring(st, nc, "turn_bank", S.bank, [6, 7])
        norm = Norm(st, nc, S, g[:, :], bb[:, :], tr_ring, normed, None)
        with nc.Block() as block:
            @block.sync
            def _(sp):
                load_w_out(S, A, sp, i, range(K_AHEAD, KD))
                load_rows(nc, sp, gb_in, g, bb, A.ln1_g[i, :], A.ln1_b[i, :])

            @block.tensor
            def _(pe):
                for t in range(NT):
                    for h in range(2):
                        b = mm_ring.fill(pe)
                        for k in range(KD):
                            if t == 0 and h == 0:
                                pe.wait_ge(S.wo_in[k], 16)
                            last = nc.tensor.matmul(b, S.mixT[:, k, t * P:(t + 1) * P], S.wo(k)[:, h * HALF:(h + 1) * HALF], start=(k == 0), stop=(k == KD - 1))
                        last.then_inc(mm_ring.full, 1)
                    if t:
                        norm.transpose(pe, t - 1)
                norm.transpose(pe, NT - 1)

            @block.scalar
            def _(act):
                step = Steps(act, act_step)
                for t in range(NT):
                    norm.root(act, step, t)
                    norm.copy(act, step, t)

            @block.vector
            def _(dve):
                step = Steps(dve, dve_step)
                dve.wait_ge(gb_in, 32)
                for t in range(NT):
                    for h in range(2):
                        b, x = mm_ring.take(dve), S.x[:, t, h * HALF:(h + 1) * HALF]
                        step(nc.vector.scalar_tensor_tensor(x, x, ALPHA, b, ALU.mult, ALU.add), mm_ring.freed)
                    norm.statistics(step, t)
                    norm.scale(dve, step, t)


def stage_dense(nc, S, A, i):
    S.tag = f"dense{i}_"
    j = i // 2
    F = F_TILES
    PARTS, AHEAD_H = 3, 4
    wg_v = A.ffn_w_gate[j].rearrange("(k p) n -> p k n", p=P)
    wu_v = A.ffn_w_up[j].rearrange("(k p) n -> p k n", p=P)
    wd_v = A.ffn_w_down[j].rearrange("(c p) n -> p c n", p=P)
    with Stage(nc, S.tag) as st:
        sem = lambda n: st.semaphore(n)
        sb = lambda n, *s: st.enter_context(nc.sbuf_tensor(S.tag + n, list(s), F32))
        hT = sb("hT", P, F, T)
        sg = sb("sg", P, 2, T)
        g, bb = sg[:, :, :].rearrange("p a n -> p (a n)"), sb("b", P, D)
        gb_in, act_step, dve_step, normed, silu, multiplied, down_done = (
            sem("gb_in"), sem("act_step"), sem("dve_step"), sem("normed"), sem("silu"), sem("multiplied"), sem("down_done"))
        gate, up = Ring(st, nc, "gate_bank", S.bank, [0, 1, 2]), Ring(st, nc, "up_bank", S.bank, [3, 4, 5])
        tr_ring = Ring(st, nc, "turn_bank", S.bank, [0, 1])
        norm = Norm(st, nc, S, g, bb[:, :], tr_ring, normed, None)

        def through(n):
            return (down_done, n - 2 * F + 1) if n >= 2 * F else ((gate, up)[n % 2].full, n // 2 + 1)

        w = SplitWeights(st, nc, S.tag, 4, PARTS, through)
        xs = SplitTiles(st, nc, S.tag, "x", KD)
        with nc.Block() as block:
            @block.sync
            def _(sp):
                for f in range(F):
                    for q, src in enumerate((wg_v, wu_v)):
                        w.load(sp, 2 * f + q, src[:, :, f * P:(f + 1) * P])
                for f in range(F):
                    w.load(sp, 2 * F + f, wd_v[:, f, :])
                sp.wait_ge(multiplied, F)
                load_rows(nc, sp, gb_in, g, bb, A.ln2_g[i, :], A.ln2_b[i, :])

            @block.tensor
            def _(pe):
                for f in range(F):
                    for q, ring in enumerate((gate, up)):
                        b = ring.fill(pe)
                        hi, lo = w.take(pe, 2 * f + q)
                        for k in range(KD):
                            if f == 0 and q == 0:
                                pe.wait_ge(xs.low, k + 1)
                            ks = slice(k * P, (k + 1) * P)
                            last = three_passes(nc, b, (hi[:, ks], lo[:, ks]), (xs.hi[:, k, :], xs.lo[:, k, :]), k == 0, k == KD - 1)
                        last.then_inc(ring.full, 1)
                pe.wait_ge(gate.freed, F)
                pe.wait_ge(up.freed, F)
                for f in range(F):
                    hi, lo = w.take(pe, 2 * F + f)
                    pe.wait_ge(xs.low, KD + f + 1)
                    m = f % KD
                    for t in range(NT):
                        ts = slice(t * P, (t + 1) * P)
                        for h in range(2):
                            hc = slice(h * HALF, (h + 1) * HALF)
                            last = three_passes(nc, S.bank[:, 2 * t + h, :], (xs.hi[:, m, ts], xs.lo[:, m, ts]), (hi[:, hc], lo[:, hc]),
                                                f == 0, f == F - 1, skip_group_check=True)
                    last.then_inc(down_done, 1)
                for t in range(NT):
                    norm.transpose(pe, t)

            @block.scalar
            def _(act):
                step = Steps(act, act_step)
                for k in range(KD):
                    xs.make_high(act, k, S.xT[:, k, :])
                for n in range(PARTS):
                    w.make_high(act, n)
                for f in range(F):
                    if f >= 2:
                        act.wait_ge(multiplied, f - 1)
                    b = gate.take(act)
                    step(nc.scalar.activation(sg[:, f % 2, :], b, ACT.Silu), gate.freed)
                    act.sem_inc(silu, 1)
                    for n in range(2):
                        w.make_high(act, 2 * f + PARTS + n)

                def high_h(f):
                    if f >= AHEAD_H:
                        act.wait_ge(*through(2 * F + f - AHEAD_H))
                    act.wait_ge(multiplied, F)
                    xs.make_high(act, KD + f, hT[:, f, :])

                for f in range(AHEAD_H):
                    high_h(f)
                for f in range(F):
                    if f + AHEAD_H < F:
                        high_h(f + AHEAD_H)
                    if 2 * F + 2 + f < 3 * F and f > 0:
                        w.make_high(act, 2 * F + 2 + f)
                for t in range(NT):
                    norm.root(act, step, t)
                for t in range(NT):
                    norm.copy(act, step, t)

            @block.vector
            def _(dve):
                step = Steps(dve, dve_step)
                for k in range(KD):
                    xs.make_low(dve, k, S.xT[:, k, :])
                for n in range(PARTS):
                    w.make_low(dve, n)
                for f in range(F):
                    w.make_low(dve, 2 * f + PARTS)
                    dve.wait_ge(silu, f + 1)
                    b = up.take(dve)
                    step(nc.vector.tensor_tensor(hT[:, f, :], b, sg[:, f % 2, :], ALU.mult), up.freed)
                    dve.sem_inc(multiplied, 1)
                    w.make_low(dve, 2 * f + PARTS + 1)
                for f in range(AHEAD_H):
                    xs.make_low(dve, KD + f, hT[:, f, :])
                for f in range(F):
                    if f + AHEAD_H < F:
                        xs.make_low(dve, KD + f + AHEAD_H, hT[:, f + AHEAD_H, :])
                    if 2 * F + 2 + f < 3 * F and f > 0:
                        w.make_low(dve, 2 * F + 2 + f)
                dve.wait_ge(gb_in, 32)
                dve.wait_ge(down_done, F)
                for t in range(NT):
                    for h in range(2):
                        x = S.x[:, t, h * HALF:(h + 1) * HALF]
                        step(nc.vector.scalar_tensor_tensor(x, x, ALPHA, S.bank[:, 2 * t + h, :], ALU.mult, ALU.add))
                    norm.statistics(step, t)
                for t in range(NT):
                    norm.scale(dve, step, t)


def stage_embedding(nc, S, A, i, out):
    S.tag = f"embedding{i}_"
    last_layer = i == DEPTH - 1
    KP = GW // P
    with Stage(nc, S.tag) as st:
        sem = lambda n: st.semaphore(n)
        sb = lambda n, *s: st.enter_context(nc.sbuf_tensor(S.tag + n, list(s), F32))
        wg, wp = sb("wg", P, KD, D), sb("wp", P, KP, D)
        p, pT = sb("p", P, NT, GW), sb("pT", P, KP, T)
        sg = sb("sg", P, 4, HALF)
        wg_in = [sem(f"wg_in{h}") for h in range(2)]
        wp_in, p_in, act_step, dve_step, sig, added, turned, stored = (
            sem("wp_in"), sem("p_in"), sem("act_step"), sem("dve_step"), sem("sig"), sem("added"), sem("p_turned"), sem("stored"))
        gate, proj = Ring(st, nc, "gate_bank", S.bank, [0, 1, 2]), Ring(st, nc, "proj_bank", S.bank, [3, 4, 5])
        tr_ring = Ring(st, nc, "turn_bank", S.bank, [6, 7])
        with nc.Block() as block:
            @block.sync
            def _(sp):
                sp.dma_start(p[:, :, :], A.p[i, 0].rearrange("(t p) n -> p t n", p=P)).then_inc(p_in, 16)
                sp.dma_start(wp[:, :, :], A.ple_proj[i].rearrange("(k p) n -> p k n", p=P)).then_inc(wp_in, 16)
                for h in range(2):
                    sp.dma_start(wg[:, :, h * HALF:(h + 1) * HALF], A.ple_gate[i].rearrange("(k p) n -> p k n", p=P)[:, :, h * HALF:(h + 1) * HALF]).then_inc(wg_in[h], 16)
                if not last_layer:
                    load_first_w_in(S, A, sp, i + 1)
                else:
                    for t in range(NT):
                        sp.wait_ge(added, 2 * t + 2)
                        sp.dma_start(out[0, t * P:(t + 1) * P, :], S.x[:, t, :]).then_inc(stored, 16)
                    sp.wait_ge(stored, 16 * NT)

            @block.tensor
            def _(pe):
                pe.wait_ge(p_in, 16)
                for k in range(KP):
                    b = tr_ring.fill(pe)
                    for t in range(NT):
                        last = nc.tensor.transpose(b[:, t * P:(t + 1) * P], p[:, t, k * P:(k + 1) * P], S.ident[:, :])
                    last.then_inc(tr_ring.full, 1)
                pe.wait_ge(turned, KP)
                pe.wait_ge(wp_in, 16)

                def turn(t):
                    pe.wait_ge(added, 2 * t + 2)
                    for h in range(2):
                        b = tr_ring.fill(pe)
                        for j in range(4):
                            k = 4 * h + j
                            last = nc.tensor.transpose(b[:, j * P:(j + 1) * P], S.x[:, t, k * P:(k + 1) * P], S.ident[:, :])
                        last.then_inc(tr_ring.full, 1)

                for t in range(NT):
                    for h in range(2):
                        cols, ts = slice(h * HALF, (h + 1) * HALF), slice(t * P, (t + 1) * P)
                        b = proj.fill(pe)
                        for k in range(KP):
                            last = nc.tensor.matmul(b, pT[:, k, ts], wp[:, k, cols], start=(k == 0), stop=(k == KP - 1))
                        last.then_inc(proj.full, 1)
                        b = gate.fill(pe)
                        pe.wait_ge(wg_in[h], 16)
                        for k in range(KD):
                            last = nc.tensor.matmul(b, S.xT[:, k, ts], wg[:, k, cols], start=(k == 0), stop=(k == KD - 1))
                        last.then_inc(gate.full, 1)
                    if t and not last_layer:
                        turn(t - 1)
                if not last_layer:
                    turn(NT - 1)

            @block.scalar
            def _(act):
                step = Steps(act, act_step)
                for k in range(KP):
                    b = tr_ring.take(act)
                    step(nc.scalar.activation(pT[:, k, :], b, ACT.Copy), tr_ring.freed)
                    act.sem_inc(turned, 1)

                def copy(t):
                    for h in range(2):
                        b = tr_ring.take(act)
                        step(nc.scalar.activation(S.xT[:, 4 * h:4 * h + 4, t * P:(t + 1) * P], blocks4(b), ACT.Copy), tr_ring.freed)

                for n in range(2 * NT):
                    if n >= 4:
                        act.wait_ge(added, n - 3)
                    b = gate.take(act)
                    step(nc.scalar.activation(sg[:, n % 4, :], b, ACT.Sigmoid), gate.freed)
                    act.sem_inc(sig, 1)
                    if n >= 3 and n % 2 and not last_layer:
                        copy(n // 2 - 1)
                if not last_layer:
                    copy(NT - 1)

            @block.vector
            def _(dve):
                step = Steps(dve, dve_step)
                for n in range(2 * NT):
                    t, h = n // 2, n % 2
                    x = S.x[:, t, h * HALF:(h + 1) * HALF]
                    dve.wait_ge(sig, n + 1)
                    b = proj.take(dve)
                    step(nc.vector.tensor_tensor(sg[:, n % 4, :], sg[:, n % 4, :], b, ALU.mult), proj.freed)
                    step(nc.vector.tensor_tensor(x, x, sg[:, n % 4, :], ALU.add), added)


def stage_route(nc, S, A, j):
    S.tag = "route_"
    with Stage(nc, S.tag) as st:
        sem = lambda n: st.semaphore(n)
        sb = lambda n, s, dt=F32: st.enter_context(nc.sbuf_tensor(S.tag + n, s, dt))
        router, logits = sb("router", [P, KD, N_EXP]), sb("logits", [P, NT, N_EXP])
        top, idx, idxf = sb("top", [P, NT, 8]), sb("idx", [P, NT, 8], U32), sb("idxf", [P, NT, 8])
        first, second, member = sb("first", [P, NT, N_EXP]), sb("second", [P, NT, N_EXP]), sb("member", [P, NT, N_EXP])
        e2, g = sb("e2", [P, NT]), sb("gates2", [P, NT])
        before = sb("before", [P, P])
        pool_step, masks_ready = sem("pool_step"), sem("masks_ready")
        counts, more, running = sb("counts", [P, N_EXP]), sb("more", [P, N_EXP]), sb("running", [P, N_EXP])
        r_in, logits_full, dve_step, act_step, gap, exped, member_ready, counted = (
            sem("router_in"), sem("logits_full"), sem("dve_step"), sem("act_step"), sem("gap_ready"), sem("exped"), sem("member_ready"), sem("counted"))
        with nc.Block() as block:
            @block.sync
            def _(sp):
                sp.dma_start(router[:, :, :], A.moe_router[j].rearrange("(k p) e -> p k e", p=P)).then_inc(r_in, 16)

            @block.gpsimd
            def _(pool):
                step = Steps(pool, pool_step)
                step(nc.gpsimd.memset(before[:, :], 1.0))
                step(nc.gpsimd.affine_select(out=before[:, :], in_=before[:, :], compare_op=ALU.is_gt, fill=0.0, base=0,
                                             pattern=[[1, P]], channel_multiplier=-1))
                nc.gpsimd.iota(S.slots[:, :], pattern=[[1, T]], base=0, channel_multiplier=0,
                               allow_small_or_imprecise_dtypes=True).then_inc(masks_ready, 1)

            @block.tensor
            def _(pe):
                pe.wait_ge(r_in, 16)
                for t in range(NT):
                    for k in range(KD):
                        last = nc.tensor.matmul(S.bank[:, 0, t * N_EXP:(t + 1) * N_EXP], S.xT[:, k, t * P:(t + 1) * P], router[:, k, :], start=(k == 0), stop=(k == KD - 1))
                last.then_inc(logits_full, 1)
                pe.wait_ge(masks_ready, 1)
                pe.wait_ge(member_ready, 1)
                for t in range(NT + 1):
                    o = S.bank[:, 1, t * N_EXP:(t + 1) * N_EXP]
                    for s in range(min(t, NT - 1) + 1):
                        left = before if s == t else S.ones
                        last = nc.tensor.matmul(o, left[:, :], member[:, s, :], start=(s == 0), stop=(s == min(t, NT - 1)))
                last.then_inc(counted, 1)

            @block.scalar
            def _(act):
                act.wait_ge(gap, 1)
                nc.scalar.activation(e2[:, :], e2[:, :], ACT.Exp).then_inc(exped, 1)

            @block.vector
            def _(dve):
                step = Steps(dve, dve_step)
                v = nc.vector
                dve.wait_ge(masks_ready, 1)
                dve.wait_ge(logits_full, 1)
                step(v.tensor_copy(logits[:, :, :], S.bank[:, 0, 0:NT * N_EXP].rearrange("p (t e) -> p t e", t=NT)))
                for t in range(NT):
                    step(v.max(top[:, t, :], logits[:, t, :]))
                    step(v.max_index(idx[:, t, :], top[:, t, :], logits[:, t, :]))
                step(v.tensor_tensor(e2[:, :], top[:, :, 1], top[:, :, 0], ALU.subtract), gap)
                step(v.tensor_copy(idxf[:, :, :], idx[:, :, :]))
                for k, to in ((0, first), (1, second)):
                    step(v.tensor_tensor(to[:, :, :], over(S.slots[:, 0:N_EXP], NT), idxf[:, :, k:k + 1].broadcast_to([P, NT, N_EXP]), ALU.is_equal))
                step(v.tensor_tensor(member[:, :, :], first[:, :, :], second[:, :, :], ALU.add), member_ready)
                dve.wait_ge(exped, 1)
                step(v.tensor_scalar(g[:, :], e2[:, :], 1.0, None, ALU.add))
                step(v.reciprocal(g[:, :], g[:, :]))
                step(v.tensor_tensor(e2[:, :], e2[:, :], g[:, :], ALU.mult))
                wide = lambda ap: ap.unsqueeze(2).broadcast_to([P, NT, N_EXP])
                step(v.tensor_tensor(first[:, :, :], first[:, :, :], wide(g[:, :]), ALU.mult))
                step(v.tensor_tensor(second[:, :, :], second[:, :, :], wide(e2[:, :]), ALU.mult))
                step(v.tensor_tensor(S.gates[:, :, :], first[:, :, :], second[:, :, :], ALU.add))
                dve.wait_ge(counted, 1)
                step(v.scalar_tensor_tensor(S.place[:, :, 0:N_EXP], S.bank[:, 1, 0:NT * N_EXP].rearrange("p (t e) -> p t e", t=NT), 1.0, member[:, :, :], ALU.add, ALU.mult))
                step(v.tensor_scalar(S.place[:, :, 0:N_EXP], S.place[:, :, 0:N_EXP], -1.0, None, ALU.add))
                step(v.tensor_scalar(more[:, :], S.bank[:, 1, NT * N_EXP:(NT + 1) * N_EXP], float(P), 1.0, ALU.is_gt, ALU.add))
                step(v.tensor_copy(counts[:, :], S.bank[:, 1, NT * N_EXP:(NT + 1) * N_EXP]))
                for n in range(2, NT):
                    step(v.scalar_tensor_tensor(more[:, :], counts[:, :], float(n * P), more[:, :], ALU.is_gt, ALU.add))
                step(v.tensor_tensor_scan(running[:, :], S.ones[:, 0:N_EXP], more[:, :], 0.0, ALU.mult, ALU.add))
                step(v.tensor_tensor(running[:, :], running[:, :], more[:, :], ALU.subtract))
                step(v.tensor_copy(S.blocks[0:1, 0:N_EXP], more[0:1, :]))
                step(v.tensor_copy(S.blocks[0:1, N_EXP:2 * N_EXP], running[0:1, :]))


def stage_experts(nc, S, A, i):
    S.tag = f"experts{i}_"
    j = i // 2
    FC = 256
    NCH = D_FFE // FC
    Q = FC // P
    PIECE = 2048
    GW_, UW_, DW_ = 0, 1, 2
    OWN = 1408
    wg_v = A.moe_w_gate[j].rearrange("e (k p) n -> e p k n", p=P)
    wu_v = A.moe_w_up[j].rearrange("e (k p) n -> e p k n", p=P)
    wd_v = A.moe_w_down[j].rearrange("e (c p) n -> e p c n", p=P)
    with Stage(nc, S.tag) as st:
        sem = lambda n: st.semaphore(n)
        sb = lambda n, *s: st.enter_context(nc.sbuf_tensor(S.tag + n, list(s), F32))
        sr = lambda n, *s: st.enter_context(nc.sbuf_tensor(S.tag + n, list(s), F32R))
        raw = sb("raw", P, 2, 3, PIECE)
        w_hi, w_lo = sr("w_hi", P, 3, PIECE), sr("w_lo", P, 3, PIECE)
        xg_hi, xg_lo = sr("xg_hi", P, NT, KD * P), sr("xg_lo", P, NT, KD * P)
        ysum = sb("ysum", P, NT * D)
        acc = S.xT[:, :, :].rearrange("p k t -> p (k t)").rearrange("p (t d) -> p t d", t=NT)
        pick, pick_w, back = sb("pick", P, NT, P), sb("pick_w", P, NT, P), sb("back", P, NT, P)
        sg, h = sb("sg", P, FC), sb("h", P, FC)
        hT_hi, hT_lo = sr("hT_hi", P, FC), sr("hT_lo", P, FC)
        names = ("gate", "up", "down")
        raw_in = [[sem(f"raw{r}_{n}_in") for n in names] for r in range(2)]
        hi_ready, lo_ready = ([sem(f"{w}_{n}") for n in names] for w in ("hi_ready", "lo_ready"))
        gate_full, up_full, silu_ready, h_ready = sem("gate_full"), sem("up_full"), sem("silu_ready"), sem("h_ready")
        t_full, t_hi, t_lo, y_full, y_free = sem("t_full"), sem("t_hi"), sem("t_lo"), sem("y_full"), sem("y_free")
        through = (gate_full, up_full, y_full)
        pick_ready, gath_full, g_hi, g_lo = sem("pick_ready"), sem("gath_full"), sem("g_hi"), sem("g_lo")
        back_pick, back_turned, back_ready, sc_full, sc_done = sem("back_pick"), sem("back_turned"), sem("back_ready"), sem("sc_full"), sem("sc_done")
        place_ready = sem("place_ready")
        cleared, zeroed, gb_in, act_step, normed = sem("cleared"), sem("zeroed"), sem("gb_in"), sem("act_step"), sem("normed")
        GB, UB, TR, Y, GA = 0, 1, 2, 4, 6
        bank = S.bank

        def experts(eng):
            with eng.Fori(0, N_EXP) as e:
                nb = eng.value_load(S.blocks[0:1, bass.ds(e, 1)], min_val=1, max_val=NT)
                base = eng.value_load(S.blocks[0:1, bass.ds(e + N_EXP, 1)], min_val=0, max_val=2 * N_EXP)
                yield e, nb, base

        def chunks(eng):
            with eng.Fori(0, (NCH - 2) // 2) as c2:
                yield c2 * 2 + 1, 1, c2, c2 + 1
                yield c2 * 2 + 2, 0, c2 + 1, c2 + 1
            yield NCH - 1, 1, NCH // 2 - 1, None

        def units(eng, nb, unit):
            with eng.If(nb < 2):
                unit(0, True, True)
            with eng.If(nb > 1):
                unit(0, True, False)
                with eng.If(nb > 2):
                    with eng.Fori(1, nb - 1) as b:
                        unit(b, False, False)
                unit(nb - 1, False, True)

        def each_block(eng, nb, first=0):
            for b in range(first, NT):
                if b == 0:
                    yield b
                else:
                    with eng.If(nb > b):
                        yield b

        with nc.Block() as block:
            @block.sync
            def _(sp):
                with sp.Fori(0, N_EXP) as e:
                    with sp.Fori(0, NCH // 2) as c2:
                        for r in range(2):
                            c = c2 * 2 + r
                            for p in (GW_, UW_, DW_):
                                sp.wait_ge(lo_ready[p], (e * NCH + c + 1) * 2)
                                to = raw[:, r, p, :]
                                if p == DW_:
                                    sp.dma_start(to.rearrange("p (c n) -> p c n", c=Q), wd_v[bass.ds(e, 1), :, bass.ds(c * Q, Q), :].rearrange("a p c n -> (a p) c n")).then_inc(raw_in[r][p], 16)
                                else:
                                    src = (wg_v, wu_v)[p]
                                    sp.dma_start(to.rearrange("p (k n) -> p k n", k=KD), src[bass.ds(e, 1), :, :, bass.ds(c * FC, FC)].rearrange("a p k n -> (a p) k n")).then_inc(raw_in[r][p], 16)

            @block.tensor
            def _(pe):
                mm = nc.tensor.matmul

                def three(o, x_hi, x_lo, p, cols, start, stop):
                    mm(o, x_hi, w_hi[:, p, cols], start=start, stop=False)
                    mm(o, x_hi, w_lo[:, p, cols], start=False, stop=False)
                    return mm(o, x_lo, w_hi[:, p, cols], start=False, stop=stop)

                def gate_up(e, base, c, b, u):
                    pe.wait_ge(g_lo, (base + b) * 2 + 3)
                    for p, bk, read, full in ((GW_, GB, silu_ready, gate_full), (UW_, UB, h_ready, up_full)):
                        pe.wait_ge(lo_ready[p], (e * NCH + c + 3) * 2)
                        pe.wait_ge(read, u + 1)
                        for k in range(KD):
                            last = three(bank[:, bk, 0:FC], xg_hi[:, b, k * P:(k + 1) * P], xg_lo[:, b, k * P:(k + 1) * P], p,
                                         slice(k * FC, (k + 1) * FC), k == 0, k == KD - 1)
                        last.then_inc(full, 1)

                def turn(u):
                    pe.wait_ge(h_ready, u + 2)
                    for q in range(Q):
                        last = nc.tensor.transpose(bank[:, TR, q * P:(q + 1) * P], h[:, q * P:(q + 1) * P], S.ident[:, :])
                    last.then_inc(t_full, 1)

                def down(e, c, u):
                    pe.wait_ge(t_lo, u + 1)
                    pe.wait_ge(y_free, u + 2)
                    pe.wait_ge(lo_ready[DW_], (e * NCH + c + 3) * 2)
                    for q in range(Q):
                        for half in range(2):
                            at = q * D + half * HALF
                            last = three(bank[:, Y + half, :], hT_hi[:, q * P:(q + 1) * P], hT_lo[:, q * P:(q + 1) * P], DW_, slice(at, at + HALF), q == 0, q == Q - 1)
                    last.then_inc(y_full, 1)

                pe.wait_ge(cleared, 1)
                for e, nb, base in experts(pe):
                    for b in each_block(pe, nb):
                        v = base + b
                        pe.wait_ge(sc_done, base * 8 + 1)
                        pe.wait_ge(g_lo, v * 2 + 1)
                        pe.wait_ge(pick_ready, v + 1)
                        for hh in range(2):
                            for q in range(4):
                                k = 4 * hh + q
                                for t in range(NT):
                                    last = mm(bank[:, GA + hh, q * P:(q + 1) * P], S.x[:, t, k * P:(k + 1) * P], pick[:, t, :], start=(t == 0), stop=(t == NT - 1))
                            last.then_inc(gath_full, 1)
                    u0 = base * NCH
                    for b in each_block(pe, nb):
                        gate_up(e, base, 0, b, u0 + b)
                        if b:
                            down(e, 0, u0 + (b - 1))
                        turn(u0 + b)
                    for c, _, _, _ in chunks(pe):
                        uc = u0 + c * nb
                        for b in each_block(pe, nb):
                            gate_up(e, base, c, b, uc + b)
                            down(e, c if b else c - 1, uc + (b - 1))
                            turn(uc + b)

                    def turn_back(v):
                        pe.wait_ge(back_pick, v + 1)
                        pe.wait_ge(sc_done, v * 8 + 1)
                        for t in range(NT):
                            last = nc.tensor.transpose(bank[:, GA, t * P:(t + 1) * P], pick_w[:, t, :], S.ident[:, :])
                        last.then_inc(back_turned, 1)

                    turn_back(base)
                    down(e, NCH - 1, u0 + NCH * nb - 1)
                    for b in each_block(pe, nb):
                        v = base + b
                        if b:
                            turn_back(v)
                        pe.wait_ge(y_free, (base + nb) * NCH + 2)
                        pe.wait_ge(back_ready, v + 1)
                        for t in range(NT):
                            for hh in range(2):
                                mm(bank[:, 2 * t + hh, :], back[:, t, :], ysum[:, b * D + hh * HALF:b * D + (hh + 1) * HALF], start=True, stop=True).then_inc(sc_full, 1)

            @block.scalar
            def _(act):
                f = nc.scalar.activation

                def split(p, e, parity, before, units_done):
                    act.wait_ge(through[p], units_done + 1)
                    act.wait_ge(raw_in[parity][p], (e * (NCH // 2) + before + 1) * 16)
                    f(w_hi[:, p, :], raw[:, parity, p, :], ACT.Copy).then_inc(hi_ready[p], 1)

                def silu(u):
                    act.wait_ge(h_ready, u + 1)
                    act.wait_ge(gate_full, u + 2)
                    f(sg[:, :], bank[:, GB, 0:FC], ACT.Silu).then_inc(silu_ready, 1)

                def turned(u):
                    act.wait_ge(t_full, u + 1)
                    f(hT_hi[:, :], bank[:, TR, 0:FC], ACT.Copy).then_inc(t_hi, 1)

                def chunk(e, nb, u0, parity, before, before_next):
                    def unit(b, first, last):
                        u = u0 + b
                        silu(u)
                        if last and before_next is not None:
                            split(GW_, e, 1 - parity, before_next, u + 1)
                            split(UW_, e, 1 - parity, before_next, u + 1)
                        turned(u)
                        if first:
                            split(DW_, e, parity, before, u)

                    units(act, nb, unit)

                for s in (*through, silu_ready, h_ready):
                    act.sem_inc(s, 1)
                act.wait_ge(cleared, 1)
                f(sg[:, 0:1], acc[:, 0, 0:1], ACT.Silu).then_inc(act_step, 1)
                act.wait_ge(act_step, 1)
                for e, nb, base in experts(act):
                    split(GW_, e, 0, 0, base * NCH)
                    split(UW_, e, 0, 0, base * NCH)
                    for b in each_block(act, nb):
                        for hh in range(2):
                            n = (base + b) * 2 + hh
                            act.wait_ge(gath_full, n + 2)
                            f(xg_hi[:, b, hh * HALF:(hh + 1) * HALF], bank[:, GA + hh, :], ACT.Copy).then_inc(g_hi, 1)
                    u0 = base * NCH
                    chunk(e, nb, u0, 0, 0, 0)
                    for c, parity, before, before_next in chunks(act):
                        chunk(e, nb, u0 + c * nb, parity, before, before_next)
                    for b in each_block(act, nb):
                        v = base + b
                        act.wait_ge(back_turned, v + 1)
                        f(back[:, :, :], blocks4(bank[:, 6, :]), ACT.Copy).then_inc(back_ready, 1)

            @block.gpsimd
            def _(pool):
                def split(p, e, c, parity):
                    pool.wait_ge(hi_ready[p], e * NCH + c + 1)
                    nc.gpsimd.tensor_tensor(w_lo[:, p, OWN:], raw[:, parity, p, OWN:], w_hi[:, p, OWN:].bitcast(F32), ALU.subtract).then_inc(lo_ready[p], 1)

                def chunk(e, nb, c, parity):
                    with pool.If(nb > 1):
                        split(DW_, e, c, parity)
                    split(GW_, e, c + 1, 1 - parity)
                    split(UW_, e, c + 1, 1 - parity)
                    with pool.If(nb < 2):
                        split(DW_, e, c, parity)

                for e, nb, base in experts(pool):
                    split(GW_, e, 0, 0)
                    split(UW_, e, 0, 0)
                    with pool.Fori(0, NCH // 2 - 1) as c2:
                        chunk(e, nb, c2 * 2, 0)
                        chunk(e, nb, c2 * 2 + 1, 1)
                    chunk(e, nb, NCH - 2, 0)
                    split(DW_, e, NCH - 1, 1)

            @block.vector
            def _(dve):
                tt, ts = nc.vector.tensor_tensor, nc.vector.tensor_scalar

                def split(p, e, c, parity):
                    dve.wait_ge(hi_ready[p], e * NCH + c + 1)
                    tt(w_lo[:, p, 0:OWN], raw[:, parity, p, 0:OWN], w_hi[:, p, 0:OWN].bitcast(F32), ALU.subtract).then_inc(lo_ready[p], 1)

                def product(u):
                    dve.wait_ge(silu_ready, u + 2)
                    dve.wait_ge(up_full, u + 2)
                    tt(h[:, :], sg[:, :], bank[:, UB, 0:FC], ALU.mult).then_inc(h_ready, 1)

                def turned(u):
                    dve.wait_ge(t_hi, u + 1)
                    tt(hT_lo[:, :], bank[:, TR, 0:FC], hT_hi[:, :].bitcast(F32), ALU.subtract).then_inc(t_lo, 1)

                def drain(blocks_zeroed, u, b):
                    dve.wait_ge(zeroed, blocks_zeroed)
                    dve.wait_ge(y_free, u + 1)
                    dve.wait_ge(y_full, u + 1)
                    y = ysum[:, bass.ds(b * D, D)] if not isinstance(b, int) else ysum[:, b * D:(b + 1) * D]
                    tt(y, y, bank[:, Y:Y + 2, :].rearrange("p a n -> p (a n)"), ALU.add).then_inc(y_free, 1)

                for s in (y_free, y_free, gath_full, g_lo, sc_done):
                    dve.sem_inc(s, 1)
                for s in lo_ready:
                    dve.sem_inc(s, 4)

                def one_hot(b, e):
                    for t in range(NT):
                        last = ts(pick[:, t, :], S.slots[:, b * P:(b + 1) * P], S.place[:, t, bass.ds(e, 1)], None, ALU.is_equal)
                    last.then_inc(pick_ready, 1)

                nc.vector.memset(S.place[:, :, N_EXP:N_EXP + 1], -1.0).then_inc(place_ready, 1)
                dve.wait_ge(place_ready, 1)
                one_hot(0, 0)
                nc.vector.memset(acc, 0.0).then_inc(cleared, 1)
                dve.wait_ge(cleared, 1)
                for e, nb, base in experts(dve):
                    for b in each_block(dve, nb):
                        v = base + b
                        if b:
                            dve.wait_ge(gath_full, v * 2 + 1)
                            one_hot(b, e)
                        nc.vector.memset(ysum[:, b * D:(b + 1) * D], 0.0).then_inc(zeroed, 1)
                        if b == 0:
                            split(GW_, e, 0, 0)
                            split(UW_, e, 0, 0)
                        for hh in range(2):
                            dve.wait_ge(g_hi, v * 2 + (hh + 1))
                            tt(xg_lo[:, b, hh * HALF:(hh + 1) * HALF], bank[:, GA + hh, :], xg_hi[:, b, hh * HALF:(hh + 1) * HALF].bitcast(F32), ALU.subtract).then_inc(g_lo, 1)
                    u0 = base * NCH
                    zs = base + nb

                    def chunk(c, uc, parity, last_one):
                        def unit(b, first, last):
                            u = uc + b
                            if last and not last_one:
                                split(GW_, e, c + 1, 1 - parity)
                            product(u)
                            if last and not last_one:
                                split(UW_, e, c + 1, 1 - parity)
                            turned(u)
                            if not first:
                                drain(zs, u, (b + nb - 1) % nb)
                            elif not isinstance(c, int) or c:
                                drain(zs, u, nb - 1)
                            if first:
                                split(DW_, e, c, parity)

                        units(dve, nb, unit)

                    chunk(0, u0, 0, False)
                    for c, parity, _, before_next in chunks(dve):
                        chunk(c, u0 + c * nb, parity, before_next is None)

                    def weighted(b):
                        for t in range(NT):
                            last = ts(pick_w[:, t, :], S.slots[:, b * P:(b + 1) * P], S.place[:, t, bass.ds(e, 1)], S.gates[:, t, bass.ds(e, 1)],
                                      ALU.is_equal, ALU.mult)
                        last.then_inc(back_pick, 1)

                    weighted(0)
                    drain(zs, u0 + NCH * nb, nb - 1)
                    dve.wait_ge(gath_full, (base + nb) * 2 + 1)
                    one_hot(0, e + 1)
                    for b in each_block(dve, nb):
                        v = base + b
                        if b:
                            weighted(b)
                        for n in range(2 * NT):
                            dve.wait_ge(sc_full, v * 8 + (n + 1))
                            dve.wait_ge(sc_done, v * 8 + (n + 1))
                            a = acc[:, n // 2, (n % 2) * HALF:(n % 2 + 1) * HALF]
                            tt(a, a, bank[:, n, :], ALU.add).then_inc(sc_done, 1)

        with nc.Block() as block:
            g, bb = ysum[:, 0:D], ysum[:, D:2 * D]
            tr_ring = Ring(st, nc, "turn_bank", S.bank, [0, 1, 2, 3])
            norm = Norm(st, nc, S, g, bb, tr_ring, normed, None)
            norm_step, norm_act_step = sem("norm_step"), sem("norm_act_step")

            @block.sync
            def _(sp):
                load_rows(nc, sp, gb_in, g, bb, A.ln2_g[i, :], A.ln2_b[i, :])

            @block.tensor
            def _(pe):
                for t in range(NT):
                    norm.transpose(pe, t)

            @block.scalar
            def _(act):
                step = Steps(act, norm_act_step)
                for t in range(NT):
                    norm.root(act, step, t)
                    norm.copy(act, step, t)

            @block.vector
            def _(dve):
                step = Steps(dve, norm_step)
                for t in range(NT):
                    step(nc.vector.scalar_tensor_tensor(S.x[:, t, :], S.x[:, t, :], ALPHA, acc[:, t, :], ALU.mult, ALU.add))
                dve.wait_ge(gb_in, 32)
                for t in range(NT):
                    norm.statistics(step, t)
                    norm.scale(dve, step, t)


def build_trunk(nc, A, out):
    with ExitStack() as ctx:
        sb = lambda n, s, dt=F32: ctx.enter_context(nc.sbuf_tensor(n, s, dt))
        S = Buffers()
        S.bank = ctx.enter_context(nc.psum_tensor("bank", [P, 8, HALF], F32))
        S.x = sb("x_tok", [P, NT, D])
        S.xT = sb("x_ch", [P, KD, T])
        S.mixT = S.xT
        S.ident = sb("ident", [P, P])
        S.ones = sb("ones", [P, P])
        S.eps, S.par, S.sinks = sb("eps", [P, 8]), sb("par", [P, DEPTH * R_ROWS]), sb("sinks", [P, DEPTH * 4])
        S.lb = sb("lb", [P, 10])
        with ExitStack() as low:
            sl = lambda n, s: low.enter_context(nc.sbuf_tensor(n, s, F32))
            S.v_first = sl("v_first", [P, 2, T])
            S.head_ones, S.head_mean = sl("head_ones", [P, P]), sl("head_mean", [P, P])
            S.chunk_before, S.chunk_upto = sl("chunk_before", [P, P]), sl("chunk_upto", [P, P])
            S.gla_heads = sl("gla_heads", [P, GW])
            S.own_bias, S.prev_bias = sl("own_bias", [P, P]), sl("prev_bias", [P, P])
            S.lower = sl("lower", [P, len(LEVELS), P])
            S.carry128, S.carry64 = sl("carry128", [P, T]), sl("carry64", [P, T])
            S.w_low, S.w_up = sl("w_low", [P, KD, P]), sl("w_up", [P, U_END])
            S.ahead = sl("ahead", [P, W_SLOTS, KD * GW])
            S.wo_ahead = S.ahead[:, :, :].rearrange("p s n -> p (s n)").rearrange("p (k n) -> p k n", k=K_AHEAD)
            S.wo = lambda k: S.wo_ahead[:, k, :]

            def open_weights(i):
                weights = Stage(nc, f"weights{i}_")
                S.w_landed = [weights.semaphore(f"w_in_landed{n}") for n in range(W_SLOTS)]
                S.wo_in = [weights.semaphore(f"w_out_in{k}") for k in range(KD)]
                return weights

            weights = open_weights(0)
            stage_constants(nc, S, A)
            for i in range(DEPTH):
                with ExitStack() as lay:
                    sy = lambda n, s: lay.enter_context(nc.sbuf_tensor(f"{n}_layer{i}", s, F32))
                    S.rw_w, S.rw_a, S.rw_g = sy("rw_w", [P, 2, T]), sy("rw_a", [P, 2, T]), sy("rw_g", [P, 2, T])
                    S.r, S.k, S.v = sy("r", [P, 2, T]), sy("k", [P, 2, T]), sy("v", [P, 2, T]) if i else None
                    with ExitStack() as pre:
                        sp = lambda n, s: pre.enter_context(nc.sbuf_tensor(f"{n}_layer{i}", s, F32))
                        S.z = sp("z", [P, 13, T])
                        S.v_gla, S.v_hgrn, S.v_swa = sp("v_gla", [P, NT, GW]), sp("v_hgrn", [P, NT, GW]), sp("v_swa", [P, NT, P])
                        S.log_decay, S.h_key = sp("log_decay", [P, 3, T]), sp("h_key", [P, 2, T])
                        with ExitStack() as gat:
                            sg = lambda n, s: gat.enter_context(nc.sbuf_tensor(f"{n}_layer{i}", s, F32))
                            S.zr = sg("zr", [P, 7, T + 1])
                            stage_projection(nc, S, A, i)
                            S.low, S.gk_pre, S.soft, S.rw_vg = sg("low", [P, T]), sg("gk_pre", [P, T]), sg("soft", [P, 3, T]), sg("rw_vg", [P, 2, T])
                            stage_gates(nc, S, A, i)
                        stage_gated_linear(nc, S, A, i)
                        stage_window(nc, S, A, i)
                    stage_rwkv(nc, S, A, i)
                stage_mix_out(nc, S, A, i)
                weights.close()
                if i % 2 == 0:
                    stage_dense(nc, S, A, i)
                    weights = open_weights(i + 1)
                    stage_embedding(nc, S, A, i, out)
        S.gates, S.place = sb("gates", [P, NT, N_EXP]), sb("place", [P, NT, N_EXP + 1])
        S.blocks, S.slots = sb("blocks", [1, 2 * N_EXP], I32), sb("slots", [P, T])
        stage_route(nc, S, A, 0)
        stage_experts(nc, S, A, DEPTH - 1)
        stage_embedding(nc, S, A, DEPTH - 1, out)


_INS = ['x', 'p', 'w_in', 'w_out', 'gla_gk_up', 'gla_gk_bias', 'gla_norm_w', 'hgrn_lower_bounds', 'hgrn_norm_w',
        'swa_sinks', 'rwkv_mu', 'rwkv_w0', 'rwkv_w_up', 'rwkv_a0', 'rwkv_a_up', 'rwkv_g_up', 'rwkv_k_k', 'rwkv_k_a',
        'rwkv_r_k', 'rwkv_lnx_w', 'rwkv_lnx_b', 'rwkv_vres_down', 'rwkv_vres_mu', 'rwkv_v0', 'rwkv_vres_up',
        'ln1_g', 'ln1_b', 'ln2_g', 'ln2_b', 'ffn_w_gate', 'ffn_w_up', 'ffn_w_down', 'moe_router', 'moe_w_gate',
        'moe_w_up', 'moe_w_down', 'ple_proj', 'ple_gate']


def kernel(**inputs):
    import numpy as np
    import concourse.bacc as bacc
    from concourse.bass_utils import run_bass_kernel_spmd

    nc = bacc.Bacc("TRN2", target_bir_lowering=False, num_devices=1)
    arrays, aps = {}, {}
    for name in _INS:
        a = np.ascontiguousarray(inputs[name])
        arrays[name + "_in"] = a
        aps[name] = nc.dram_tensor(name + "_in", a.shape, mybir.dt.from_np(a.dtype), kind="ExternalInput").ap()
    out = nc.dram_tensor("out_0", (1, T, D), F32, kind="ExternalOutput").ap()
    build_trunk(nc, Inputs(aps), out)
    result = run_bass_kernel_spmd(nc, [arrays], core_ids=[0])
    return result.results[0]["out_0"]
```
